# Optimizing a Trainium2 kernel written in Bass

```python
import math
import jax, jax.numpy as jnp
from jax import lax
import numpy as np

D_MODEL = 1024
BATCH = 1
SEQ = 512
DEPTH = 1

A_HEADS = 4
A_QK_DIM = 64
A_V_DIM = 2 * A_QK_DIM
A_WIDTH = A_HEADS * A_V_DIM
B_PAIRS = ((128, 1), (512, 4), (2048, 16))
B_GROUPS = len(B_PAIRS)
B_HEADS = 4
B_HEAD_DIM = 128
B_WIDTH = B_HEADS * B_HEAD_DIM
B_BLOCK = 128
Q_BLOCK = 128
A_Q_COLS = A_HEADS * 2 * A_QK_DIM
A_K_COLS = A_HEADS * 2 * A_QK_DIM
A_V_COLS = A_HEADS * A_V_DIM
B_COLS = B_GROUPS * B_WIDTH
GATE_COLS = 2 * D_MODEL
IN_COLS = A_Q_COLS + A_K_COLS + A_V_COLS + 3 * B_COLS + GATE_COLS
D_FF = 2816
CONV_WIDTH = 3
ROPE_THETA = 10000.0
NORM_EPS = 1e-6


def rms_norm(x, g):
    xf = x.astype(jnp.float32)
    y = xf * lax.rsqrt(jnp.mean(xf * xf, axis=-1, keepdims=True) + NORM_EPS)
    return (y * g.astype(jnp.float32)).astype(x.dtype)

def rope_tables(positions, dim):
    inv = ROPE_THETA ** (-jnp.arange(0, dim, 2, dtype=jnp.float32) / dim)
    ang = positions.astype(jnp.float32)[..., None] * inv
    return jnp.cos(ang)[:, :, None, None, :], jnp.sin(ang)[:, :, None, None, :]

def apply_rope(t, cos, sin):
    tf = t.astype(jnp.float32)
    t1, t2 = jnp.split(tf, 2, axis=-1)
    return jnp.concatenate([t1 * cos - t2 * sin, t2 * cos + t1 * sin], axis=-1).astype(t.dtype)

def diff_attention(q, k, v, lam):
    b, s, h, _, dqk = q.shape
    nq = s // Q_BLOCK
    scale = dqk ** -0.5
    qb = q.reshape(b, nq, Q_BLOCK, h, 2, dqk).transpose(1, 0, 2, 3, 4, 5)
    kpos = jnp.arange(s)

    def one_block(args):
        qi, i = args
        sc = jnp.einsum('bqhcd,bkhcd->bchqk', qi, k).astype(jnp.float32) * scale
        qpos = i * Q_BLOCK + jnp.arange(Q_BLOCK)
        causal = kpos[None, :] <= qpos[:, None]
        p = jax.nn.softmax(jnp.where(causal, sc, -jnp.inf), axis=-1)
        a = p[:, 0] - lam * p[:, 1]
        return jnp.einsum('bhqk,bkhd->bqhd', a.astype(v.dtype), v)

    o = lax.map(one_block, (qb, jnp.arange(nq)))
    return o.transpose(1, 0, 2, 3, 4).reshape(b, s, h, v.shape[-1])

def dilated_group(q, k, v, window, dil):
    b, s, h, d = q.shape
    L = s // dil
    nwin = window // dil
    nb = -(-L // B_BLOCK)
    Lp = nb * B_BLOCK

    def to_blocks(t):
        t = t.reshape(b, L, dil, h, d).transpose(0, 2, 1, 3, 4)
        t = jnp.pad(t, ((0, 0), (0, 0), (0, Lp - L), (0, 0), (0, 0)))
        return t.reshape(b, dil, nb, B_BLOCK, h, d)

    def with_prev(t):
        prev = jnp.pad(t[:, :, :-1], ((0, 0), (0, 0), (1, 0), (0, 0), (0, 0), (0, 0)))
        return jnp.concatenate([prev, t], axis=3)

    qb, kb, vb = to_blocks(q), to_blocks(k), to_blocks(v)
    kk, vv = with_prev(kb), with_prev(vb)
    sc = jnp.einsum('brnqhd,brnkhd->brnhqk', qb, kk).astype(jnp.float32) * (d ** -0.5)
    qi = jnp.arange(B_BLOCK)[:, None]
    kj = jnp.arange(2 * B_BLOCK)[None, :]
    rel = qi - kj + B_BLOCK
    kabs = jnp.arange(nb)[:, None, None] * B_BLOCK + kj - B_BLOCK
    valid = (rel >= 0) & (rel <= nwin) & (kabs >= 0)
    sc = jnp.where(valid[None, None, :, None], sc, -jnp.inf)
    m = jnp.max(sc, axis=-1, keepdims=True)
    p = jnp.exp(sc - m)
    den = jnp.sum(p, axis=-1, keepdims=True)
    o = jnp.einsum('brnhqk,brnkhd->brnqhd', (p / den).astype(v.dtype), vv)
    lse = (m + jnp.log(den))[..., 0].transpose(0, 1, 2, 4, 3)

    def from_blocks(t):
        t = t.reshape((b, dil, Lp) + t.shape[4:])[:, :, :L]
        t = jnp.moveaxis(t, 1, 2)
        return t.reshape((b, s) + t.shape[3:])

    return from_blocks(o), from_blocks(lse)

def causal_depthwise_conv(u, w, bias):
    s = u.shape[1]
    up = jnp.pad(u, ((0, 0), (CONV_WIDTH - 1, 0), (0, 0)))
    out = sum(up[:, j:j + s] * w[j] for j in range(CONV_WIDTH))
    return out + bias

def first_inputs(seed: int = 0) -> dict:
    key = jax.random.key(seed)
    ks = jax.random.split(key, 20)
    f32 = jnp.float32

    def nrm(k, shape, scale):
        return jax.random.normal(k, shape, f32) * scale

    def gain(k, shape):
        return 1.0 + 0.05 * jax.random.normal(k, shape, f32)

    x = jax.random.normal(ks[0], (BATCH, SEQ, D_MODEL), f32)
    offset = jax.random.randint(ks[1], (BATCH, 1), 0, 1024, dtype=jnp.int32)
    positions = (offset + jnp.arange(SEQ, dtype=jnp.int32)[None, :]).astype(jnp.int32)
    return {
        "x": x,
        "positions": positions,
        "pre_mix_g": gain(ks[2], (DEPTH, D_MODEL)),
        "w_in": nrm(ks[3], (DEPTH, D_MODEL, IN_COLS), D_MODEL ** -0.5),
        "diff_lambda": nrm(ks[4], (DEPTH, 4, A_QK_DIM), 0.1),
        "diff_head_g": gain(ks[5], (DEPTH, A_V_DIM)),
        "w_a_out": nrm(ks[6], (DEPTH, A_WIDTH, D_MODEL), A_WIDTH ** -0.5),
        "w_b_out": nrm(ks[7], (DEPTH, B_WIDTH, D_MODEL), B_WIDTH ** -0.5),
        "w_mix_out": nrm(ks[8], (DEPTH, D_MODEL, D_MODEL), D_MODEL ** -0.5),
        "post_mix_g": gain(ks[9], (DEPTH, D_MODEL)),
        "pre_ffn_g": gain(ks[10], (DEPTH, D_MODEL)),
        "w_up": nrm(ks[11], (DEPTH, D_MODEL, 2 * D_FF), D_MODEL ** -0.5),
        "conv_w": nrm(ks[12], (DEPTH, CONV_WIDTH, 2 * D_FF), CONV_WIDTH ** -0.5),
        "conv_b": nrm(ks[13], (DEPTH, 2 * D_FF), 0.01),
        "w_down": nrm(ks[14], (DEPTH, D_FF, D_MODEL), D_FF ** -0.5),
        "post_ffn_g": gain(ks[15], (DEPTH, D_MODEL)),
    }

def first_block(x, positions, pre_mix_g, w_in, diff_lambda, diff_head_g, w_a_out, w_b_out,
              w_mix_out, post_mix_g, pre_ffn_g, w_up, conv_w, conv_b, w_down, post_ffn_g):
    b, s, _ = x.shape
    cos_a, sin_a = rope_tables(positions, A_QK_DIM)
    cos_b, sin_b = rope_tables(positions, B_HEAD_DIM)
    split_at = np.cumsum([A_Q_COLS, A_K_COLS, A_V_COLS, B_COLS, B_COLS, B_COLS]).tolist()

    for l in range(DEPTH):
        h = rms_norm(x, pre_mix_g[l])
        proj = h @ w_in[l]
        qa, ka, va, qb, kb, vb, gates = jnp.split(proj, split_at, axis=-1)

        qa = apply_rope(qa.reshape(b, s, A_HEADS, 2, A_QK_DIM), cos_a, sin_a)
        ka = apply_rope(ka.reshape(b, s, A_HEADS, 2, A_QK_DIM), cos_a, sin_a)
        va = va.reshape(b, s, A_HEADS, A_V_DIM)
        lam_init = 0.8 - 0.6 * math.exp(-0.3 * l)
        lv = diff_lambda[l].astype(jnp.float32)
        lam = jnp.exp(jnp.sum(lv[0] * lv[1])) - jnp.exp(jnp.sum(lv[2] * lv[3])) + lam_init
        oa = diff_attention(qa, ka, va, lam)
        oa = rms_norm(oa, diff_head_g[l]) * (1.0 - lam_init)
        ya = oa.reshape(b, s, A_WIDTH) @ w_a_out[l]

        qb = apply_rope(qb.reshape(b, s, B_GROUPS, B_HEADS, B_HEAD_DIM), cos_b, sin_b)
        kb = apply_rope(kb.reshape(b, s, B_GROUPS, B_HEADS, B_HEAD_DIM), cos_b, sin_b)
        vb = vb.reshape(b, s, B_GROUPS, B_HEADS, B_HEAD_DIM)
        outs, lses = [], []
        for g, (window, dil) in enumerate(B_PAIRS):
            o_g, lse_g = dilated_group(qb[:, :, g], kb[:, :, g], vb[:, :, g], window, dil)
            outs.append(o_g)
            lses.append(lse_g)
        wts = jax.nn.softmax(jnp.stack(lses, axis=0), axis=0)
        ob = jnp.einsum('gbsh,gbshd->bshd', wts.astype(x.dtype), jnp.stack(outs, axis=0))
        yb = ob.reshape(b, s, B_WIDTH) @ w_b_out[l]

        g_a, g_b = jnp.split(jax.nn.sigmoid(gates), 2, axis=-1)
        mix = (g_a * ya + g_b * yb) @ w_mix_out[l]
        x = x + rms_norm(mix, post_mix_g[l])

        h = rms_norm(x, pre_ffn_g[l])
        u = causal_depthwise_conv(h @ w_up[l], conv_w[l], conv_b[l])
        gate, val = jnp.split(u, 2, axis=-1)
        y = (jax.nn.gelu(gate, approximate=True) * val) @ w_down[l]
        x = x + rms_norm(y, post_ffn_g[l])
    return x


DEPTH_2 = 2

HEAD_DIM = 64
NSA_HEADS = 4
NSA_KV_HEADS = 1
CMP_LEN = 32
CMP_STRIDE = 16
CMP_HIDDEN = 128
SEL_BLOCK = 64
SEL_TOP = 16
NSA_WINDOW = 512
MLA_HEADS = 4
MLA_Q_RANK = 256
MLA_KV_RANK = 128
MLA_NOPE = 64
MLA_ROPE = 32
MLA_V = 64
SWA_HEADS = 8
SWA_KV_HEADS = 1
SWA_WINDOW = 128
REL_BUCKETS = 32
REL_MAX_DIST = 512
N_BIAS_HEADS = NSA_HEADS + SWA_HEADS

NEG = -1e30
BIG = 1e9

W_A = NSA_HEADS * HEAD_DIM
W_B = MLA_HEADS * MLA_V
W_C = SWA_HEADS * HEAD_DIM
D_MIX = W_A + W_B + W_C

A_Q = NSA_HEADS * HEAD_DIM
A_KV = 6 * NSA_KV_HEADS * HEAD_DIM
A_GATE = 3 * NSA_HEADS
B_CQ = MLA_Q_RANK
B_CKV = MLA_KV_RANK
B_KR = MLA_ROPE
C_Q = SWA_HEADS * HEAD_DIM
C_KV = 2 * SWA_KV_HEADS * HEAD_DIM
IN_SIZES = (A_Q, A_KV, A_GATE, B_CQ, B_CKV, B_KR, C_Q, C_KV, D_MIX)
D_IN = A_Q + A_KV + A_GATE + B_CQ + B_CKV + B_KR + C_Q + C_KV + D_MIX


def rms_norm_2(x, g):
    xf = x.astype(jnp.float32)
    y = xf * lax.rsqrt(jnp.mean(xf * xf, axis=-1, keepdims=True) + NORM_EPS)
    return (y * g.astype(jnp.float32)).astype(x.dtype)

def split_cols(h):
    outs, o = [], 0
    for s in IN_SIZES:
        outs.append(h[..., o:o + s])
        o += s
    return outs

def t5_bucket(dist):
    dist = jnp.maximum(dist, 0)
    exact = REL_BUCKETS // 2
    large = exact + (jnp.log(jnp.maximum(dist, 1).astype(jnp.float32) / exact)
                     / math.log(REL_MAX_DIST / exact) * (REL_BUCKETS - exact)).astype(jnp.int32)
    large = jnp.minimum(large, REL_BUCKETS - 1)
    return jnp.where(dist < exact, dist, large)

def rope(x, pos):
    half = x.shape[-1] // 2
    inv = ROPE_THETA ** (-jnp.arange(half, dtype=jnp.float32) / half)
    ang = pos.astype(jnp.float32)[:, None] * inv[None, :]
    cos, sin = jnp.cos(ang)[:, None, :], jnp.sin(ang)[:, None, :]
    x1, x2 = x[..., :half].astype(jnp.float32), x[..., half:].astype(jnp.float32)
    return jnp.concatenate([x1 * cos - x2 * sin, x2 * cos + x1 * sin], axis=-1).astype(x.dtype)

def banded_attention(q, k, v, window, bias_heads, sinks):
    B, T, H, dh = q.shape
    G = k.shape[2]
    hpg = H // G
    nq = T // Q_BLOCK
    nb = window // Q_BLOCK
    K = (nb + 1) * Q_BLOCK
    pad = ((0, 0), (nb * Q_BLOCK, 0), (0, 0), (0, 0))

    def band(t):
        tp = jnp.pad(t, pad).reshape(B, nq + nb, Q_BLOCK, G, dh)
        return jnp.concatenate([tp[:, i:i + nq] for i in range(nb + 1)], axis=2)

    kb, vb = band(k), band(v)
    qb = q.reshape(B, nq, Q_BLOCK, G, hpg, dh)
    logits = jnp.einsum('bnqghd,bnkgd->bnghqk', qb, kb).astype(jnp.float32) * (dh ** -0.5)
    i = jnp.arange(Q_BLOCK)[:, None]
    j = jnp.arange(K)[None, :]
    dist = nb * Q_BLOCK + i - j
    kpos = (jnp.arange(nq)[:, None, None] - nb) * Q_BLOCK + j[None]
    mask = (dist >= 0) & (dist < window) & (kpos >= 0)
    bias = bias_heads[:, t5_bucket(dist)].reshape(G, hpg, Q_BLOCK, K)
    logits = jnp.where(mask[None, :, None, None], logits + bias, NEG)
    if sinks is None:
        p = jax.nn.softmax(logits, axis=-1)
    else:
        s = jnp.broadcast_to(sinks.reshape(G, hpg, 1, 1).astype(jnp.float32), logits.shape[:-1] + (1,))
        p = jax.nn.softmax(jnp.concatenate([logits, s], axis=-1), axis=-1)[..., :-1]
    out = jnp.einsum('bnghqk,bnkgd->bnqghd', p.astype(v.dtype), vb)
    return out.reshape(B, T, H, dh)

def causal_block_attention(q, k, v, scale):
    B, T, H, dk = q.shape
    nq = T // Q_BLOCK
    qb = q.reshape(B, nq, Q_BLOCK, H, dk).transpose(1, 0, 2, 3, 4)
    kpos = jnp.arange(T)

    def one(args):
        qc, n = args
        logits = jnp.einsum('bqhd,bkhd->bhqk', qc, k).astype(jnp.float32) * scale
        qpos = n * Q_BLOCK + jnp.arange(Q_BLOCK)
        mask = kpos[None, :] <= qpos[:, None]
        p = jax.nn.softmax(jnp.where(mask, logits, NEG), axis=-1)
        return jnp.einsum('bhqk,bkhd->bqhd', p.astype(v.dtype), v)

    out = lax.map(one, (qb, jnp.arange(nq)))
    return out.transpose(1, 0, 2, 3, 4).reshape(B, T, H, v.shape[-1])

def nsa_attention(q, kv, gates, cmp_pos, cmp_w1, cmp_w2, bias_heads):
    B, T, H, dh = q.shape
    G = kv.shape[3]
    hpg = H // G
    scale = dh ** -0.5
    k_cmp, v_cmp, k_slc, v_slc, k_win, v_win = [kv[:, :, i] for i in range(6)]
    pos = jnp.arange(T)
    qg = q.reshape(B, T, G, hpg, dh)

    nc = T // CMP_STRIDE - 1

    def compress(t, pe, w1, w2):
        ch = t.reshape(B, T // CMP_STRIDE, CMP_STRIDE, G, dh)
        blk = jnp.concatenate([ch[:, :-1], ch[:, 1:]], axis=2) + pe[:, None, :]
        blk = blk.transpose(0, 1, 3, 2, 4).reshape(B, nc, G, CMP_LEN * dh)
        return jax.nn.silu(blk @ w1) @ w2

    kc = compress(k_cmp, cmp_pos[0], cmp_w1[0], cmp_w2[0])
    vc = compress(v_cmp, cmp_pos[1], cmp_w1[1], cmp_w2[1])
    lc = jnp.einsum('btghd,bcgd->bghtc', qg, kc).astype(jnp.float32) * scale
    cend = jnp.arange(nc) * CMP_STRIDE + CMP_LEN - 1
    dist_c = pos[:, None] - cend[None, :]
    valid_c = dist_c >= 0
    lc = lc + bias_heads[:, t5_bucket(dist_c)].reshape(G, hpg, T, nc)
    p_c = jax.nn.softmax(jnp.where(valid_c, lc, NEG), axis=-1) * valid_c
    o_cmp = jnp.einsum('bghtc,bcgd->btghd', p_c.astype(vc.dtype), vc)

    ns = T // SEL_BLOCK
    n_top = min(SEL_TOP, ns)
    sstart = np.arange(ns) * SEL_BLOCK
    cstart = np.arange(nc) * CMP_STRIDE
    overlap = (np.clip(np.minimum(cstart[:, None] + CMP_LEN, sstart[None, :] + SEL_BLOCK)
                       - np.maximum(cstart[:, None], sstart[None, :]), 0, None) / CMP_STRIDE).astype(np.float32)
    imp = jnp.einsum('bghtc,cs->bgts', p_c, jnp.asarray(overlap))
    blk = jnp.arange(ns)[None, :]
    cur = (pos // SEL_BLOCK)[:, None]
    forced = (blk == 0) | (blk == cur) | (blk == cur - 1)
    imp = jnp.where(forced, BIG, jnp.where(blk <= cur, imp, -BIG))
    _, idx = lax.top_k(imp, n_top)

    ksb = k_slc.reshape(B, ns, SEL_BLOCK, G, dh).transpose(0, 3, 1, 2, 4)
    vsb = v_slc.reshape(B, ns, SEL_BLOCK, G, dh).transpose(0, 3, 1, 2, 4)
    nq = T // Q_BLOCK
    qch = qg.reshape(B, nq, Q_BLOCK, G, hpg, dh).transpose(1, 0, 3, 4, 2, 5)
    ich = idx.reshape(B, G, nq, Q_BLOCK, n_top).transpose(2, 0, 1, 3, 4)
    gather = jax.vmap(jax.vmap(lambda blocks, ids: blocks[ids]))
    tok = jnp.arange(SEL_BLOCK)
    bias_g = bias_heads.reshape(G, hpg, REL_BUCKETS)
    group_bias = jax.vmap(lambda tab, bk: jnp.moveaxis(tab[:, bk], 0, 1), in_axes=(0, 1), out_axes=1)
    nk = n_top * SEL_BLOCK

    def sel_block(args):
        qc, ic, n = args
        kg = gather(ksb, ic).reshape(B, G, Q_BLOCK, nk, dh)
        vg = gather(vsb, ic).reshape(B, G, Q_BLOCK, nk, dh)
        kpos = (ic[..., None] * SEL_BLOCK + tok).reshape(B, G, Q_BLOCK, nk)
        qpos = n * Q_BLOCK + jnp.arange(Q_BLOCK)
        dist = qpos[:, None] - kpos
        l = jnp.einsum('bghqd,bgqkd->bghqk', qc, kg).astype(jnp.float32) * scale
        l = l + group_bias(bias_g, t5_bucket(dist))
        p = jax.nn.softmax(jnp.where((dist >= 0)[:, :, None], l, NEG), axis=-1)
        return jnp.einsum('bghqk,bgqkd->bqghd', p.astype(vg.dtype), vg)

    o_slc = lax.map(sel_block, (qch, ich, jnp.arange(nq)))
    o_slc = o_slc.transpose(1, 0, 2, 3, 4, 5).reshape(B, T, H, dh)

    o_win = banded_attention(q, k_win, v_win, NSA_WINDOW, bias_heads, None)

    g = jax.nn.sigmoid(gates.astype(jnp.float32)).astype(q.dtype)
    o = (g[..., 0:1] * o_cmp.reshape(B, T, H, dh) + g[..., 1:2] * o_slc + g[..., 2:3] * o_win)
    return o.reshape(B, T, H * dh)

def hybrid_layer(x, w_in, w_out, g_pre, g_post, cmp_pos, cmp_w1, cmp_w2,
                 q_norm, w_uq, kv_norm, w_ukv, sinks, rel_bias):
    B, T, _ = x.shape
    pos = jnp.arange(T)
    h = rms_norm_2(x, g_pre)
    a_q, a_kv, a_g, b_cq, b_ckv, b_kr, c_q, c_kv, z = split_cols(h @ w_in)

    o_a = nsa_attention(a_q.reshape(B, T, NSA_HEADS, HEAD_DIM),
                        a_kv.reshape(B, T, 6, NSA_KV_HEADS, HEAD_DIM),
                        a_g.reshape(B, T, NSA_HEADS, 3),
                        cmp_pos, cmp_w1, cmp_w2, rel_bias[:NSA_HEADS])

    qb = (rms_norm_2(b_cq, q_norm) @ w_uq).reshape(B, T, MLA_HEADS, MLA_NOPE + MLA_ROPE)
    q_full = jnp.concatenate([qb[..., :MLA_NOPE], rope(qb[..., MLA_NOPE:], pos)], axis=-1)
    kvb = (rms_norm_2(b_ckv, kv_norm) @ w_ukv).reshape(B, T, MLA_HEADS, MLA_NOPE + MLA_V)
    k_rope = rope(b_kr.reshape(B, T, 1, MLA_ROPE), pos)
    k_full = jnp.concatenate([kvb[..., :MLA_NOPE],
                              jnp.broadcast_to(k_rope, (B, T, MLA_HEADS, MLA_ROPE))], axis=-1)
    o_b = causal_block_attention(q_full, k_full, kvb[..., MLA_NOPE:], (MLA_NOPE + MLA_ROPE) ** -0.5)

    ckv = c_kv.reshape(B, T, 2, SWA_KV_HEADS, HEAD_DIM)
    o_c = banded_attention(c_q.reshape(B, T, SWA_HEADS, HEAD_DIM), ckv[:, :, 0], ckv[:, :, 1],
                           SWA_WINDOW, rel_bias[NSA_HEADS:], sinks)

    mixed = jnp.concatenate([o_a, o_b.reshape(B, T, W_B), o_c.reshape(B, T, W_C)], axis=-1) * jax.nn.silu(z)
    return x + rms_norm_2(mixed @ w_out, g_post)

def second_inputs(seed: int = 0) -> dict:
    key = jax.random.key(seed)
    ks = jax.random.split(key, 14)
    f32 = jnp.float32

    def nrm(k, shape, scale):
        return jax.random.normal(k, shape, f32) * scale

    return {
        'x': nrm(ks[0], (BATCH, SEQ, D_MODEL), 1.0),
        'w_in': nrm(ks[1], (DEPTH_2, D_MODEL, D_IN), D_MODEL ** -0.5),
        'w_out': nrm(ks[2], (DEPTH_2, D_MIX, D_MODEL), D_MIX ** -0.5),
        'norm_pre': 1.0 + nrm(ks[3], (DEPTH_2, D_MODEL), 0.05),
        'norm_post': 1.0 + nrm(ks[4], (DEPTH_2, D_MODEL), 0.05),
        'cmp_pos': nrm(ks[5], (DEPTH_2, 2, CMP_LEN, HEAD_DIM), 0.1),
        'cmp_w1': nrm(ks[6], (DEPTH_2, 2, CMP_LEN * HEAD_DIM, CMP_HIDDEN), (CMP_LEN * HEAD_DIM) ** -0.5),
        'cmp_w2': nrm(ks[7], (DEPTH_2, 2, CMP_HIDDEN, HEAD_DIM), CMP_HIDDEN ** -0.5),
        'mla_q_norm': 1.0 + nrm(ks[8], (DEPTH_2, MLA_Q_RANK), 0.05),
        'mla_w_uq': nrm(ks[9], (DEPTH_2, MLA_Q_RANK, MLA_HEADS * (MLA_NOPE + MLA_ROPE)), MLA_Q_RANK ** -0.5),
        'mla_kv_norm': 1.0 + nrm(ks[10], (DEPTH_2, MLA_KV_RANK), 0.05),
        'mla_w_ukv': nrm(ks[11], (DEPTH_2, MLA_KV_RANK, MLA_HEADS * (MLA_NOPE + MLA_V)), MLA_KV_RANK ** -0.5),
        'swa_sinks': nrm(ks[12], (DEPTH_2, SWA_HEADS), 0.5),
        'rel_bias': nrm(ks[13], (N_BIAS_HEADS, REL_BUCKETS), 0.5),
    }

def second_block(x, w_in, w_out, norm_pre, norm_post, cmp_pos, cmp_w1, cmp_w2,
              mla_q_norm, mla_w_uq, mla_kv_norm, mla_w_ukv, swa_sinks, rel_bias):
    for l in range(DEPTH_2):
        x = hybrid_layer(x, w_in[l], w_out[l], norm_pre[l], norm_post[l],
                         cmp_pos[l], cmp_w1[l], cmp_w2[l],
                         mla_q_norm[l], mla_w_uq[l], mla_kv_norm[l], mla_w_ukv[l],
                         swa_sinks[l], rel_bias)
    return x


def setup_inputs(seed=0):
    out = dict(first_inputs(seed))
    for name, value in second_inputs(seed + 1).items():
        if name != "x":
            out[name + "_2"] = value
    return out


def reference(
    x, positions, pre_mix_g, w_in, diff_lambda, diff_head_g, w_a_out, w_b_out, w_mix_out,
    post_mix_g, pre_ffn_g, w_up, conv_w, conv_b, w_down, post_ffn_g, w_in_2, w_out_2,
    norm_pre_2, norm_post_2, cmp_pos_2, cmp_w1_2, cmp_w2_2, mla_q_norm_2, mla_w_uq_2,
    mla_kv_norm_2, mla_w_ukv_2, swa_sinks_2, rel_bias_2,
):
    x = first_block(
        x, positions, pre_mix_g, w_in, diff_lambda, diff_head_g, w_a_out, w_b_out, w_mix_out,
        post_mix_g, pre_ffn_g, w_up, conv_w, conv_b, w_down, post_ffn_g,
    )
    return second_block(
        x, w_in_2, w_out_2, norm_pre_2, norm_post_2, cmp_pos_2, cmp_w1_2, cmp_w2_2,
        mla_q_norm_2, mla_w_uq_2, mla_kv_norm_2, mla_w_ukv_2, swa_sinks_2, rel_bias_2,
    )


_drawn_inputs = setup_inputs


def setup_inputs(seed=0):
    import zlib

    import numpy as np

    out = dict(_drawn_inputs(seed))
    spreads = {}
    factors = {'diff_lambda': 3.92,
     'conv_b': 4.646,
     'mla_q_norm_2': 7.271,
     'mla_kv_norm_2': 2.763,
     'swa_sinks_2': 8.0,
     'cmp_pos_2': 3.228}
    for name, (base, spread) in spreads.items():
        noise = np.random.default_rng([zlib.crc32(name.encode()), seed]).standard_normal(out[name].shape)
        drawn = base * np.exp(spread * noise) if base else spread * noise
        out[name] = __import__('jax').numpy.asarray(drawn.astype(out[name].dtype))
    for name, factor in factors.items():
        out[name] = (out[name] * factor).astype(out[name].dtype)
    return out
```

```python
import math
from contextlib import ExitStack

import numpy as np

import concourse.bass as bass
from concourse import mybir

F32 = mybir.dt.float32
I32 = mybir.dt.int32
ALU = mybir.AluOpType
ACT = mybir.ActivationFunctionType
AX_X = mybir.AxisListType.X

P = 128
T = 512
TT = T // P
D = 1024
DC = D // P
EPS = 1e-6
NEG = -1e30
FF = 2816
FC = FF // P
HEADS = 4
CLASSES = 4
A_DIM = 64
LAM_INIT = 0.8 - 0.6 * math.exp(0.0)
LAYERS = 2
NSA_H, MLA_H, SWA_H = 4, 4, 8
HD = 64
CMP = T // 16 - 1
D_IN2 = 2732
THETA = 10000.0
LOOK = 2
NPROB = 4

VECS = {"pre_mix_g": (0, 8), "post_mix_g": (8, 8), "pre_ffn_g": (16, 8), "post_ffn_g": (24, 8),
        "norm_pre_2": (32, 16), "norm_post_2": (48, 16), "mla_q_norm_2": (64, 4), "mla_kv_norm_2": (68, 2),
        "diff_head_g": (70, 1)}
NVEC = 71


def shape_constants():
    f = np.float32
    p = np.arange(P)
    cols = np.zeros((P, 8), f)
    inv64 = f(THETA) ** (-np.arange(0, 64, 2, dtype=f) / f(64))
    inv128 = f(THETA) ** (-np.arange(0, 128, 2, dtype=f) / f(128))
    cols[:, 0] = inv64[p % 32]
    cols[:, 1] = inv128[p % 64]
    cols[:, 2] = np.where(p % 64 < 32, 1.0, -1.0)
    cols[:, 3] = np.where(p < 64, 1.0, -1.0)
    cols[:, 4] = p >= 31
    j = np.arange(T)
    causal = np.where(p[:, None] + (T - P) - j[None] >= 0, 0.0, NEG).astype(f)
    i = np.arange(P)
    mask_b = np.full((P, CLASSES, 6 * P), NEG, f)
    for r in range(CLASSES):
        for b in range(CLASSES):
            dist = CLASSES * (p[:, None] - i[None]) + r - b
            mask_b[:, r, b * P:(b + 1) * P] = np.where((dist >= 0) & (dist <= 128), 0.0, NEG)
        back = p[:, None] - i[None]
        mask_b[:, r, 4 * P:5 * P] = np.where(back >= 0, 0.0, NEG)
        mask_b[:, r, 5 * P:6 * P] = np.where((back >= 0) & (back % 4 == 0), 0.0, NEG)
    dist = np.arange(-T, T)
    d0 = np.maximum(dist, 0)
    large = 16 + (np.log(np.maximum(d0, 1).astype(f) / f(16)) / f(math.log(512 / 16)) * f(16)).astype(np.int32)
    bucket = np.where(d0 < 16, d0, np.minimum(large, 31))
    hot = np.zeros((34, 2 * T), f)
    hot[bucket, np.arange(2 * T)] = 1.0
    hot[32] = np.where(dist < 0, NEG, 0.0)
    hot[33] = np.where(dist >= 128, NEG, 0.0)
    back_hot = np.zeros_like(hot)
    back_hot[:, :2 * T - 1] = hot[:, 1:][:, ::-1]
    mask_rows = np.zeros((2, NSA_H + SWA_H), f)
    mask_rows[0] = 1.0
    mask_rows[1, NSA_H:] = 1.0
    inv32 = f(THETA) ** (-np.arange(16, dtype=f) / f(16))
    ang = np.arange(T, dtype=f)[None] * inv32[:, None]
    cos, sin = np.cos(ang), np.sin(ang)
    rope_m = np.concatenate([cos, cos, -sin, sin]).astype(f)
    return {"c_cols": cols, "c_causal": causal, "c_mask_b": mask_b, "c_hot": hot, "c_back_hot": back_hot,
            "c_mask_rows": mask_rows, "c_rope_m": rope_m}


class Counted:

    def __init__(self, handle):
        self.handle, self.base = handle, 0

    def at(self, n):
        return self.base + n

    def close(self, n):
        self.base += n


class Ring:

    SLOTS = 2

    def __init__(self, tensor, loaded, free):
        self.tensor, self.loaded, self.free = tensor, loaded, free
        self.loads = self.uses = 0
        self.total = [0, 0]
        self.seen = []

    def slot(self, n, *shape):
        v = self.tensor[:, n % 2, 0:int(np.prod(shape))]
        names = "abc"[:len(shape)]
        if len(shape) == 1:
            return v
        return v.rearrange(f"p ({' '.join(names)}) -> p {' '.join(names)}", **dict(zip(names, shape)))

    def load(self, sp, parts, it=None, pairs=0):
        n = self.loads
        s = n % 2
        if n >= 2 or it is not None:
            sp.wait_ge(self.free[s], n // 2 + (0 if it is None else it * pairs))
        for dst, src in parts:
            sp.dma_start(dst(n), src).then_inc(self.loaded[s], 16)
        self.total[s] += 16 * len(parts)
        self.seen.append(self.total[s])
        self.loads += 1

    def use(self, pe, it=None, step=0):
        n = self.uses
        pe.wait_ge(self.loaded[n % 2], self.seen[n] + (0 if it is None else it * step))
        self.uses += 1
        return n

    def skip(self, rounds, slots, parts):
        for _ in range(rounds):
            for _ in range(slots):
                self.total[self.loads % 2] += 16 * parts
                self.seen.append(self.total[self.loads % 2])
                self.loads += 1


class Kit:
    pass


def columns(w, r0, kt, c0, n):
    return w[r0:r0 + kt * P, c0:c0 + n].rearrange("(k p) n -> p k n", p=P)



def stage_setup(nc, K, dr):
    with ExitStack() as ctx:
        def sb(name, shape, dt=F32):
            return ctx.enter_context(nc.sbuf_tensor(name, shape, dt))

        def sem(name):
            return ctx.enter_context(nc.semaphore(name))

        x_tok = sb("x_tok", [P, TT, D])
        vec_rows = sb("vec_rows", [NVEC, P])
        conv_rows = sb("conv_rows", [2 * FC, 4, P])
        pos_rows = sb("pos_rows", [P, P])
        pos_i = sb("pos_i", [P, T], I32)
        pos_f = sb("pos_f", [P, T])
        ang = sb("ang", [P, T])
        turns = sb("turns", [P, T])
        red = sb("red", [P, T])
        lam_in = sb("lam_in", [P, 4 * A_DIM])
        lam_prod = sb("lam_prod", [P, 2, A_DIM])
        lam_sum = sb("lam_sum", [P, 2])
        lam_exp = sb("lam_exp", [P, 2])
        s_in, s_ident, s_tr = sem("setup_loaded"), sem("ident_ready"), sem("setup_transposed")
        s_free_v, s_free_a = sem("setup_bank_free_dve"), sem("setup_bank_free_act")
        s_red, s_sin, s_lsum, s_lexp = sem("angle_reduced"), sem("sin_done"), sem("lam_summed"), sem("lam_exped")
        block = ctx.enter_context(nc.Block())
        n_loads = 0

        @block.sync
        def _(sp):
            nonlocal n_loads

            def load(dst, src):
                nonlocal n_loads
                sp.dma_start(dst, src).then_inc(s_in, 16)
                n_loads += 1

            load(x_tok[:], dr["x"].rearrange("b (t p) d -> p (b t) d", p=P))
            for name, (r0, n) in VECS.items():
                load(vec_rows[r0:r0 + n, :], dr[name].rearrange("l (c p) -> (l c) p", p=P))
            load(conv_rows[:, 0:3, :], dr["conv_w"].rearrange("l j (c p) -> c (l j) p", p=P))
            load(conv_rows[:, 3, :], dr["conv_b"].rearrange("l (c p) -> (l c) p", p=P))
            for half in range(2):
                load(pos_rows[:, half * HD:(half + 1) * HD], dr["cmp_pos_2"].rearrange("l i s d -> (l i s) d"))
            load(pos_i[:], dr["positions"].partition_broadcast(P)[:, 0, :])
            load(lam_in[:], dr["diff_lambda"].rearrange("l a d -> l (a d)").partition_broadcast(P)[:, 0, :])
            load(K.cols[:], dr["c_cols"])
            load(K.causal[:], dr["c_causal"])

        @block.gpsimd
        def _(pool):
            nc.gpsimd.memset(K.ident[:], 0.0)
            nc.gpsimd.memset(K.ones[:], 1.0)
            nc.gpsimd.memset(K.eps[:], EPS)
            pool.drain()
            nc.gpsimd.affine_select(out=K.ident[:], in_=K.ident[:], compare_op=ALU.not_equal, fill=1.0, base=0,
                                    pattern=[[-1, P]], channel_multiplier=1).then_inc(s_ident, 1)

        N_TR = DC + 6

        @block.tensor
        def _(pe):
            pe.wait_ge(s_ident, 1)
            pe.wait_ge(s_in, 16 * n_loads)
            for n in range(N_TR):
                if n >= 8:
                    pe.wait_ge((s_free_v, s_free_a)[n % 2], (n - 8) // 2 + 1)
                bank = K.ps[:, n % 8, :]
                if n < DC:
                    for t in range(TT):
                        last = nc.tensor.transpose(bank[:, t * P:(t + 1) * P], x_tok[:, t, n * P:(n + 1) * P], K.ident[:])
                elif n == DC:
                    last = nc.tensor.transpose(bank[:, 0:NVEC], vec_rows[:], K.ident[0:NVEC, 0:NVEC])
                elif n < DC + 5:
                    last = nc.tensor.transpose(bank[:, 0:2 * FC], conv_rows[:, n - DC - 1, :], K.ident[0:2 * FC, 0:2 * FC])
                else:
                    last = nc.tensor.transpose(bank[:, 0:P], pos_rows[:], K.ident[:])
                last.then_inc(s_tr, 1)

        def copy_of(n):
            bank = K.ps[:, n % 8, :]
            if n < DC:
                return K.xT[:, n, :], bank[:, 0:T]
            if n == DC:
                return K.vec[:], bank[:, 0:NVEC]
            if n < DC + 5:
                return K.conv[:, n - DC - 1, :], bank[:, 0:2 * FC]
            return K.peT[:], bank[:, 0:P]

        TWO_PI = 2 * math.pi
        HI = 6.28125
        MID = float(np.float32(np.round((TWO_PI - HI) * 2 ** 21) / 2 ** 21))
        LO = TWO_PI - HI - MID
        MAGIC = 1.5 * 2 ** 23
        tables = [(0, 0, K.sin_a), (0, 1, K.cos_a), (1, 0, K.sin_b), (1, 1, K.cos_b)]

        @block.vector
        def _(dve):
            v = nc.vector
            dve.wait_ge(s_in, 16 * n_loads)
            for n in range(0, N_TR, 2):
                dve.wait_ge(s_tr, n + 1)
                v.tensor_copy(*copy_of(n)).then_inc(s_free_v, 1)
            lam4 = lam_in[:].rearrange("p (a d) -> p a d", d=A_DIM)
            v.tensor_tensor(lam_prod[:], lam4[:, 0:4:2, :], lam4[:, 1:4:2, :], ALU.mult)
            v.tensor_copy(pos_f[:], pos_i[:])
            dve.drain()
            v.reduce_sum(lam_sum[:], lam_prod[:], AX_X).then_inc(s_lsum, 1)
            for n, (col, quarter, _) in enumerate(tables):
                if not quarter:
                    v.tensor_scalar(ang[:], pos_f[:], K.cols[:, col:col + 1], None, ALU.mult)
                    dve.drain()
                v.tensor_scalar(turns[:], ang[:], 1 / TWO_PI, 0.25 * quarter, ALU.mult, ALU.add)
                dve.drain()
                v.tensor_scalar(turns[:], turns[:], MAGIC, None, ALU.add)
                dve.drain()
                v.tensor_scalar(turns[:], turns[:], MAGIC, None, ALU.subtract)
                dve.drain()
                if n:
                    dve.wait_ge(s_sin, n)
                v.scalar_tensor_tensor(out=red[:], in0=turns[:], scalar=-HI, in1=ang[:], op0=ALU.mult, op1=ALU.add)
                dve.drain()
                v.scalar_tensor_tensor(out=red[:], in0=turns[:], scalar=-MID, in1=red[:], op0=ALU.mult, op1=ALU.add)
                dve.drain()
                v.scalar_tensor_tensor(out=red[:], in0=turns[:], scalar=-LO, in1=red[:], op0=ALU.mult, op1=ALU.add)
                dve.drain()
                if quarter:
                    v.tensor_scalar(red[:], red[:], math.pi / 2, None, ALU.add)
                    dve.drain()
                v.tensor_scalar(red[:], red[:], 3.1415925, -3.1415925, ALU.min, ALU.max).then_inc(s_red, 1)
            dve.wait_ge(s_sin, 4)
            v.tensor_scalar(K.sin_a[:], K.sin_a[:], K.cols[:, 2:3], None, ALU.mult)
            v.tensor_scalar(K.sin_b[:], K.sin_b[:], K.cols[:, 3:4], None, ALU.mult)
            dve.wait_ge(s_lexp, 1)
            v.tensor_scalar(K.neg_lam[:], lam_exp[:, 1:2], lam_exp[:, 0:1], -LAM_INIT, ALU.subtract, ALU.add)
            v.tensor_scalar(K.vec[:, 70:71], K.vec[:, 70:71], 1.0 - LAM_INIT, None, ALU.mult)
            dve.drain()

        @block.scalar
        def _(act):
            for n in range(1, N_TR, 2):
                act.wait_ge(s_tr, n + 1)
                nc.scalar.activation(*copy_of(n), ACT.Copy).then_inc(s_free_a, 1)
            act.wait_ge(s_lsum, 1)
            nc.scalar.activation(lam_exp[:], lam_sum[:], ACT.Exp).then_inc(s_lexp, 1)
            for n, (_, _, table) in enumerate(tables):
                act.wait_ge(s_red, n + 1)
                nc.scalar.activation(table[:], red[:], ACT.Sin).then_inc(s_sin, 1)


def stage_norm(nc, K, src, chunks, gain, dst, dim):
    with ExitStack() as ctx:
        sq = ctx.enter_context(nc.sbuf_tensor(K.name("sq"), [P, 2, T], F32))
        rstd = ctx.enter_context(nc.sbuf_tensor(K.name("rstd"), [P, T], F32))
        block = ctx.enter_context(nc.Block())
        stat = K.ps[:, 0, :]
        squared, summed, rooted = K.s("squared"), K.s("summed"), K.s("rooted")

        @block.scalar
        def _(act):
            for c in range(chunks):
                if c >= 2:
                    act.wait_ge(summed.handle, summed.at(c - 1))
                nc.scalar.activation(sq[:, c % 2, :], src(c), ACT.Square).then_inc(squared.handle, 1)
            act.wait_ge(summed.handle, summed.at(chunks))
            nc.scalar.activation(rstd[:], stat, ACT.Sqrt, bias=K.eps[:], scale=1.0 / dim).then_inc(rooted.handle, 1)

        @block.tensor
        def _(pe):
            for c in range(chunks):
                pe.wait_ge(squared.handle, squared.at(c + 1))
                nc.tensor.matmul(stat, K.ones[:], sq[:, c % 2, :], start=(c == 0), stop=(c == chunks - 1))\
                    .then_inc(summed.handle, 1)

        @block.vector
        def _(dve):
            dve.wait_ge(rooted.handle, rooted.at(1))
            nc.vector.reciprocal(rstd[:], rstd[:])
            dve.drain()
            for c in range(chunks):
                nc.vector.scalar_tensor_tensor(out=dst(c), in0=src(c), scalar=gain(c), in1=rstd[:],
                                               op0=ALU.mult, op1=ALU.mult)
            dve.drain()

        squared.close(chunks)
        summed.close(chunks)
        rooted.close(1)


def stage_head_norm(nc, K, oT, gain):
    with ExitStack() as ctx:
        sq = ctx.enter_context(nc.sbuf_tensor(K.name("hsq"), [P, HEADS, T], F32))
        rstd = ctx.enter_context(nc.sbuf_tensor(K.name("hrstd"), [P, HEADS, T], F32))
        block = ctx.enter_context(nc.Block())
        squared, summed, rooted = K.s("squared"), K.s("summed"), K.s("rooted")

        @block.scalar
        def _(act):
            for h in range(HEADS):
                nc.scalar.activation(sq[:, h, :], oT[:, h, :], ACT.Square).then_inc(squared.handle, 1)
            for h in range(HEADS):
                act.wait_ge(summed.handle, summed.at(h + 1))
                nc.scalar.activation(rstd[:, h, :], K.ps[:, h, :], ACT.Sqrt, bias=K.eps[:], scale=1.0 / P)\
                    .then_inc(rooted.handle, 1)

        @block.tensor
        def _(pe):
            for h in range(HEADS):
                pe.wait_ge(squared.handle, squared.at(h + 1))
                nc.tensor.matmul(K.ps[:, h, :], K.ones[:], sq[:, h, :], start=True, stop=True)\
                    .then_inc(summed.handle, 1)

        @block.vector
        def _(dve):
            for h in range(HEADS):
                dve.wait_ge(rooted.handle, rooted.at(h + 1))
                nc.vector.reciprocal(rstd[:, h, :], rstd[:, h, :])
            dve.drain()
            for h in range(HEADS):
                nc.vector.scalar_tensor_tensor(out=oT[:, h, :], in0=oT[:, h, :], scalar=gain, in1=rstd[:, h, :],
                                               op0=ALU.mult, op1=ALU.mult)
            dve.drain()

        squared.close(HEADS)
        summed.close(HEADS)
        rooted.close(HEADS)


def product(nc, bank, w, src, kt):
    for k in range(kt):
        last = nc.tensor.matmul(bank, w(k), src(k), start=(k == 0), stop=(k == kt - 1))
    return last


def stage_project_a(nc, K, dr, qk, v_tok):
    with ExitStack() as ctx:
        rot = ctx.enter_context(nc.sbuf_tensor(K.name("rot"), [P, 2, T], F32))
        block = ctx.enter_context(nc.Block())
        w_in = dr["w_in"][0]
        ring = K.ring
        ready, free, used = K.s("chunk_ready"), [K.s(f"bank_free{b}") for b in range(4)], ring.free
        N = 2 * HEADS + TT

        @block.sync
        def _(sp):
            for g in range(3):
                ring.load(sp, [(lambda n: ring.slot(n, DC, T), columns(w_in, 0, DC, g * T, T))])

        @block.tensor
        def _(pe):
            for g in range(3):
                n = ring.use(pe)
                w = ring.slot(n, DC, T)
                for j in range(4):
                    c = 4 * g + j
                    if c >= 4:
                        pe.wait_ge(free[c % 4].handle, free[c % 4].at(c // 4))
                    bank = K.ps[:, c % 4, :]
                    for k in range(DC):
                        if g < 2:
                            last = nc.tensor.matmul(bank, w[:, k, j * P:(j + 1) * P], K.hT[:, k, :],
                                                    start=(k == 0), stop=(k == DC - 1))
                        else:
                            last = nc.tensor.matmul(bank, K.hT[:, k, j * P:(j + 1) * P], w[:, k, :],
                                                    start=(k == 0), stop=(k == DC - 1))
                    last.then_inc(ready.handle, 1)
                pe.drain().then_inc(used[n % 2], 1)

        @block.vector
        def _(dve):
            v = nc.vector
            for c in range(N):
                dve.wait_ge(ready.handle, ready.at(c + 1))
                bank = K.ps[:, c % 4, :]
                if c >= 2 * HEADS:
                    v.tensor_copy(v_tok[:, c - 2 * HEADS, :], bank).then_inc(free[c % 4].handle, 1)
                    continue
                for q in range(4):
                    o = 32 * (q ^ 1)
                    v.tensor_tensor(rot[o:o + 32, c % 2, :], bank[32 * q:32 * q + 32, :],
                                    K.sin_a[32 * q:32 * q + 32, :], ALU.mult)
                v.tensor_tensor(qk[:, c, :], bank, K.cos_a[:], ALU.mult).then_inc(free[c % 4].handle, 1)
                dve.drain()
                v.tensor_tensor(qk[:, c, :], qk[:, c, :], rot[:, c % 2, :], ALU.add)
            dve.drain()

        ready.close(N)
        for b in range(4):
            free[b].close(3)


def stage_project_b(nc, K, dr, qk, v_tok):
    with ExitStack() as ctx:
        rot = ctx.enter_context(nc.sbuf_tensor(K.name("rotb"), [P, 2, T], F32))
        block = ctx.enter_context(nc.Block())
        w_in = dr["w_in"][0]
        ring = K.ring
        c0 = 3 * T
        ready, free, used = K.s("chunk_ready"), [K.s(f"bank_free{b}") for b in range(4)], ring.free

        @block.sync
        def _(sp):
            with sp.Fori(0, 3) as i:
                for u in range(2):
                    ring.load(sp, [(lambda n: ring.slot(n, DC, T),
                                    w_in[:, bass.ds(c0 + (2 * i + u) * T, T)].rearrange("(k p) n -> p k n", p=P))],
                              it=i, pairs=1)
            ring.skip(2, 2, 1)
            for g in range(3):
                ring.load(sp, [(lambda n: ring.slot(n, DC, T), columns(w_in, 0, DC, c0 + (6 + g) * T, T))])

        @block.tensor
        def _(pe):
            with pe.Fori(0, 3) as i:
                for u in range(2):
                    n = ring.use(pe, it=i, step=16)
                    w = ring.slot(n, DC, T)
                    for j in range(4):
                        pe.wait_ge(free[j].handle, free[j].at(0) + 2 * i + u)
                        for k in range(DC):
                            last = nc.tensor.matmul(K.ps[:, j, :], w[:, k, j * P:(j + 1) * P], K.hT[:, k, :],
                                                    start=(k == 0), stop=(k == DC - 1))
                        last.then_inc(ready.handle, 1)
                    pe.drain().then_inc(used[n % 2], 1)
            ring.uses += 4
            for g in range(3):
                n = ring.use(pe)
                w = ring.slot(n, DC, T)
                for r in range(CLASSES):
                    pe.wait_ge(free[r].handle, free[r].at(6 + g))
                    for k in range(DC):
                        last = nc.tensor.matmul(K.ps[:, r, :], K.hT[:, k, r:T:CLASSES], w[:, k, :],
                                                start=(k == 0), stop=(k == DC - 1))
                    last.then_inc(ready.handle, 1)
                pe.drain().then_inc(used[n % 2], 1)

        @block.vector
        def _(dve):
            v = nc.vector
            with dve.Fori(0, 6) as g:
                for h in range(4):
                    dve.wait_ge(ready.handle, ready.at(h + 1) + 4 * g)
                    bank = K.ps[:, h, :]
                    for q in range(2):
                        o = 64 * (q ^ 1)
                        v.tensor_tensor(rot[o:o + 64, h % 2, :], bank[64 * q:64 * q + 64, :],
                                        K.sin_b[64 * q:64 * q + 64, :], ALU.mult)
                    v.tensor_tensor(K.rope_tmp[:, h % 2, :], bank, K.cos_b[:], ALU.mult).then_inc(free[h].handle, 1)
                    dve.drain()
                    v.tensor_tensor(qk[:, bass.ds(4 * g + h, 1), :].rearrange("p a (r i) -> p (a i) r", r=CLASSES),
                                    K.rope_tmp[:, h % 2, :].rearrange("p (i r) -> p i r", r=CLASSES),
                                    rot[:, h % 2, :].rearrange("p (i r) -> p i r", r=CLASSES), ALU.add)
            for g in range(3):
                for r in range(CLASSES):
                    dve.wait_ge(ready.handle, ready.at(24 + 4 * g + r + 1))
                    v.tensor_copy(v_tok[:, g, r, :], K.ps[:, r, :]).then_inc(free[r].handle, 1)
            dve.drain()

        ready.close(36)
        for b in range(4):
            free[b].close(9)


def stage_attention(nc, K, jobs, width, n_s, n_t):
    with ExitStack() as ctx:
        def sb(name, shape):
            return ctx.enter_context(nc.sbuf_tensor(K.name(name), shape, F32))

        banks = -(-width // T)
        prob = sb("prob", [P, NPROB, width])
        prob_t = sb("prob_t", [P, 2, width])
        top = sb("top", [P, NPROB])
        neg_top = sb("neg_top", [P, NPROB])
        den = sb("den", [P, NPROB])
        sink_exp = sb("sink_exp", [P, NPROB])
        coef = sb("coef", [P, NPROB])
        block = ctx.enter_context(nc.Block())
        n = len(jobs)
        flat = K.ps[:].rearrange("p b t -> p (b t)")

        def scores_at(j):
            o = (j % n_s) * banks * T
            return flat[:, o:o + width]

        def probs_t_at(j):
            o = (n_s + j % n_t) * banks * T
            return flat[:, o:o + width]

        o_bank = (n_s + n_t) * banks
        group, g = [], 0
        for job in jobs:
            group.append(g)
            g += job["last"]
        n_out = g

        def out_at(j):
            p0, m = jobs[j]["rows"]
            return K.ps[p0:p0 + m, o_bank + group[j] % 2, 0:P]

        scored, masked, topped = K.s("scored"), K.s("masked"), K.s("topped")
        exped, weighed, scaled = K.s("exped"), K.s("weighed"), K.s("scaled")
        turned, copied, mixed, stored = K.s("turned"), K.s("copied"), K.s("mixed"), K.s("stored")

        @block.tensor
        def _(pe):
            def scores(j):
                if j >= n_s:
                    pe.wait_ge(masked.handle, masked.at(j - n_s + 1))
                for c0, q, k in jobs[j]["scores"]:
                    last = nc.tensor.matmul(scores_at(j)[:, c0:c0 + k.shape[-1]], q, k, start=True, stop=True)
                last.then_inc(scored.handle, 1)

            def turn(j):
                pe.wait_ge(scaled.handle, scaled.at(j + 1))
                if j >= n_t:
                    pe.wait_ge(copied.handle, copied.at(j - n_t + 1))
                for c0, m, _ in jobs[j]["values"]:
                    src = prob[:, j % NPROB, c0:c0 + m]
                    if m == P:
                        last = nc.tensor.transpose(probs_t_at(j)[:, c0:c0 + P], src, K.ident[:])
                    else:
                        last = nc.tensor.matmul(probs_t_at(j)[0:m, c0:c0 + P], src, K.ident[:], start=True, stop=True)
                last.then_inc(turned.handle, 1)

            def mix(j):
                pe.wait_ge(copied.handle, copied.at(j + 1))
                if jobs[j]["first"] and group[j] >= 2:
                    pe.wait_ge(stored.handle, stored.at(group[j] - 1))
                values = jobs[j]["values"]
                for i, (c0, m, v) in enumerate(values):
                    last = nc.tensor.matmul(out_at(j), v, prob_t[0:m, j % 2, c0:c0 + P],
                                            start=jobs[j]["first"] and i == 0,
                                            stop=jobs[j]["last"] and i == len(values) - 1)
                last.then_inc(mixed.handle, 1)

            for s in range(n + LOOK + 1):
                if s < n:
                    scores(s)
                if 0 <= s - LOOK < n:
                    turn(s - LOOK)
                if 0 <= s - LOOK - 1 < n:
                    mix(s - LOOK - 1)

        @block.vector
        def _(dve):
            v = nc.vector

            def mask_and_top(j):
                job = jobs[j]
                b, w = j % NPROB, job["width"]
                dve.wait_ge(scored.handle, scored.at(j + 1))
                if j >= NPROB:
                    dve.wait_ge(turned.handle, turned.at(j - NPROB + 1))
                v.tensor_tensor_reduce(out=prob[:, b, 0:w], in0=scores_at(j)[:, 0:w], in1=job["bias"], scale=1.0,
                                       scalar=-3e38, op0=ALU.add, op1=ALU.max, accum_out=top[:, b:b + 1])\
                    .then_inc(masked.handle, 1)
                dve.drain()
                if job["sink"] is None:
                    v.tensor_scalar(neg_top[:, b:b + 1], top[:, b:b + 1], -job["scale"], None, ALU.mult)\
                        .then_inc(topped.handle, 1)
                else:
                    v.tensor_scalar(neg_top[:, b:b + 1], top[:, b:b + 1], job["sink"][0], -job["scale"],
                                    ALU.max, ALU.mult).then_inc(topped.handle, 1)

            def weigh(j):
                job = jobs[j]
                b = j % NPROB
                dve.wait_ge(exped.handle, exped.at(j + 1))
                d = den[:, b:b + 1]
                if job["sink"] is not None:
                    v.tensor_tensor(d, d, sink_exp[:, b:b + 1], ALU.add)
                    dve.drain()
                out = coef[:, b:b + 1]
                if job["gate"] is None:
                    v.reciprocal(out, d).then_inc(weighed.handle, 1)
                else:
                    v.reciprocal(d, d)
                    dve.drain()
                    v.tensor_tensor(out, d, job["gate"], ALU.mult).then_inc(weighed.handle, 1)

            def store(j):
                job = jobs[j]
                if not job["last"]:
                    return
                dve.wait_ge(mixed.handle, mixed.at(j + 1))
                if job["times"] is None:
                    v.tensor_copy(job["out"], out_at(j)).then_inc(stored.handle, 1)
                else:
                    v.tensor_tensor(job["out"], out_at(j), job["times"], ALU.mult).then_inc(stored.handle, 1)

            for s in range(n + LOOK + 2):
                if s < n:
                    mask_and_top(s)
                if 0 <= s - 1 < n:
                    weigh(s - 1)
                if 0 <= s - LOOK - 2 < n:
                    store(s - LOOK - 2)
            dve.drain()

        @block.scalar
        def _(act):
            a = nc.scalar

            def exp(j):
                job = jobs[j]
                b, w = j % NPROB, job["width"]
                act.wait_ge(topped.handle, topped.at(j + 1))
                if job["sink"] is not None:
                    a.activation(sink_exp[:, b:b + 1], job["sink"][1], ACT.Exp, bias=neg_top[:, b:b + 1])
                a.activation(prob[:, b, 0:w], prob[:, b, 0:w], ACT.Exp, bias=neg_top[:, b:b + 1], scale=job["scale"],
                             accum_out=den[:, b:b + 1]).then_inc(exped.handle, 1)

            def copy(j):
                act.wait_ge(turned.handle, turned.at(j + 1))
                if j >= 2:
                    act.wait_ge(mixed.handle, mixed.at(j - 1))
                rows, end = jobs[j]["turned"]
                a.activation(prob_t[0:rows, j % 2, 0:end], probs_t_at(j)[0:rows, 0:end], ACT.Copy)\
                    .then_inc(copied.handle, 1)

            for s in range(n + LOOK):
                if s < n:
                    exp(s)
                if 0 <= s - LOOK < n:
                    copy(s - LOOK)

        @block.gpsimd
        def _(pool):
            for j in range(n):
                b, w = j % NPROB, jobs[j]["width"]
                pool.wait_ge(weighed.handle, weighed.at(j + 1))
                nc.gpsimd.tensor_scalar(prob[:, b, 0:w], prob[:, b, 0:w], coef[:, b:b + 1], None, ALU.mult)\
                    .then_inc(scaled.handle, 1)

        for c in (scored, masked, topped, exped, weighed, scaled, turned, copied, mixed):
            c.close(n)
        stored.close(n_out)


def job(scores, width, bias, scale, values, out, rows=(0, P), first=True, last=True, gate=None, sink=None,
        times=None, turned=None):
    return dict(scores=scores, width=width, bias=bias, scale=scale, values=values, out=out, rows=rows, first=first,
                last=last, gate=gate, sink=sink, times=times, turned=turned or (P, width))


def stage_gate_mix(nc, K, dr, oa, ob, dst):
    with ExitStack() as ctx:
        sig = ctx.enter_context(nc.sbuf_tensor(K.name("sig"), [P, 2, 2, T], F32))
        block = ctx.enter_context(nc.Block())
        ring = K.ring
        w_in, w_a, w_b = dr["w_in"][0], dr["w_a_out"][0], dr["w_b_out"][0]
        gate0 = 8192 - 2 * D
        KA = oa.shape[1]
        parts = 4
        ready, gated, free = K.s("chunk_ready"), K.s("gated"), K.s("bank_free0")
        summed = K.s("summed")

        @block.sync
        def _(sp):
            with sp.Fori(0, DC // 2) as i:
                for u in range(2):
                    def cols(w, kt, c0):
                        return w[:, bass.ds(c0 + (2 * i + u) * P, P)].rearrange("(k p) n -> p k n", p=P)
                    def at(k0, kt):
                        return lambda n: ring.slot(n, 24, P)[:, k0:k0 + kt, :]
                    ring.load(sp, [(at(0, 4), cols(w_a, 4, 0)), (at(4, 4), cols(w_b, 4, 0)),
                                   (at(8, 8), cols(w_in, 8, gate0)), (at(16, 8), cols(w_in, 8, gate0 + D))],
                              it=i, pairs=1)
            ring.skip(DC // 2 - 1, 2, parts)

        @block.tensor
        def _(pe):
            with pe.Fori(0, DC // 2) as i:
                for u in range(2):
                    n = ring.use(pe, it=i, step=16 * parts)
                    w = ring.slot(n, 24, P)
                    pe.wait_ge(free.handle, free.at(u) + 2 * i)
                    for b, (k0, kt, src) in enumerate([(8, 8, K.hT), (16, 8, K.hT), (0, KA, oa), (4, KA, ob)]):
                        for k in range(kt):
                            last = nc.tensor.matmul(K.ps[:, 4 * u + b, :], w[:, k0 + k, :], src[:, k, :],
                                                    start=(k == 0), stop=(k == kt - 1))
                        last.then_inc(ready.handle, 1)
                    pe.drain().then_inc(ring.free[n % 2], 1)
            ring.uses += DC - 2

        @block.scalar
        def _(act):
            with act.Fori(0, DC // 2) as i:
                for u in range(2):
                    act.wait_ge(summed.handle, summed.at(u) + 2 * i)
                    for b in range(2):
                        act.wait_ge(ready.handle, ready.at(4 * u + b + 1) + 8 * i)
                        nc.scalar.activation(sig[:, u, b, :], K.ps[:, 4 * u + b, :], ACT.Sigmoid)\
                            .then_inc(gated.handle, 1)

        @block.vector
        def _(dve):
            v = nc.vector
            dve.drain().then_inc(free.handle, 1)
            dve.drain().then_inc(summed.handle, 1)
            with dve.Fori(0, DC // 2) as i:
                for u in range(2):
                    dve.wait_ge(ready.handle, ready.at(4 * u + 4) + 8 * i)
                    dve.wait_ge(gated.handle, gated.at(2 * u + 2) + 4 * i)
                    v.tensor_tensor(sig[:, u, 0, :], sig[:, u, 0, :], K.ps[:, 4 * u + 2, :], ALU.mult)
                    v.tensor_tensor(sig[:, u, 1, :], sig[:, u, 1, :], K.ps[:, 4 * u + 3, :], ALU.mult)\
                        .then_inc(free.handle, 1)
                    dve.drain()
                    v.tensor_tensor(dst[:, bass.ds(2 * i + u, 1), :].rearrange("p a t -> p (a t)"),
                                    sig[:, u, 0, :], sig[:, u, 1, :], ALU.add).then_inc(summed.handle, 1)
            dve.drain()

        ready.close(4 * DC)
        gated.close(2 * DC)
        free.close(DC + 1)
        summed.close(DC + 1)


def stage_out_project(nc, K, w, kt, per_slot, src, gain):
    with ExitStack() as ctx:
        def sb(name, shape):
            return ctx.enter_context(nc.sbuf_tensor(K.name(name), shape, F32))

        sq, total, rstd = sb("sq", [P, 2, T]), sb("total", [P, T]), sb("rstd", [P, T])
        block = ctx.enter_context(nc.Block())
        ring, yT = K.ring, K.hT
        ready, read, squared, summed = K.s("chunk_ready"), K.s("chunk_read"), K.s("squared"), K.s("summed")
        totaled, stat_ready, rooted, scaled = K.s("totaled"), K.s("stat_ready"), K.s("rooted"), K.s("y_scaled")
        slots = DC // per_slot
        rounds, body = slots // 2, 2 * per_slot
        banks = min(4, body)
        stat = K.ps[:, 7, :]

        @block.sync
        def _(sp):
            with sp.Fori(0, rounds) as i:
                for u in range(2):
                    cols = w[:, bass.ds((2 * i + u) * per_slot * P, per_slot * P)].rearrange("(k p) n -> p k n", p=P)
                    ring.load(sp, [(lambda n: ring.slot(n, kt, per_slot * P), cols)], it=i, pairs=1)
            ring.skip(rounds - 1, 2, 1)

        @block.tensor
        def _(pe):
            with pe.Fori(0, rounds) as i:
                for u in range(2):
                    n = ring.use(pe, it=i, step=16)
                    wt = ring.slot(n, kt, per_slot * P)
                    for j in range(per_slot):
                        q = u * per_slot + j
                        pe.wait_ge(read.handle, read.at(q) + body * i)
                        product(nc, K.ps[:, q % banks, :], lambda k: wt[:, k, j * P:(j + 1) * P], src, kt)\
                            .then_inc(ready.handle, 1)
                    pe.drain().then_inc(ring.free[n % 2], 1)
            ring.uses += 2 * (rounds - 1)
            pe.wait_ge(totaled.handle, totaled.at(DC))
            nc.tensor.matmul(stat, K.ones[:], total[:], start=True, stop=True).then_inc(stat_ready.handle, 1)

        @block.scalar
        def _(act):
            for _ in range(banks - 1):
                act.drain().then_inc(read.handle, 1)
            with act.Fori(0, rounds) as i:
                for q in range(body):
                    act.wait_ge(ready.handle, ready.at(q + 1) + body * i)
                    bank = K.ps[:, q % banks, :]
                    nc.scalar.activation(yT[:, bass.ds(body * i + q, 1), :].rearrange("p a t -> p (a t)"), bank, ACT.Copy)
                    act.wait_ge(summed.handle, summed.at(q) + body * i)
                    nc.scalar.activation(sq[:, q % 2, :], bank, ACT.Square).then_inc(squared.handle, 1)
                    act.drain().then_inc(read.handle, 1)
            act.wait_ge(stat_ready.handle, stat_ready.at(1))
            nc.scalar.activation(rstd[:], stat, ACT.Sqrt, bias=K.eps[:], scale=1.0 / D).then_inc(rooted.handle, 1)

        @block.gpsimd
        def _(pool):
            nc.gpsimd.memset(total[:], 0.0)
            pool.drain().then_inc(summed.handle, 1)
            with pool.Fori(0, rounds) as i:
                for q in range(body):
                    pool.wait_ge(squared.handle, squared.at(q + 1) + body * i)
                    nc.gpsimd.tensor_tensor(total[:], total[:], sq[:, q % 2, :], ALU.add).then_inc(summed.handle, 1)
                    pool.drain().then_inc(totaled.handle, 1)
            for c in range(DC):
                pool.wait_ge(scaled.handle, scaled.at(c + 1))
                nc.gpsimd.tensor_tensor(K.xT[:, c, :], K.xT[:, c, :], yT[:, c, :], ALU.add)
            pool.drain()

        @block.vector
        def _(dve):
            dve.wait_ge(rooted.handle, rooted.at(1))
            nc.vector.reciprocal(rstd[:], rstd[:])
            dve.drain()
            for c in range(DC):
                nc.vector.scalar_tensor_tensor(out=yT[:, c, :], in0=yT[:, c, :], scalar=gain(c), in1=rstd[:],
                                               op0=ALU.mult, op1=ALU.mult).then_inc(scaled.handle, 1)

        ready.close(DC)
        read.close(DC + banks - 1)
        squared.close(DC)
        summed.close(DC + 1)
        totaled.close(DC)
        stat_ready.close(1)
        rooted.close(1)
        scaled.close(DC)


def stage_ffn_up(nc, K, dr, dst):
    with ExitStack() as ctx:
        def sb(name, shape):
            return ctx.enter_context(nc.sbuf_tensor(K.name(name), shape, F32))

        taps = sb("taps", [P, 2, 4, 2])
        u_sb = sb("u_sb", [P, 2, 2, T])
        block = ctx.enter_context(nc.Block())
        ring, w = K.ring, dr["w_up"][0]
        ready, free, tapped = K.s("chunk_ready"), K.s("banks_read"), K.s("taps_ready")
        biased, conved, gelued, done = K.s("biased"), K.s("conved"), K.s("gelued"), K.s("ffn_done")

        @block.sync
        def _(sp):
            with sp.Fori(0, FC // 2) as i:
                for u in range(2):
                    def at(half):
                        return lambda n: ring.slot(n, DC, 2, P)[:, :, half, :]
                    ring.load(sp, [(at(half), w[:, bass.ds(half * FF + (2 * i + u) * P, P)]
                                    .rearrange("(k p) n -> p k n", p=P)) for half in range(2)], it=i, pairs=1)
            ring.skip(FC // 2 - 1, 2, 2)

        @block.tensor
        def _(pe):
            with pe.Fori(0, FC // 2) as i:
                for u in range(2):
                    n = ring.use(pe, it=i, step=32)
                    wt = ring.slot(n, DC, 2, P)
                    pe.wait_ge(free.handle, free.at(u) + 2 * i)
                    for half in range(2):
                        product(nc, K.ps[:, 2 * u + half, :], lambda k: wt[:, k, half, :], lambda k: K.hT[:, k, :], DC)\
                            .then_inc(ready.handle, 1)
                    pe.drain().then_inc(ring.free[n % 2], 1)
            ring.uses += FC - 2

        @block.gpsimd
        def _(pool):
            conv = K.conv[:].rearrange("p j (h c) -> p j h c", h=2)
            with pool.Fori(0, FC // 2) as i:
                for u in range(2):
                    pool.wait_ge(done.handle, done.at(u) + 2 * i)
                    nc.gpsimd.tensor_copy(taps[:, u, :, :].unsqueeze(3), conv[:, :, :, bass.ds(2 * i + u, 1)])\
                        .then_inc(tapped.handle, 1)

        @block.scalar
        def _(act):
            with act.Fori(0, FC // 2) as i:
                for u in range(2):
                    act.wait_ge(tapped.handle, tapped.at(u + 1) + 2 * i)
                    act.wait_ge(done.handle, done.at(u) + 2 * i)
                    for half in range(2):
                        act.wait_ge(ready.handle, ready.at(2 * u + half + 1) + 4 * i)
                        nc.scalar.activation(u_sb[:, u, half, :], K.ps[:, 2 * u + half, :], ACT.Identity,
                                             bias=taps[:, u, 3, half:half + 1], scale=taps[:, u, 2, half:half + 1])\
                            .then_inc(biased.handle, 1)
                    act.wait_ge(conved.handle, conved.at(u + 1) + 2 * i)
                    nc.scalar.activation(u_sb[:, u, 0, :], u_sb[:, u, 0, :], ACT.Gelu_apprx_tanh)\
                        .then_inc(gelued.handle, 1)

        @block.vector
        def _(dve):
            v = nc.vector
            dve.drain().then_inc(free.handle, 1)
            dve.drain().then_inc(done.handle, 1)
            with dve.Fori(0, FC // 2) as i:
                for u in range(2):
                    for half in range(2):
                        dve.wait_ge(biased.handle, biased.at(2 * u + half + 1) + 4 * i)
                        for back in (1, 2):
                            out = u_sb[:, u, half, back:T]
                            last = v.scalar_tensor_tensor(out=out, in0=K.ps[:, 2 * u + half, 0:T - back],
                                                          scalar=taps[:, u, 2 - back, half:half + 1], in1=out,
                                                          op0=ALU.mult, op1=ALU.add)
                            if back == 1:
                                dve.drain()
                            elif half == 0:
                                last.then_inc(conved.handle, 1)
                            else:
                                last.then_inc(free.handle, 1)
                    dve.drain()
                    dve.wait_ge(gelued.handle, gelued.at(u + 1) + 2 * i)
                    v.tensor_tensor(dst[:, bass.ds(2 * i + u, 1), :].rearrange("p a t -> p (a t)"), u_sb[:, u, 0, :],
                                    u_sb[:, u, 1, :], ALU.mult).then_inc(done.handle, 1)
            dve.drain()

        ready.close(2 * FC)
        free.close(FC + 1)
        tapped.close(FC)
        biased.close(2 * FC)
        conved.close(FC)
        gelued.close(FC)
        done.close(FC + 1)


def stage_bias(nc, K, dr):
    with ExitStack() as ctx:
        def sb(name, shape):
            return ctx.enter_context(nc.sbuf_tensor(name, shape, F32))

        NH = NSA_H + SWA_H
        rel = sb("rel", [34, NH])
        hot = sb("hot", [34, 2, 2 * T])
        vecs = sb("bias_vecs", [NH, 2, 2 * T])
        cmp_t = sb("cmp_t", [CMP, NSA_H, T])
        flip = sb("flip", [P, P])
        s_in, s_rel, s_vec, s_cp = (ctx.enter_context(nc.semaphore(x)) for x in
                                    ("bias_in", "rel_scaled", "bias_by_distance", "bias_copied"))
        s_flip = ctx.enter_context(nc.semaphore("flip_ready"))
        s_out, s_back, s_turn = (ctx.enter_context(nc.semaphore(x)) for x in
                                 ("bias_in_dram", "bias_tiles_loaded", "cmp_bias_turned"))
        block = ctx.enter_context(nc.Block())
        scratch = dr["scratch"]

        @block.sync
        def _(sp):
            sp.dma_start(rel[0:32, :], dr["rel_bias_2"].rearrange("h b -> b h"), allow_slow_non_contiguous=True).then_inc(s_in, 16)
            sp.dma_start(rel[32:34, :], dr["c_mask_rows"]).then_inc(s_in, 16)
            sp.dma_start(hot[:, 0, :], dr["c_hot"]).then_inc(s_in, 16)
            sp.dma_start(hot[:, 1, :], dr["c_back_hot"]).then_inc(s_in, 16)
            sp.dma_start(K.sinks[:, 0, :, :], dr["swa_sinks_2"].partition_broadcast(P)).then_inc(s_in, 16)
            sp.dma_start(K.rope_m[64:128, :], dr["c_rope_m"]).then_inc(s_in, 16)
            sp.wait_ge(s_cp, 4)
            sp.dma_start(scratch.rearrange("a h m -> h a m"), vecs[:]).then_inc(s_out, 16)
            sp.wait_ge(s_out, 16)
            row, back = 2 * T, NH * 2 * T
            sp.dma_start(K.bias_nsa[:], bass.AP(tensor=scratch.tensor, offset=back,
                                                ap=[[1, P], [row, NSA_H], [1, T]])).then_inc(s_back, 16)
            sp.dma_start(K.bias_swa[:], bass.AP(tensor=scratch.tensor, offset=back + NSA_H * row + T - 2 * P,
                                                ap=[[1, P], [row, SWA_H], [1, 2 * P]])).then_inc(s_back, 16)
            sp.dma_start(cmp_t[:], bass.AP(tensor=scratch.tensor, offset=T - 31 - 16 * (CMP - 1),
                                           ap=[[16, CMP], [row, NSA_H], [1, T]])).then_inc(s_back, 16)

        @block.gpsimd
        def _(pool):
            nc.gpsimd.memset(flip[:], 0.0)
            pool.drain()
            nc.gpsimd.affine_select(out=flip[:], in_=flip[:], compare_op=ALU.not_equal, fill=1.0, base=1 - P,
                                    pattern=[[1, P]], channel_multiplier=1).then_inc(s_flip, 1)

        @block.tensor
        def _(pe):
            pe.wait_ge(s_in, 16 * 6)
            pe.wait_ge(s_rel, 1)
            for a in range(4):
                nc.tensor.matmul(K.ps[0:NH, a, :], rel[:], hot[:, a // 2, (a % 2) * T:(a % 2 + 1) * T],
                                 start=True, stop=True).then_inc(s_vec, 1)
            pe.wait_ge(s_back, 48)
            pe.wait_ge(s_flip, 1)
            for h in range(NSA_H):
                nc.tensor.matmul(K.ps[:, h, :], flip[:], K.bias_nsa[:, h, :], start=True, stop=True)\
                    .then_inc(s_turn, 1)
            for b in range(4):
                nc.tensor.matmul(K.ps[:, 4 + b, :], flip[:], K.bias_swa[:, 2 * b:2 * b + 2, :], start=True, stop=True)\
                    .then_inc(s_turn, 1)
            pe.wait_ge(s_cp, 5)
            for h in range(NSA_H):
                for i in range(TT):
                    o = (h * TT + i) * 32
                    last = nc.tensor.matmul(K.ps[:, 0, o:o + CMP], cmp_t[:, h, i * P:(i + 1) * P],
                                            flip[0:CMP, P - CMP:P], start=True, stop=True)
            last.then_inc(s_turn, 1)

        @block.vector
        def _(dve):
            v = nc.vector
            dve.wait_ge(s_in, 16 * 6)
            v.tensor_scalar(rel[0:32, :], rel[0:32, :], 8.0, None, ALU.mult).then_inc(s_rel, 1)
            v.tensor_scalar(K.sinks[:, 1, :, :], K.sinks[:, 0, :, :], 8.0, None, ALU.mult)
            for a in range(4):
                dve.wait_ge(s_vec, a + 1)
                v.tensor_copy(vecs[:, a // 2, (a % 2) * T:(a % 2 + 1) * T], K.ps[0:NH, a, :]).then_inc(s_cp, 1)
            for h in range(NSA_H):
                dve.wait_ge(s_turn, h + 1)
                v.tensor_copy(K.bias_nsa[:, h, :], K.ps[:, h, :]).then_inc(s_cp, 1)
            for b in range(4):
                dve.wait_ge(s_turn, NSA_H + b + 1)
                v.tensor_copy(K.bias_swa[:, 2 * b:2 * b + 2, :].rearrange("p h j -> p (h j)"), K.ps[:, 4 + b, :])
            dve.wait_ge(s_turn, NSA_H + 5)
            v.tensor_copy(K.bias_cmp[:, :, :, 0:CMP],
                          K.ps[:, 0, :].rearrange("p (h i c) -> p h i c", h=NSA_H, c=32)[:, :, :, 0:CMP])
            dve.drain()


def stage_layer_project(nc, K, dr, l, L):
    with ExitStack() as ctx:
        rot = ctx.enter_context(nc.sbuf_tensor(K.name("rotk"), [P, T], F32))
        kr = ctx.enter_context(nc.sbuf_tensor(K.name("kr"), [P, T], F32))
        block = ctx.enter_context(nc.Block())
        ring, w = K.ring, dr["w_in_2"][l]
        ready, free = K.s("chunk_ready"), [K.s(f"bank_free{b}") for b in range(4)]
        slots = [[(0, 0, 512)], [(0, 512, 396)],
                 [(0, 908, 128), (128, 1580, 64), (192, 1036, 32), (224, 1052, 16), (240, 1036, 16), (256, 1644, 64)],
                 [(0, 1068, 512)], [(0, 1708, 512)], [(0, 2220, 512)]]
        chunks = [(0, 0, P, "q0"), (0, 128, P, "q1"), (0, 256, P, "kv_cmp"), (0, 384, P, "kv_slc"),
                  (1, 0, P, "kv_win"), (1, 128, 12, "gates"), (1, 140, P, "cq0"), (1, 268, P, "cq1"),
                  (2, 0, P, "ckv"), (2, 128, P, "k_swa_rope"), (2, 256, 64, "v_swa")]
        chunks += [(3, j * P, P, f"qs{j}") for j in range(4)] + [(4 + j // 4, j % 4 * P, P, f"z{j}") for j in range(8)]
        by_act = ("gates", "z")
        N = len(chunks)

        @block.sync
        def _(sp):
            for parts in slots:
                ring.load(sp, [(lambda n, o=o, m=m: ring.slot(n, DC, T)[:, :, o:o + m], columns(w, 0, DC, c, m))
                               for o, c, m in parts])

        @block.tensor
        def _(pe):
            at = -1
            for c, (s, o, m, what) in enumerate(chunks):
                if s != at:
                    if at >= 0:
                        pe.drain().then_inc(ring.free[n % 2], 1)
                    at, n = s, ring.use(pe)
                    wt = ring.slot(n, DC, T)
                if c >= 4:
                    pe.wait_ge(free[c % 4].handle, free[c % 4].at(c // 4))
                bank = K.ps[:, c % 4, :]
                if what == "gates":
                    for t in range(TT):
                        last = product(nc, bank[:, 12 * t:12 * t + 12], lambda k: K.hT[:, k, t * P:(t + 1) * P],
                                       lambda k: wt[:, k, o:o + m], DC)
                else:
                    last = product(nc, bank[0:m, :], lambda k: wt[:, k, o:o + m], lambda k: K.hT[:, k, :], DC)
                last.then_inc(ready.handle, 1)
            pe.drain().then_inc(ring.free[n % 2], 1)

        @block.vector
        def _(dve):
            v = nc.vector
            copies = {"q0": L.qn[:, 0, :], "q1": L.qn[:, 1, :], "cq0": L.cq[:, 0, :], "cq1": L.cq[:, 1, :],
                      "ckv": L.cq[:, 2, :]} | {f"qs{j}": L.qs[:, j, :] for j in range(4)}
            for c, (_, _, m, what) in enumerate(chunks):
                if what.startswith(by_act):
                    continue
                dve.wait_ge(ready.handle, ready.at(c + 1))
                bank = K.ps[:, c % 4, :]
                if what in copies:
                    last = v.tensor_copy(copies[what], bank)
                elif what == "kv_cmp":
                    for i in range(2):
                        rows = slice(64 * i, 64 * i + 64)
                        for e in range(2):
                            for m0 in range(2):
                                src = bank[rows, :].rearrange("p (c s) -> p s c", s=16)[:, e:16:2, m0:m0 + CMP]
                                pe0 = (2 * l + i) * 32 + 16 * m0 + e
                                pos = K.peT[rows, pe0:pe0 + 15:2].unsqueeze(2).to_broadcast([64, 8, CMP])
                                last = v.tensor_tensor(L.blk[64 * e:64 * e + 64, i, 8 * m0:8 * m0 + 8, 0:CMP], src, pos,
                                                       ALU.add)
                elif what in ("kv_slc", "kv_win"):
                    k, vt = (L.k_slc, L.v_t[:, 0, :]) if what == "kv_slc" else (L.k_win, L.v_t[:, 1, :])
                    v.tensor_copy(k[0:64, :], bank[0:64, :])
                    v.tensor_copy(k[64:128, :], bank[0:64, :])
                    last = v.tensor_copy(vt[64:128, :], bank[64:128, :])
                elif what == "k_swa_rope":
                    v.tensor_copy(L.k_swa[0:64, :], bank[0:64, :])
                    v.tensor_copy(L.k_swa[64:128, :], bank[0:64, :])
                    v.tensor_tensor(rot[64:96, :], bank[96:128, :], K.rope_m[96:128, :], ALU.mult)
                    v.tensor_tensor(kr[64:96, :], bank[64:96, :], K.rope_m[64:96, :], ALU.mult)
                    dve.drain()
                    for h in range(MLA_H):
                        last = v.tensor_tensor(L.kf[64:96, h, :], kr[64:96, :], rot[64:96, :], ALU.add)
                elif what == "v_swa":
                    last = v.tensor_copy(L.v_t[0:64, 0, :], bank[0:64, :])
                last.then_inc(free[c % 4].handle, 1)
            dve.drain()

        @block.scalar
        def _(act):
            for c, (_, _, _, what) in enumerate(chunks):
                if not what.startswith(by_act):
                    continue
                act.wait_ge(ready.handle, ready.at(c + 1))
                bank = K.ps[:, c % 4, :]
                if what == "gates":
                    last = nc.scalar.activation(L.gates[:], bank[:, 0:12 * TT], ACT.Sigmoid)
                else:
                    last = nc.scalar.activation(L.sz[:, int(what[1:]), :], bank, ACT.Silu)
                last.then_inc(free[c % 4].handle, 1)

        ready.close(N)
        for b in range(4):
            free[b].close(len(range(b, N, 4)))


def stage_latents(nc, K, dr, l, L):
    with ExitStack() as ctx:
        def sb(name, shape):
            return ctx.enter_context(nc.sbuf_tensor(K.name(name), shape, F32))

        sq, rstd = sb("lsq", [P, 3, T]), sb("lrstd", [P, 2, T])
        hid = sb("hid", [P, 2, 32])
        rot, qr = sb("rotq", [P, T]), sb("qr", [P, T])
        block = ctx.enter_context(nc.Block())
        ring = K.ring
        ready, free = K.s("chunk_ready"), [K.s(f"bank_free{b}") for b in range(4)]
        squared, rooted, normed, hidden = K.s("squared"), K.s("rooted"), K.s("latents_normed"), K.s("hidden")
        w1, w2 = dr["cmp_w1_2"][l], dr["cmp_w2_2"][l]
        uq, ukv = dr["mla_w_uq_2"][l], dr["mla_w_ukv_2"][l]
        products = ["ss_q", "ss_kv", "hid0", "hid1", "v_slc", "v_win", "v_swa", "kc", "vc"]
        products += [f"uq{h}" for h in range(4)] + [f"uk{h}" for h in range(4)] + ["uv0", "uv1"]
        N = len(products)

        def slot_u(n):
            s = ring.tensor[:, n % 2, :]
            return (s[:, 0:1024].rearrange("p (k h c) -> p k h c", k=2, h=4), s[:, 1024:1536],
                    s[:, 1536:1664].rearrange("p (i d) -> p i d", i=2))

        @block.sync
        def _(sp):
            ring.load(sp, [(lambda n, i=i: ring.slot(n, 2, 16, P)[:, i, :, :],
                            w1[i].rearrange("(m p) n -> p m n", p=P)) for i in range(2)])
            uq4 = uq.rearrange("(k p) (h c) -> p k h c", p=P, h=4)
            parts = []
            for k in range(2):
                parts += [(lambda n, k=k: slot_u(n)[0][:, k, :, 0:96], uq4[:, k]),
                          (lambda n, k=k: slot_u(n)[0][:, k, :, 96:112], uq4[:, k, :, 80:96]),
                          (lambda n, k=k: slot_u(n)[0][:, k, :, 112:128], uq4[:, k, :, 64:80])]
            parts += [(lambda n: slot_u(n)[1], ukv), (lambda n: slot_u(n)[2], w2.rearrange("i p d -> p i d"))]
            ring.load(sp, parts)

        @block.tensor
        def _(pe):
            t = nc.tensor
            for c, what in enumerate(products):
                if c >= 4:
                    pe.wait_ge(free[c % 4].handle, free[c % 4].at(c // 4))
                bank = K.ps[:, c % 4, :]
                if what == "ss_q":
                    pe.wait_ge(squared.handle, squared.at(2))
                    last = product(nc, bank, lambda k: K.ones[:], lambda k: sq[:, k, :], 2)
                elif what == "ss_kv":
                    pe.wait_ge(squared.handle, squared.at(3))
                    last = product(nc, bank, lambda k: K.ones[:], lambda k: sq[:, 2, :], 1)
                elif what.startswith("hid"):
                    i = int(what[3:])
                    if i == 0:
                        n = ring.use(pe)
                        w = ring.slot(n, 2, 16, P)
                    last = product(nc, bank[:, 0:CMP], lambda m: w[:, i, m, :], lambda m: L.blk[:, i, m, 0:CMP], 16)
                elif what in ("v_slc", "v_win", "v_swa"):
                    i = ("v_slc", "v_win", "v_swa").index(what)
                    rows, half = (slice(64, 128), i) if i < 2 else (slice(0, 64), 0)
                    for b in range(TT):
                        last = t.matmul(bank[:, 64 * b:64 * b + 64], L.v_t[rows, half, b * P:(b + 1) * P],
                                        K.ident[rows, rows], start=True, stop=True)
                elif what == "kc":
                    pe.drain().then_inc(ring.free[n % 2], 1)
                    n = ring.use(pe)
                    wq, wkv, wc = slot_u(n)
                    pe.wait_ge(hidden.handle, hidden.at(2))
                    for half in range(2):
                        last = t.matmul(bank[64 * half:64 * half + 64, 0:CMP], wc[:, 0, :], hid[:, 0, 0:CMP],
                                        start=True, stop=True)
                elif what == "vc":
                    last = t.matmul(bank[0:CMP, 0:64], hid[:, 1, 0:CMP], wc[:, 1, :], start=True, stop=True)
                elif what.startswith("uq"):
                    pe.wait_ge(normed.handle, normed.at(2))
                    last = product(nc, bank, lambda k: wq[:, k, int(what[2:]), :], lambda k: L.cq[:, k, :], 2)
                elif what.startswith("uk"):
                    h = int(what[2:])
                    pe.wait_ge(normed.handle, normed.at(3))
                    last = product(nc, bank[0:64, :], lambda k: wkv[:, h * P:h * P + 64], lambda k: L.cq[:, 2, :], 1)
                else:
                    values = wkv.rearrange("p (h c) -> p h c", h=4)[:, :, 64:128]
                    for b in range(2):
                        tile = 2 * int(what[2:]) + b
                        last = t.matmul(bank[:, 256 * b:256 * b + 256], L.cq[:, 2, tile * P:(tile + 1) * P], values,
                                        start=True, stop=True)
                last.then_inc(ready.handle, 1)
            pe.drain().then_inc(ring.free[n % 2], 1)

        @block.scalar
        def _(act):
            for i in range(3):
                nc.scalar.activation(sq[:, i, :], L.cq[:, i, :], ACT.Square).then_inc(squared.handle, 1)
            for c, what in enumerate(products):
                bank = K.ps[:, c % 4, :]
                if what.startswith("ss"):
                    act.wait_ge(ready.handle, ready.at(c + 1))
                    nc.scalar.activation(rstd[:, c, :], bank, ACT.Sqrt, bias=K.eps[:], scale=(1.0 / 256, 1.0 / 128)[c])\
                        .then_inc(rooted.handle, 1)
                    act.drain().then_inc(free[c % 4].handle, 1)
                elif what.startswith("hid"):
                    act.wait_ge(ready.handle, ready.at(c + 1))
                    nc.scalar.activation(hid[:, c - 2, 0:CMP], bank[:, 0:CMP], ACT.Silu).then_inc(hidden.handle, 1)
                    act.drain().then_inc(free[c % 4].handle, 1)

        @block.vector
        def _(dve):
            v = nc.vector
            v.tensor_scalar(L.gates[:, 0:12:3], L.gates[:, 0:12:3], K.cols[:, 4:5], None, ALU.mult)
            dve.wait_ge(rooted.handle, rooted.at(2))
            v.reciprocal(rstd[:], rstd[:])
            dve.drain()
            for i in range(3):
                col = 64 + 2 * l + i if i < 2 else 68 + l
                v.scalar_tensor_tensor(out=L.cq[:, i, :], in0=L.cq[:, i, :], scalar=K.vec[:, col:col + 1],
                                       in1=rstd[:, i // 2, :], op0=ALU.mult, op1=ALU.mult).then_inc(normed.handle, 1)
            for c, what in enumerate(products):
                if c < 4:
                    continue
                dve.wait_ge(ready.handle, ready.at(c + 1))
                bank = K.ps[:, c % 4, :]
                if what in ("v_slc", "v_win", "v_swa"):
                    dst = (L.v_slc, L.v_win, L.v_swa)[c - 4]
                    last = v.tensor_copy(dst[:].rearrange("p b d -> p (b d)"), bank[:, 0:256])
                elif what == "kc":
                    last = v.tensor_copy(L.kc[:, 0:CMP], bank[:, 0:CMP])
                elif what == "vc":
                    last = v.tensor_copy(L.vc[0:CMP, :], bank[0:CMP, 0:64])
                elif what.startswith("uq"):
                    h = int(what[2:])
                    v.tensor_tensor(rot[64:96, :], bank[96:128, :], K.rope_m[96:128, :], ALU.mult)
                    v.tensor_tensor(qr[64:96, :], bank[64:96, :], K.rope_m[64:96, :], ALU.mult)
                    last = v.tensor_copy(L.qf[0:64, h, :], bank[0:64, :])
                elif what.startswith("uk"):
                    last = v.tensor_copy(L.kf[0:64, int(what[2:]), :], bank[0:64, :])
                else:
                    b = 2 * int(what[2:])
                    last = v.tensor_copy(L.v_mla[:, b:b + 2, :].rearrange("p b d -> p (b d)"), bank)
                last.then_inc(free[c % 4].handle, 1)
                if what.startswith("uq"):
                    dve.drain()
                    v.tensor_tensor(L.qf[64:96, h, :], qr[64:96, :], rot[64:96, :], ALU.add)
                    dve.drain()
            dve.drain()

        ready.close(N)
        squared.close(3)
        rooted.close(2)
        normed.close(3)
        hidden.close(2)
        for b in range(4):
            free[b].close(len(range(b, N, 4)))


def stage_store(nc, K, out):
    with ExitStack() as ctx:
        o_tok = ctx.enter_context(nc.sbuf_tensor("o_tok", [P, TT, D], F32))
        s_tr, s_cp, s_out = (ctx.enter_context(nc.semaphore(x)) for x in ("out_turned", "out_copied", "out_stored"))
        block = ctx.enter_context(nc.Block())

        @block.tensor
        def _(pe):
            for n in range(2 * TT):
                if n >= 4:
                    pe.wait_ge(s_cp, n - 3)
                for c in range(4):
                    last = nc.tensor.transpose(K.ps[:, n % 4, c * P:(c + 1) * P],
                                               K.xT[:, 4 * (n % 2) + c, (n // 2) * P:(n // 2 + 1) * P], K.ident[:])
                last.then_inc(s_tr, 1)

        @block.vector
        def _(dve):
            for n in range(2 * TT):
                dve.wait_ge(s_tr, n + 1)
                nc.vector.tensor_copy(o_tok[:, n // 2, (n % 2) * T:(n % 2 + 1) * T], K.ps[:, n % 4, :]).then_inc(s_cp, 1)

        @block.sync
        def _(sp):
            for t in range(TT):
                sp.wait_ge(s_cp, 2 * t + 2)
                sp.dma_start(out[0, t * P:(t + 1) * P, :], o_tok[:, t, :]).then_inc(s_out, 16)
            sp.wait_ge(s_out, 16 * TT)



def diff_jobs(K, qk, v_tok, oT):
    for h in range(HEADS):
        for t in range(TT):
            w = P * (t + 1)
            for c in range(2):
                rows = slice(64 * c, 64 * c + 64)
                yield job([(0, qk[rows, h, t * P:(t + 1) * P], qk[rows, HEADS + h, 0:w])], w,
                          K.causal[:, T - w:T], A_DIM ** -0.5,
                          [(b * P, P, v_tok[:, b, h * P:(h + 1) * P]) for b in range(t + 1)],
                          oT[:, h, t * P:(t + 1) * P], first=c == 0, last=c == 1,
                          gate=K.neg_lam[:] if c else None)


def dilated_jobs(mask, qk, v_tok, oT):
    for h in range(HEADS):
        for r in range(CLASSES):
            own = slice(r * P, (r + 1) * P)
            q = [qk[:, 4 * g + h, own] for g in range(3)]
            k = [qk[:, 12 + 4 * g + h, :] for g in range(3)]
            head = slice(h * P, (h + 1) * P)
            yield job([(0, q[0], k[0]), (T, q[1], k[1][:, own]), (T + P, q[2], k[2][:, own])], T + 2 * P,
                      mask[:, r, :], P ** -0.5,
                      [(b * P, P, v_tok[:, 0, b, head]) for b in range(CLASSES)]
                      + [((3 + g) * P, P, v_tok[:, g, r, head]) for g in (1, 2)],
                      oT[:, h, r:T:CLASSES])


def layer_jobs(K, L, l):
    for h in range(NSA_H):
        rows = slice(64 * (h % 2), 64 * (h % 2) + 64)
        for t in range(TT):
            w, own = P * (t + 1), slice(t * P, (t + 1) * P)
            q = L.qn[rows, h // 2, own]
            common = dict(out=L.mix[rows, h // 2, own], rows=(rows.start, 64), times=L.sz[rows, h // 2, own])
            gates = [L.gates[:, 12 * t + 3 * h + b:12 * t + 3 * h + b + 1] for b in range(3)]
            yield job([(0, q, L.kc[rows, 0:CMP])], CMP, K.bias_cmp[:, h, t, 0:CMP], HD ** -0.5,
                      [(0, CMP, L.vc[0:CMP, :])], first=True, last=False, gate=gates[0], turned=(CMP, P), **common)
            for b, (k, v) in enumerate([(L.k_slc, L.v_slc), (L.k_win, L.v_win)]):
                yield job([(0, q, k[rows, 0:w])], w, K.bias_nsa[:, h, T - w:T], HD ** -0.5,
                          [(i * P, P, v[:, i, :]) for i in range(t + 1)], first=False, last=b == 1,
                          gate=gates[1 + b], **common)
    for h in range(MLA_H):
        rows = slice(64 * (h % 2), 64 * (h % 2) + 64)
        for t in range(TT):
            w, own = P * (t + 1), slice(t * P, (t + 1) * P)
            yield job([(0, L.qf[0:96, h, own], L.kf[0:96, h, 0:w])], w, K.causal[:, T - w:T], 96 ** -0.5,
                      [(i * P, P, L.v_mla[:, i, 64 * h:64 * h + 64]) for i in range(t + 1)],
                      L.mix[rows, 2 + h // 2, own], rows=(rows.start, 64), times=L.sz[rows, 2 + h // 2, own])
    for h in range(SWA_H):
        rows = slice(64 * (h % 2), 64 * (h % 2) + 64)
        for t in range(TT):
            w = min(2, t + 1) * P
            lo, own = (t + 1) * P - w, slice(t * P, (t + 1) * P)
            yield job([(0, L.qs[rows, h // 2, own], L.k_swa[rows, lo:lo + w])], w, K.bias_swa[:, h, 2 * P - w:2 * P],
                      HD ** -0.5, [(i * P, P, L.v_swa[:, lo // P + i, :]) for i in range(w // P)],
                      L.mix[rows, 4 + h // 2, own], rows=(rows.start, 64), times=L.sz[rows, 4 + h // 2, own],
                      sink=(K.sinks[:, 1, l, h:h + 1], K.sinks[:, 0, l, h:h + 1]))


def build(nc, dr, out, stop=None, probes=None):
    with ExitStack() as ctx:
        K = Kit()

        def sb(name, shape, dt=F32, scope=ctx):
            return scope.enter_context(nc.sbuf_tensor(name, shape, dt))

        names, counted = {}, {}

        def name(n):
            names[n] = names.get(n, 0) + 1
            return f"{n}_{names[n]}"

        def s(n):
            if n not in counted:
                counted[n] = Counted(ctx.enter_context(nc.semaphore(n)))
            return counted[n]

        K.name, K.s = name, s
        K.ps = ctx.enter_context(nc.psum_tensor("ps", [P, 8, T], F32))
        K.ring = Ring(sb("ring", [P, 2, DC * T]), [ctx.enter_context(nc.semaphore(f"slot{i}_loaded")) for i in range(2)],
                      [ctx.enter_context(nc.semaphore(f"slot{i}_free")) for i in range(2)])
        K.xT, K.hT = sb("xT", [P, DC, T]), sb("hT", [P, DC, T])
        K.ident, K.ones, K.eps = sb("ident", [P, P]), sb("ones", [P, P]), sb("eps", [P, 1])
        K.cols, K.causal = sb("cols", [P, 8]), sb("causal", [P, T])
        K.vec, K.conv, K.peT = sb("vec", [P, NVEC]), sb("conv", [P, 4, 2 * FC]), sb("peT", [P, P])
        K.neg_lam = sb("neg_lam", [P, 1])

        def norm(first, n=DC):
            stage_norm(nc, K, lambda c: K.xT[:, c, :], DC, lambda c: K.vec[:, first + c:first + c + 1],
                       lambda c: K.hT[:, c, :], D)

        def probe(what, tensor):
            if probes is not None and what in probes:
                with ExitStack() as e:
                    sm = e.enter_context(nc.semaphore(name("probe")))
                    blk = e.enter_context(nc.Block())

                    @blk.sync
                    def _(sp):
                        sp.dma_start(probes[what], tensor).then_inc(sm, 16)
                        sp.wait_ge(sm, 16)

        with ExitStack() as first:
            oa, ob = sb("oa", [P, HEADS, T], scope=first), sb("ob", [P, HEADS, T], scope=first)
            with ExitStack() as tables:
                K.sin_a, K.cos_a, K.sin_b, K.cos_b = (sb(x, [P, T], scope=tables) for x in
                                                      ("sin_a", "cos_a", "sin_b", "cos_b"))
                stage_setup(nc, K, dr)
                norm(VECS["pre_mix_g"][0])
                probe("h", K.hT[:])
                with ExitStack() as e:
                    qk, v = sb("qk_a", [P, 2 * HEADS, T], scope=e), sb("v_a", [P, TT, T], scope=e)
                    stage_project_a(nc, K, dr, qk, v)
                    probe("qk_a", qk[:])
                    stage_attention(nc, K, list(diff_jobs(K, qk, v, oa)), T, 3, 3)
                stage_head_norm(nc, K, oa, K.vec[:, 70:71])
                probe("oa", oa[:])
                with ExitStack() as e:
                    qk, v = sb("qk_b", [P, 24, T], scope=e), sb("v_b", [P, 3, CLASSES, T], scope=e)
                    with ExitStack() as e2:
                        K.rope_tmp = sb("rope_tmp", [P, 2, T], scope=e2)
                        stage_project_b(nc, K, dr, qk, v)
                    mask = sb("mask_b", [P, CLASSES, 6 * P], scope=e)
                    s_mask = e.enter_context(nc.semaphore("mask_loaded"))
                    with nc.Block() as block:
                        @block.sync
                        def _(sp):
                            sp.dma_start(mask[:], dr["c_mask_b"]).then_inc(s_mask, 16)
                            sp.wait_ge(s_mask, 16)
                    stage_attention(nc, K, list(dilated_jobs(mask, qk, v, ob)), 6 * P, 2, 1)
                probe("ob", ob[:])
            with ExitStack() as e:
                mixed = sb("mixed", [P, DC, T], scope=e)
                stage_gate_mix(nc, K, dr, oa, ob, mixed)
                probe("mixed", mixed[:])
                stage_out_project(nc, K, dr["w_mix_out"][0], DC, 4, lambda k: mixed[:, k, :],
                                  lambda c: K.vec[:, 8 + c:9 + c])
                probe("x1", K.xT[:])
            norm(VECS["pre_ffn_g"][0])
            with ExitStack() as e:
                hidden = sb("ffn_hidden", [P, FC, T], scope=e)
                stage_ffn_up(nc, K, dr, hidden)
                stage_out_project(nc, K, dr["w_down"][0], FC, 1, lambda k: hidden[:, k, :],
                                  lambda c: K.vec[:, 24 + c:25 + c])
                probe("x2", K.xT[:])
        K.bias_nsa, K.bias_swa = sb("bias_nsa", [P, NSA_H, T]), sb("bias_swa", [P, SWA_H, 2 * P])
        K.bias_cmp, K.sinks = sb("bias_cmp", [P, NSA_H, TT, 32]), sb("sinks", [P, 2, LAYERS, SWA_H])
        K.rope_m = sb("rope_m", [P, T])
        stage_bias(nc, K, dr)
        for l in range(LAYERS):
            with ExitStack() as e:
                L = Kit()
                L.qn = sb(name("qn"), [P, 2, T], scope=e)
                L.cq = sb(name("cq"), [P, 3, T], scope=e)
                L.blk = sb(name("blk"), [P, 2, 16, 32], scope=e)
                L.k_slc = sb(name("k_slc"), [P, T], scope=e)
                L.k_win = sb(name("k_win"), [P, T], scope=e)
                L.k_swa = sb(name("k_swa"), [P, T], scope=e)
                L.v_t = sb(name("v_t"), [P, 2, T], scope=e)
                L.kf = sb(name("kf"), [P, MLA_H, T], scope=e)
                L.qf = sb(name("qf"), [P, MLA_H, T], scope=e)
                L.qs = sb(name("qs"), [P, SWA_H // 2, T], scope=e)
                L.gates = sb(name("gates"), [P, 12 * TT], scope=e)
                L.sz = sb(name("sz"), [P, DC, T], scope=e)
                L.mix = sb(name("mix"), [P, DC, T], scope=e)
                L.kc = sb(name("kc"), [P, 32], scope=e)
                L.vc = sb(name("vc"), [32, HD], scope=e)
                L.v_slc = sb(name("v_slc"), [P, TT, HD], scope=e)
                L.v_win = sb(name("v_win"), [P, TT, HD], scope=e)
                L.v_swa = sb(name("v_swa"), [P, TT, HD], scope=e)
                L.v_mla = sb(name("v_mla"), [P, TT, MLA_H * HD], scope=e)
                norm(VECS["norm_pre_2"][0] + DC * l)
                stage_layer_project(nc, K, dr, l, L)
                stage_latents(nc, K, dr, l, L)
                stage_attention(nc, K, list(layer_jobs(K, L, l)), T, 3, 3)
                probe(f"mix{l}", L.mix[:])
                stage_out_project(nc, K, dr["w_out_2"][l], DC, 4, lambda k: L.mix[:, k, :],
                                  lambda c: K.vec[:, 48 + DC * l + c:49 + DC * l + c])
                probe(f"y{l}", K.xT[:])
        stage_store(nc, K, out)


def kernel(**inputs):
    import concourse.bacc as bacc
    from concourse.bass_utils import run_bass_kernel_spmd

    nc = bacc.Bacc("TRN2", target_bir_lowering=False, num_devices=1)
    arrays = {k: np.ascontiguousarray(v) for k, v in inputs.items()}
    arrays |= shape_constants()
    dr = {k: nc.dram_tensor(f"{k}_dram", a.shape, mybir.dt.from_np(a.dtype), kind="ExternalInput").ap()
          for k, a in arrays.items()}
    dr["scratch"] = nc.dram_tensor("bias_scratch", (2, NSA_H + SWA_H, 2 * T), F32, kind="Internal").ap()
    out = nc.dram_tensor("out_dram", (1, T, D), F32, kind="ExternalOutput").ap()
    build(nc, dr, out)
    r = run_bass_kernel_spmd(nc, [{f"{k}_dram": a for k, a in arrays.items()}], core_ids=[0])
    return r.results[0]["out_dram"]
```

```python
import math
from contextlib import ExitStack

import numpy as np

import concourse.bass as bass
from concourse import mybir

F32 = mybir.dt.float32
F32R = mybir.dt.float32r
I32 = mybir.dt.int32
ALU = mybir.AluOpType
ACT = mybir.ActivationFunctionType
AX_X = mybir.AxisListType.X

P = 128
T = 512
TT = T // P
D = 1024
DC = D // P
EPS = 1e-6
NEG = -1e30
FF = 2816
FC = FF // P
HEADS = 4
CLASSES = 4
A_DIM = 64
LAM_INIT = 0.8 - 0.6 * math.exp(0.0)
LAYERS = 2
NSA_H, MLA_H, SWA_H = 4, 4, 8
HD = 64
CMP = T // 16 - 1
D_IN2 = 2732
THETA = 10000.0

VECS = {"pre_mix_g": (0, 8), "post_mix_g": (8, 8), "pre_ffn_g": (16, 8), "post_ffn_g": (24, 8),
        "norm_pre_2": (32, 16), "norm_post_2": (48, 16), "mla_q_norm_2": (64, 4), "mla_kv_norm_2": (68, 2),
        "diff_head_g": (70, 1)}
NVEC = 71


def shape_constants():
    f = np.float32
    p = np.arange(P)
    cols = np.zeros((P, 8), f)
    inv64 = f(THETA) ** (-np.arange(0, 64, 2, dtype=f) / f(64))
    inv128 = f(THETA) ** (-np.arange(0, 128, 2, dtype=f) / f(128))
    cols[:, 0] = inv64[p % 32]
    cols[:, 1] = inv128[p % 64]
    cols[:, 2] = np.where(p % 64 < 32, 1.0, -1.0)
    cols[:, 3] = np.where(p < 64, 1.0, -1.0)
    cols[:, 4] = p >= 31
    j = np.arange(T)
    causal = np.where(p[:, None] + (T - P) - j[None] >= 0, 0.0, NEG).astype(f)
    i = np.arange(P)
    mask_b = np.full((P, CLASSES, 6 * P), NEG, f)
    for r in range(CLASSES):
        for b in range(CLASSES):
            dist = CLASSES * (p[:, None] - i[None]) + r - b
            mask_b[:, r, b * P:(b + 1) * P] = np.where((dist >= 0) & (dist <= 128), 0.0, NEG)
        back = p[:, None] - i[None]
        mask_b[:, r, 4 * P:5 * P] = np.where(back >= 0, 0.0, NEG)
        mask_b[:, r, 5 * P:6 * P] = np.where((back >= 0) & (back % 4 == 0), 0.0, NEG)
    dist = np.arange(-T, T)
    d0 = np.maximum(dist, 0)
    large = 16 + (np.log(np.maximum(d0, 1).astype(f) / f(16)) / f(math.log(512 / 16)) * f(16)).astype(np.int32)
    bucket = np.where(d0 < 16, d0, np.minimum(large, 31))
    hot = np.zeros((34, 2 * T), f)
    hot[bucket, np.arange(2 * T)] = 1.0
    hot[32] = np.where(dist < 0, NEG, 0.0)
    hot[33] = np.where(dist >= 128, NEG, 0.0)
    back_hot = np.zeros_like(hot)
    back_hot[:, :2 * T - 1] = hot[:, 1:][:, ::-1]
    mask_rows = np.zeros((2, NSA_H + SWA_H), f)
    mask_rows[0] = 1.0
    mask_rows[1, NSA_H:] = 1.0
    inv32 = f(THETA) ** (-np.arange(16, dtype=f) / f(16))
    ang = np.arange(T, dtype=f)[None] * inv32[:, None]
    cos, sin = np.cos(ang), np.sin(ang)
    rope_m = np.concatenate([cos, cos, -sin, sin]).astype(f)
    return {"c_cols": cols, "c_causal": causal, "c_mask_b": mask_b, "c_hot": hot, "c_back_hot": back_hot,
            "c_mask_rows": mask_rows, "c_rope_m": rope_m}


class Counted:

    def __init__(self, handle):
        self.handle, self.base = handle, 0

    def at(self, n):
        return self.base + n

    def close(self, n):
        self.base += n


class Ring:

    SIZE = 2048

    def __init__(self, nc, raw, high, low, loaded, whole, split, used):
        self.nc, self.raw, self.high, self.low = nc, raw, high, low
        self.loaded = loaded
        self.whole = whole
        self.split = split
        self.used = used
        self.base = 0
        self.total = [0, 0]
        self.seen, self.parts = [], []

    def load(self, sp, plan, k, it=None):
        n = len(self.seen)
        parts = plan(self.raw[:, n % 2, :], k // 2 + (0 if it is None else it), k % 2)
        if n >= 2:
            sp.wait_ge(self.split, n - 1 + (0 if it is None else 2 * it))
        for dst, src in parts:
            sp.dma_start(dst, src).then_inc(self.loaded[n % 2], 16)
        self.note(len(parts))

    def note(self, parts):
        self.total[len(self.seen) % 2] += 16 * parts
        self.seen.append(self.total[len(self.seen) % 2])
        self.parts.append(parts)

    def stream(self, sp, plan, slots, following, loop=True):
        if loop and slots > 2:
            with sp.Fori(0, slots // 2 - 1) as i:
                for u in range(2):
                    self.load(sp, plan, 2 + u, i)
            for _ in range(slots // 2 - 2):
                for _ in range(2):
                    self.note(self.parts[-2])
        elif slots > 2:
            for k in range(2, slots):
                self.load(sp, plan, k)
        if following is not None:
            for k in range(2):
                self.load(sp, following, k)

    def split_high(self, act, k, it=None):
        n = self.base + k
        if n >= len(self.seen):
            return
        s = n % 2
        act.wait_ge(self.loaded[s], self.seen[n] + (0 if it is None else 16 * self.parts[n] * it))
        if n >= 2:
            act.wait_ge(self.used, n - 1 + (0 if it is None else 2 * it))
        self.nc.scalar.activation(self.high[:, s, :], self.raw[:, s, :], ACT.Copy).then_inc(self.whole, 1)

    def split_low(self, dve, k, it=None):
        n = self.base + k
        if n >= len(self.seen):
            return
        s = n % 2
        dve.wait_ge(self.whole, n + 1 + (0 if it is None else 2 * it))
        self.nc.vector.tensor_tensor(self.low[:, s, :], self.raw[:, s, :], self.high[:, s, :].bitcast(F32),
                                     ALU.subtract).then_inc(self.split, 1)

    def use(self, pe, k, it=None):
        n = self.base + k
        pe.wait_ge(self.split, n + 1 + (0 if it is None else 2 * it))
        return self.high[:, n % 2, :], self.low[:, n % 2, :]

    def close(self, slots):
        self.base += slots


def rounds_of(engine, rounds, body):
    if rounds > 1:
        with engine.Fori(0, rounds - 1) as i:
            for u in range(2):
                body(u, i)
    for u in range(2):
        body(2 * (rounds - 1) + u, None)


def index(k, it):
    return k if it is None else k + 2 * it


class Kit:
    pass


def tiles(flat, a, b):
    return flat[:, 0:a * b].rearrange("p (a b) -> p a b", b=b)


def column_plan(w, kt, width, first=0, step=None):
    step = step or width

    def plan(raw, c, u):
        src = w[:, bass.ds(first + (2 * c + u) * step, width)].rearrange("(k p) n -> p k n", p=P)
        return [(tiles(raw, kt, width), src)]
    return plan



def stage_setup(nc, K, dr):
    with ExitStack() as ctx:
        def sb(name, shape, dt=F32):
            return ctx.enter_context(nc.sbuf_tensor(name, shape, dt))

        def sem(name):
            return ctx.enter_context(nc.semaphore(name))

        x_tok = sb("x_tok", [P, TT, D])
        vec_rows = sb("vec_rows", [NVEC, P])
        conv_rows = sb("conv_rows", [2 * FC, 4, P])
        pos_rows = sb("pos_rows", [P, P])
        pos_i = sb("pos_i", [P, T], I32)
        pos_f = sb("pos_f", [P, T])
        ang = sb("ang", [P, T])
        turns = sb("turns", [P, T])
        red = sb("red", [P, T])
        lam_in = sb("lam_in", [P, 4 * A_DIM])
        lam_prod = sb("lam_prod", [P, 2, A_DIM])
        lam_sum = sb("lam_sum", [P, 2])
        lam_exp = sb("lam_exp", [P, 2])
        s_in, s_ident, s_tr = sem("setup_loaded"), sem("ident_ready"), sem("setup_transposed")
        s_free_v, s_free_a = sem("setup_bank_free_dve"), sem("setup_bank_free_act")
        s_red, s_sin, s_lsum, s_lexp = sem("angle_reduced"), sem("sin_done"), sem("lam_summed"), sem("lam_exped")
        block = ctx.enter_context(nc.Block())
        n_loads = 0

        @block.sync
        def _(sp):
            nonlocal n_loads

            def load(dst, src):
                nonlocal n_loads
                sp.dma_start(dst, src).then_inc(s_in, 16)
                n_loads += 1

            load(x_tok[:], dr["x"].rearrange("b (t p) d -> p (b t) d", p=P))
            for name, (r0, n) in VECS.items():
                load(vec_rows[r0:r0 + n, :], dr[name].rearrange("l (c p) -> (l c) p", p=P))
            load(conv_rows[:, 0:3, :], dr["conv_w"].rearrange("l j (c p) -> c (l j) p", p=P))
            load(conv_rows[:, 3, :], dr["conv_b"].rearrange("l (c p) -> (l c) p", p=P))
            for half in range(2):
                load(pos_rows[:, half * HD:(half + 1) * HD], dr["cmp_pos_2"].rearrange("l i s d -> (l i s) d"))
            load(pos_i[:], dr["positions"].partition_broadcast(P)[:, 0, :])
            load(lam_in[:], dr["diff_lambda"].rearrange("l a d -> l (a d)").partition_broadcast(P)[:, 0, :])
            load(K.cols[:], dr["c_cols"])
            load(K.causal[:], dr["c_causal"])
            K.ring.stream(sp, None, 0, plan_a(dr), loop=False)

        @block.gpsimd
        def _(pool):
            nc.gpsimd.memset(K.ident[:], 0.0)
            nc.gpsimd.memset(K.ones[:], 1.0)
            nc.gpsimd.memset(K.eps[:], EPS)
            pool.drain()
            nc.gpsimd.affine_select(out=K.ident[:], in_=K.ident[:], compare_op=ALU.not_equal, fill=1.0, base=0,
                                    pattern=[[-1, P]], channel_multiplier=1).then_inc(s_ident, 1)

        N_TR = DC + 6

        @block.tensor
        def _(pe):
            pe.wait_ge(s_ident, 1)
            pe.wait_ge(s_in, 16 * n_loads)
            for n in range(N_TR):
                if n >= 8:
                    pe.wait_ge((s_free_v, s_free_a)[n % 2], (n - 8) // 2 + 1)
                bank = K.ps[:, n % 8, :]
                if n < DC:
                    for t in range(TT):
                        last = nc.tensor.transpose(bank[:, t * P:(t + 1) * P], x_tok[:, t, n * P:(n + 1) * P], K.ident[:])
                elif n == DC:
                    last = nc.tensor.transpose(bank[:, 0:NVEC], vec_rows[:], K.ident[0:NVEC, 0:NVEC])
                elif n < DC + 5:
                    last = nc.tensor.transpose(bank[:, 0:2 * FC], conv_rows[:, n - DC - 1, :], K.ident[0:2 * FC, 0:2 * FC])
                else:
                    last = nc.tensor.transpose(bank[:, 0:P], pos_rows[:], K.ident[:])
                last.then_inc(s_tr, 1)

        def copy_of(n):
            bank = K.ps[:, n % 8, :]
            if n < DC:
                return K.xT[:, n, :], bank[:, 0:T]
            if n == DC:
                return K.vec[:], bank[:, 0:NVEC]
            if n < DC + 5:
                return K.conv[:, n - DC - 1, :], bank[:, 0:2 * FC]
            return K.peT[:], bank[:, 0:P]

        TWO_PI = 2 * math.pi
        HI = 6.28125
        MID = float(np.float32(np.round((TWO_PI - HI) * 2 ** 21) / 2 ** 21))
        LO = TWO_PI - HI - MID
        MAGIC = 1.5 * 2 ** 23
        tables = [(0, 0, K.sin_a), (0, 1, K.cos_a), (1, 0, K.sin_b), (1, 1, K.cos_b)]

        @block.vector
        def _(dve):
            v = nc.vector
            dve.wait_ge(s_in, 16 * n_loads)
            for n in range(0, N_TR, 2):
                dve.wait_ge(s_tr, n + 1)
                v.tensor_copy(*copy_of(n)).then_inc(s_free_v, 1)
            lam4 = lam_in[:].rearrange("p (a d) -> p a d", d=A_DIM)
            v.tensor_tensor(lam_prod[:], lam4[:, 0:4:2, :], lam4[:, 1:4:2, :], ALU.mult)
            v.tensor_copy(pos_f[:], pos_i[:])
            dve.drain()
            v.reduce_sum(lam_sum[:], lam_prod[:], AX_X).then_inc(s_lsum, 1)
            for n, (col, quarter, _) in enumerate(tables):
                if not quarter:
                    v.tensor_scalar(ang[:], pos_f[:], K.cols[:, col:col + 1], None, ALU.mult)
                    dve.drain()
                v.tensor_scalar(turns[:], ang[:], 1 / TWO_PI, 0.25 * quarter, ALU.mult, ALU.add)
                dve.drain()
                v.tensor_scalar(turns[:], turns[:], MAGIC, None, ALU.add)
                dve.drain()
                v.tensor_scalar(turns[:], turns[:], MAGIC, None, ALU.subtract)
                dve.drain()
                if n:
                    dve.wait_ge(s_sin, n)
                v.scalar_tensor_tensor(out=red[:], in0=turns[:], scalar=-HI, in1=ang[:], op0=ALU.mult, op1=ALU.add)
                dve.drain()
                v.scalar_tensor_tensor(out=red[:], in0=turns[:], scalar=-MID, in1=red[:], op0=ALU.mult, op1=ALU.add)
                dve.drain()
                v.scalar_tensor_tensor(out=red[:], in0=turns[:], scalar=-LO, in1=red[:], op0=ALU.mult, op1=ALU.add)
                dve.drain()
                if quarter:
                    v.tensor_scalar(red[:], red[:], math.pi / 2, None, ALU.add)
                    dve.drain()
                v.tensor_scalar(red[:], red[:], 3.1415925, -3.1415925, ALU.min, ALU.max).then_inc(s_red, 1)
            dve.wait_ge(s_sin, 4)
            v.tensor_scalar(K.sin_a[:], K.sin_a[:], K.cols[:, 2:3], None, ALU.mult)
            v.tensor_scalar(K.sin_b[:], K.sin_b[:], K.cols[:, 3:4], None, ALU.mult)
            dve.wait_ge(s_lexp, 1)
            v.tensor_scalar(K.neg_lam[:], lam_exp[:, 1:2], lam_exp[:, 0:1], -LAM_INIT, ALU.subtract, ALU.add)
            v.tensor_scalar(K.vec[:, 70:71], K.vec[:, 70:71], 1.0 - LAM_INIT, None, ALU.mult)
            for k in range(2):
                K.ring.split_low(dve, k)
            dve.drain()

        @block.scalar
        def _(act):
            for n in range(1, N_TR, 2):
                act.wait_ge(s_tr, n + 1)
                nc.scalar.activation(*copy_of(n), ACT.Copy).then_inc(s_free_a, 1)
            act.wait_ge(s_lsum, 1)
            nc.scalar.activation(lam_exp[:], lam_sum[:], ACT.Exp).then_inc(s_lexp, 1)
            for n, (_, _, table) in enumerate(tables):
                act.wait_ge(s_red, n + 1)
                nc.scalar.activation(table[:], red[:], ACT.Sin).then_inc(s_sin, 1)
            for k in range(2):
                K.ring.split_high(act, k)


def stage_norm(nc, K, gain, high, low):
    with ExitStack() as ctx:
        sq = ctx.enter_context(nc.sbuf_tensor(K.name("sq"), [P, 2, T], F32))
        rstd = ctx.enter_context(nc.sbuf_tensor(K.name("rstd"), [P, T], F32))
        block = ctx.enter_context(nc.Block())
        stat = K.ps[:, 0, :]
        squared, summed, rooted = K.s("squared"), K.s("summed"), K.s("rooted")
        normed, whole = K.s("normed"), K.s("x_high")

        @block.scalar
        def _(act):
            for c in range(DC):
                if c >= 2:
                    act.wait_ge(summed.handle, summed.at(c - 1))
                nc.scalar.activation(sq[:, c % 2, :], K.xT[:, c, :], ACT.Square).then_inc(squared.handle, 1)
            act.wait_ge(summed.handle, summed.at(DC))
            nc.scalar.activation(rstd[:], stat, ACT.Sqrt, bias=K.eps[:], scale=1.0 / D).then_inc(rooted.handle, 1)
            for c in range(DC):
                act.wait_ge(normed.handle, normed.at(c + 1))
                nc.scalar.activation(high[:, c, :], sq[:, c % 2, :], ACT.Copy).then_inc(whole.handle, 1)

        @block.tensor
        def _(pe):
            for c in range(DC):
                pe.wait_ge(squared.handle, squared.at(c + 1))
                nc.tensor.matmul(stat, K.ones[:], sq[:, c % 2, :], start=(c == 0), stop=(c == DC - 1))\
                    .then_inc(summed.handle, 1)

        @block.vector
        def _(dve):
            v = nc.vector

            def take_low(c):
                dve.wait_ge(whole.handle, whole.at(c + 1))
                v.tensor_tensor(low[:, c, :], sq[:, c % 2, :], high[:, c, :].bitcast(F32), ALU.subtract)
                dve.drain()

            dve.wait_ge(rooted.handle, rooted.at(1))
            v.reciprocal(rstd[:], rstd[:])
            dve.drain()
            for c in range(DC):
                if c >= 2:
                    take_low(c - 2)
                v.scalar_tensor_tensor(out=sq[:, c % 2, :], in0=K.xT[:, c, :], scalar=gain(c), in1=rstd[:],
                                       op0=ALU.mult, op1=ALU.mult).then_inc(normed.handle, 1)
            for c in range(DC - 2, DC):
                take_low(c)

        squared.close(DC)
        summed.close(DC)
        rooted.close(1)
        normed.close(DC)
        whole.close(DC)


def stage_head_norm(nc, K, oT, gain):
    with ExitStack() as ctx:
        sq = ctx.enter_context(nc.sbuf_tensor(K.name("hsq"), [P, HEADS, T], F32))
        rstd = ctx.enter_context(nc.sbuf_tensor(K.name("hrstd"), [P, HEADS, T], F32))
        block = ctx.enter_context(nc.Block())
        squared, summed, rooted = K.s("squared"), K.s("summed"), K.s("rooted")

        @block.scalar
        def _(act):
            for h in range(HEADS):
                nc.scalar.activation(sq[:, h, :], oT[:, h, :], ACT.Square).then_inc(squared.handle, 1)
            for h in range(HEADS):
                act.wait_ge(summed.handle, summed.at(h + 1))
                nc.scalar.activation(rstd[:, h, :], K.ps[:, h, :], ACT.Sqrt, bias=K.eps[:], scale=1.0 / P)\
                    .then_inc(rooted.handle, 1)

        @block.tensor
        def _(pe):
            for h in range(HEADS):
                pe.wait_ge(squared.handle, squared.at(h + 1))
                nc.tensor.matmul(K.ps[:, h, :], K.ones[:], sq[:, h, :], start=True, stop=True)\
                    .then_inc(summed.handle, 1)

        @block.vector
        def _(dve):
            for h in range(HEADS):
                dve.wait_ge(rooted.handle, rooted.at(h + 1))
                nc.vector.reciprocal(rstd[:, h, :], rstd[:, h, :])
            dve.drain()
            for h in range(HEADS):
                nc.vector.scalar_tensor_tensor(out=oT[:, h, :], in0=oT[:, h, :], scalar=gain, in1=rstd[:, h, :],
                                               op0=ALU.mult, op1=ALU.mult)
            dve.drain()

        squared.close(HEADS)
        summed.close(HEADS)
        rooted.close(HEADS)


def product(nc, bank, w, src, kt):
    for k in range(kt):
        last = nc.tensor.matmul(bank, w(k), src(k), start=(k == 0), stop=(k == kt - 1))
    return last


def product3(nc, bank, stationary, moving, kt, start=True, stop=True):
    for k in range(kt):
        for i, (a, b) in enumerate(((0, 0), (0, 1), (1, 0))):
            last = nc.tensor.matmul(bank, stationary(a, k), moving(b, k), start=start and k == 0 and i == 0,
                                    stop=stop and k == kt - 1 and i == 2)
    return last


def stage_project_a(nc, K, dr, qk, v_tok, following):
    with ExitStack() as ctx:
        rot = ctx.enter_context(nc.sbuf_tensor(K.name("rot"), [P, 2, T], F32))
        block = ctx.enter_context(nc.Block())
        ring, h = K.ring, K.h
        ready, free = K.s("chunk_ready"), [K.s(f"bank_free{b}") for b in range(4)]
        QK = 2 * HEADS
        N = QK + 2 * TT

        @block.sync
        def _(sp):
            ring.stream(sp, plan_a(dr), 6, following)

        @block.tensor
        def _(pe):
            c = 0
            for g in range(6):
                w = [tiles(x, DC, 256) for x in ring.use(pe, g)]
                for j in range(2 if g < 4 else TT):
                    if c >= 4:
                        pe.wait_ge(free[c % 4].handle, free[c % 4].at(c // 4))
                    bank = K.ps[:, c % 4, :]
                    if g < 4:
                        last = product3(nc, bank, lambda a, k: w[a][:, k, j * P:(j + 1) * P],
                                        lambda a, k: h[a][:, k, :], DC)
                    else:
                        last = product3(nc, bank[:, 0:256], lambda a, k: h[a][:, k, j * P:(j + 1) * P],
                                        lambda a, k: w[a][:, k, :], DC)
                    last.then_inc(ready.handle, 1)
                    c += 1
                pe.drain().then_inc(ring.used, 1)

        @block.scalar
        def _(act):
            for g in range(6):
                ring.split_high(act, g + 2)

        @block.vector
        def _(dve):
            v = nc.vector
            for c in range(N):
                dve.wait_ge(ready.handle, ready.at(c + 1))
                if c < QK and c % 2 == 1 or c >= QK and c % 4 == 3:
                    ring.split_low(dve, (c // 2 if c < QK else 4 + (c - QK) // 4) + 2)
                bank = K.ps[:, c % 4, :]
                if c >= QK:
                    t, half = (c - QK) % 4, (c - QK) // 4
                    v.tensor_copy(v_tok[:, t, 256 * half:256 * half + 256], bank[:, 0:256])\
                        .then_inc(free[c % 4].handle, 1)
                    continue
                for q in range(4):
                    o = 32 * (q ^ 1)
                    v.tensor_tensor(rot[o:o + 32, c % 2, :], bank[32 * q:32 * q + 32, :],
                                    K.sin_a[32 * q:32 * q + 32, :], ALU.mult)
                v.tensor_tensor(qk[:, c, :], bank, K.cos_a[:], ALU.mult).then_inc(free[c % 4].handle, 1)
                dve.drain()
                v.tensor_tensor(qk[:, c, :], qk[:, c, :], rot[:, c % 2, :], ALU.add)
            dve.drain()

        ready.close(N)
        for b in range(4):
            free[b].close(N // 4)
        ring.close(6)


def stage_project_b(nc, K, qk, v_tok, plan_qk, plan_v, following):
    with ExitStack() as ctx:
        rot = ctx.enter_context(nc.sbuf_tensor(K.name("rotb"), [P, 2, T], F32))
        turned = ctx.enter_context(nc.sbuf_tensor(K.name("rope_tmp"), [P, 2, T], F32))
        block = ctx.enter_context(nc.Block())
        ring, h = K.ring, K.h
        ready, free = K.s("chunk_ready"), [K.s(f"bank_free{b}") for b in range(4)]

        @block.sync
        def _(sp):
            with sp.Fori(0, 2) as i:
                for u in range(2):
                    ring.load(sp, plan_qk, 2 + u, i)
            for _ in range(2):
                ring.note(1)
            for k in range(3):
                ring.load(sp, plan_v, k)
            if following is not None:
                for k in range(2):
                    ring.load(sp, following, k)

        @block.tensor
        def _(pe):
            with pe.Fori(0, 3) as i:
                for u in range(2):
                    w = [tiles(x, DC, 256) for x in ring.use(pe, u, i)]
                    for j in range(2):
                        b = 2 * u + j
                        pe.wait_ge(free[b].handle, free[b].at(0) + i)
                        product3(nc, K.ps[:, b, :], lambda a, k: w[a][:, k, j * P:(j + 1) * P],
                                 lambda a, k: h[a][:, k, :], DC).then_inc(ready.handle, 1)
                    pe.drain().then_inc(ring.used, 1)
            for g in range(3):
                w = [tiles(x, DC, 256) for x in ring.use(pe, 6 + g)]
                for r in range(CLASSES):
                    pe.wait_ge(free[r].handle, free[r].at(3 + g))
                    product3(nc, K.ps[:, r, 0:256], lambda a, k: h[a][:, k, r:T:CLASSES],
                             lambda a, k: w[a][:, k, :], DC).then_inc(ready.handle, 1)
                pe.drain().then_inc(ring.used, 1)

        @block.scalar
        def _(act):
            with act.Fori(0, 3) as i:
                for u in range(2):
                    ring.split_high(act, u + 2, i)
            for g in range(3):
                ring.split_high(act, 6 + g + 2)

        @block.vector
        def _(dve):
            v = nc.vector
            with dve.Fori(0, 3) as i:
                for u in range(2):
                    for j in range(2):
                        b = 2 * u + j
                        dve.wait_ge(ready.handle, ready.at(b + 1) + 4 * i)
                        if j == 1:
                            ring.split_low(dve, u + 2, i)
                        bank = K.ps[:, b, :]
                        for q in range(2):
                            o = 64 * (q ^ 1)
                            v.tensor_tensor(rot[o:o + 64, j, :], bank[64 * q:64 * q + 64, :],
                                            K.sin_b[64 * q:64 * q + 64, :], ALU.mult)
                        v.tensor_tensor(turned[:, j, :], bank, K.cos_b[:], ALU.mult).then_inc(free[b].handle, 1)
                        dve.drain()
                        v.tensor_tensor(qk[:, bass.ds(4 * i + b, 1), :].rearrange("p a (r i) -> p (a i) r", r=CLASSES),
                                        turned[:, j, :].rearrange("p (i r) -> p i r", r=CLASSES),
                                        rot[:, j, :].rearrange("p (i r) -> p i r", r=CLASSES), ALU.add)
            for g in range(3):
                for r in range(CLASSES):
                    dve.wait_ge(ready.handle, ready.at(12 + 4 * g + r + 1))
                    if r == CLASSES - 1:
                        ring.split_low(dve, 6 + g + 2)
                    v.tensor_copy(v_tok[:, g, r, :], K.ps[:, r, 0:256]).then_inc(free[r].handle, 1)
            dve.drain()

        ready.close(24)
        for b in range(4):
            free[b].close(6)
        ring.close(9)


def stage_attention(nc, K, jobs, width, n_s, n_t, look):
    with ExitStack() as ctx:
        def sb(name, shape):
            return ctx.enter_context(nc.sbuf_tensor(K.name(name), shape, F32))

        banks = -(-width // T)
        n_p = look + 2
        prob = sb("prob", [P, n_p, width])
        prob_t = sb("prob_t", [P, 2, width])
        top = sb("top", [P, n_p])
        neg_top = sb("neg_top", [P, n_p])
        den = sb("den", [P, n_p])
        sink_exp = sb("sink_exp", [P, n_p])
        coef = sb("coef", [P, n_p])
        block = ctx.enter_context(nc.Block())
        n = len(jobs)
        flat = K.ps[:].rearrange("p b t -> p (b t)")

        def scores_at(j):
            o = (j % n_s) * banks * T
            return flat[:, o:o + width]

        def probs_t_at(j):
            o = (n_s + j % n_t) * banks * T
            return flat[:, o:o + width]

        o_bank = (n_s + n_t) * banks
        group, g = [], 0
        for job in jobs:
            group.append(g)
            g += job["last"]
        n_out = g

        def out_at(j):
            p0, m = jobs[j]["rows"]
            return K.ps[p0:p0 + m, o_bank + group[j] % 2, 0:P]

        scored, masked, topped = K.s("scored"), K.s("masked"), K.s("topped")
        exped, weighed, scaled = K.s("exped"), K.s("weighed"), K.s("scaled")
        turned, copied, mixed, stored = K.s("turned"), K.s("copied"), K.s("mixed"), K.s("stored")

        @block.tensor
        def _(pe):
            def scores(j):
                if j >= n_s:
                    pe.wait_ge(masked.handle, masked.at(j - n_s + 1))
                for c0, q, k in jobs[j]["scores"]:
                    last = nc.tensor.matmul(scores_at(j)[:, c0:c0 + k.shape[-1]], q, k, start=True, stop=True)
                last.then_inc(scored.handle, 1)

            def turn(j):
                pe.wait_ge(scaled.handle, scaled.at(j + 1))
                if j >= n_t:
                    pe.wait_ge(copied.handle, copied.at(j - n_t + 1))
                for c0, m, _ in jobs[j]["values"]:
                    src = prob[:, j % n_p, c0:c0 + m]
                    if m == P:
                        last = nc.tensor.transpose(probs_t_at(j)[:, c0:c0 + P], src, K.ident[:])
                    else:
                        last = nc.tensor.matmul(probs_t_at(j)[0:m, c0:c0 + P], src, K.ident[:], start=True, stop=True)
                last.then_inc(turned.handle, 1)

            def mix(j):
                pe.wait_ge(copied.handle, copied.at(j + 1))
                if jobs[j]["first"] and group[j] >= 2:
                    pe.wait_ge(stored.handle, stored.at(group[j] - 1))
                values = jobs[j]["values"]
                for i, (c0, m, v) in enumerate(values):
                    last = nc.tensor.matmul(out_at(j), v, prob_t[0:m, j % 2, c0:c0 + P],
                                            start=jobs[j]["first"] and i == 0,
                                            stop=jobs[j]["last"] and i == len(values) - 1)
                last.then_inc(mixed.handle, 1)

            for s in range(n + look + 1):
                if s < n:
                    scores(s)
                if 0 <= s - look < n:
                    turn(s - look)
                if 0 <= s - look - 1 < n:
                    mix(s - look - 1)

        @block.vector
        def _(dve):
            v = nc.vector

            def mask_and_top(j):
                job = jobs[j]
                b, w = j % n_p, job["width"]
                dve.wait_ge(scored.handle, scored.at(j + 1))
                if j >= n_p:
                    dve.wait_ge(turned.handle, turned.at(j - n_p + 1))
                v.tensor_tensor_reduce(out=prob[:, b, 0:w], in0=scores_at(j)[:, 0:w], in1=job["bias"], scale=1.0,
                                       scalar=-3e38, op0=ALU.add, op1=ALU.max, accum_out=top[:, b:b + 1])\
                    .then_inc(masked.handle, 1)
                dve.drain()
                if job["sink"] is None:
                    v.tensor_scalar(neg_top[:, b:b + 1], top[:, b:b + 1], -job["scale"], None, ALU.mult)\
                        .then_inc(topped.handle, 1)
                else:
                    v.tensor_scalar(neg_top[:, b:b + 1], top[:, b:b + 1], job["sink"][0], -job["scale"],
                                    ALU.max, ALU.mult).then_inc(topped.handle, 1)

            def weigh(j):
                job = jobs[j]
                b = j % n_p
                dve.wait_ge(exped.handle, exped.at(j + 1))
                d = den[:, b:b + 1]
                if job["sink"] is not None:
                    v.tensor_tensor(d, d, sink_exp[:, b:b + 1], ALU.add)
                    dve.drain()
                out = coef[:, b:b + 1]
                if job["gate"] is None:
                    v.reciprocal(out, d).then_inc(weighed.handle, 1)
                else:
                    v.reciprocal(d, d)
                    dve.drain()
                    v.tensor_tensor(out, d, job["gate"], ALU.mult).then_inc(weighed.handle, 1)

            def store(j):
                job = jobs[j]
                if not job["last"]:
                    return
                dve.wait_ge(mixed.handle, mixed.at(j + 1))
                if job["times"] is None:
                    v.tensor_copy(job["out"], out_at(j)).then_inc(stored.handle, 1)
                else:
                    v.tensor_tensor(job["out"], out_at(j), job["times"], ALU.mult).then_inc(stored.handle, 1)

            for s in range(n + look + 2):
                if s < n:
                    mask_and_top(s)
                if 0 <= s - 1 < n:
                    weigh(s - 1)
                if 0 <= s - look - 2 < n:
                    store(s - look - 2)
            dve.drain()

        @block.scalar
        def _(act):
            a = nc.scalar

            def exp(j):
                job = jobs[j]
                b, w = j % n_p, job["width"]
                act.wait_ge(topped.handle, topped.at(j + 1))
                if job["sink"] is not None:
                    a.activation(sink_exp[:, b:b + 1], job["sink"][1], ACT.Exp, bias=neg_top[:, b:b + 1])
                a.activation(prob[:, b, 0:w], prob[:, b, 0:w], ACT.Exp, bias=neg_top[:, b:b + 1], scale=job["scale"],
                             accum_out=den[:, b:b + 1]).then_inc(exped.handle, 1)

            def copy(j):
                act.wait_ge(turned.handle, turned.at(j + 1))
                if j >= 2:
                    act.wait_ge(mixed.handle, mixed.at(j - 1))
                rows, end = jobs[j]["turned"]
                a.activation(prob_t[0:rows, j % 2, 0:end], probs_t_at(j)[0:rows, 0:end], ACT.Copy)\
                    .then_inc(copied.handle, 1)

            for s in range(n + look):
                if s < n:
                    exp(s)
                if 0 <= s - look < n:
                    copy(s - look)

        @block.gpsimd
        def _(pool):
            for j in range(n):
                b, w = j % n_p, jobs[j]["width"]
                pool.wait_ge(weighed.handle, weighed.at(j + 1))
                nc.gpsimd.tensor_scalar(prob[:, b, 0:w], prob[:, b, 0:w], coef[:, b:b + 1], None, ALU.mult)\
                    .then_inc(scaled.handle, 1)

        for c in (scored, masked, topped, exped, weighed, scaled, turned, copied, mixed):
            c.close(n)
        stored.close(n_out)


def job(scores, width, bias, scale, values, out, rows=(0, P), first=True, last=True, gate=None, sink=None,
        times=None, turned=None):
    return dict(scores=scores, width=width, bias=bias, scale=scale, values=values, out=out, rows=rows, first=first,
                last=last, gate=gate, sink=sink, times=times, turned=turned or (P, width))


def split_all(nc, K, act, dve, pairs, whole, split):
    for n, (src, high, low) in enumerate(pairs):
        if act is not None:
            nc.scalar.activation(high, src, ACT.Copy).then_inc(whole.handle, 1)
        else:
            dve.wait_ge(whole.handle, whole.at(n + 1))
            nc.vector.tensor_tensor(low, src, high.bitcast(F32), ALU.subtract).then_inc(split.handle, 1)


def stage_gate_mix(nc, K, dr, oa, ob, dst, following):
    with ExitStack() as ctx:
        def sb(name, shape, dt=F32):
            return ctx.enter_context(nc.sbuf_tensor(K.name(name), shape, dt))

        sig = sb("sig", [P, 2, 2, T])
        o_high, o_low = sb("o_high", [P, 2, HEADS, T], F32R), sb("o_low", [P, 2, HEADS, T], F32R)
        block = ctx.enter_context(nc.Block())
        ring, h = K.ring, K.h
        KA = HEADS
        ready, gated, free = K.s("chunk_ready"), K.s("gated"), K.s("bank_free")
        summed, whole, split = K.s("summed"), K.s("x_high"), K.s("x_low")
        pairs = [(src[:, c, :], o_high[:, i, c, :], o_low[:, i, c, :]) for i, src in enumerate((oa, ob))
                 for c in range(HEADS)]

        @block.sync
        def _(sp):
            with sp.Fori(0, DC - 1) as i:
                for u in range(2):
                    ring.load(sp, plan_gate(dr), 2 + u, i)
            for _ in range(2 * (DC - 2)):
                ring.note(2)
            for k in range(2):
                ring.load(sp, following, k)

        @block.tensor
        def _(pe):
            def chunk(i):
                gates = [tiles(x, 2 * DC, P) for x in ring.use(pe, 0, i)]
                pe.wait_ge(free.handle, free.at(0) + i)
                for b in range(2):
                    product3(nc, K.ps[:, b, :], lambda a, k: gates[a][:, DC * b + k, :],
                             lambda a, k: h[a][:, k, :], DC).then_inc(ready.handle, 1)
                pe.drain().then_inc(ring.used, 1)
                outs = [tiles(x, 2 * KA, P) for x in ring.use(pe, 1, i)]
                for b in range(2):
                    product3(nc, K.ps[:, 2 + b, :], lambda a, k: outs[a][:, KA * b + k, :],
                             lambda a, k: (o_high, o_low)[a][:, b, k, :], KA).then_inc(ready.handle, 1)
                pe.drain().then_inc(ring.used, 1)

            pe.wait_ge(split.handle, split.at(2 * HEADS))
            with pe.Fori(0, DC) as i:
                chunk(i)

        def rounds(engine, body):
            with engine.Fori(0, DC - 1) as i:
                body(i, lambda k: (k, i))
            body(DC - 1, lambda k: (2 * (DC - 1) + k, None))

        @block.scalar
        def _(act):
            split_all(nc, K, act, None, pairs, whole, split)

            def chunk(i, slot):
                act.wait_ge(summed.handle, summed.at(0) + i)
                for b in range(2):
                    act.wait_ge(ready.handle, ready.at(b + 1) + 4 * i)
                    nc.scalar.activation(sig[:, 0, b, :], K.ps[:, b, :], ACT.Sigmoid).then_inc(gated.handle, 1)
                ring.split_high(act, *slot(2))
                ring.split_high(act, *slot(3))

            rounds(act, chunk)

        @block.vector
        def _(dve):
            v = nc.vector
            split_all(nc, K, None, dve, pairs, whole, split)

            def chunk(i, slot):
                dve.wait_ge(gated.handle, gated.at(2) + 2 * i)
                ring.split_low(dve, *slot(2))
                for b in range(2):
                    dve.wait_ge(ready.handle, ready.at(3 + b) + 4 * i)
                    last = v.tensor_tensor(sig[:, 1, b, :], sig[:, 0, b, :], K.ps[:, 2 + b, :], ALU.mult)
                last.then_inc(free.handle, 1)
                dve.drain()
                v.tensor_tensor(dst[:, bass.ds(i, 1), :].rearrange("p a t -> p (a t)"),
                                sig[:, 1, 0, :], sig[:, 1, 1, :], ALU.add).then_inc(summed.handle, 1)
                ring.split_low(dve, *slot(3))

            rounds(dve, chunk)
            dve.drain()

        ready.close(4 * DC)
        gated.close(2 * DC)
        free.close(DC)
        summed.close(DC)
        whole.close(2 * HEADS)
        split.close(2 * HEADS)
        ring.close(2 * DC)


def stage_out_project(nc, K, plan, kt, halves, per_slot, src, parts, gain, following):
    with ExitStack() as ctx:
        def sb(name, shape, dt=F32):
            return ctx.enter_context(nc.sbuf_tensor(K.name(name), shape, dt))

        yT = sb("yT", [P, DC, T])
        sq, total, rstd = sb("sq", [P, 2, T]), sb("total", [P, T]), sb("rstd", [P, T])
        x = parts or (sb("x_high", [P, kt, T], F32R), sb("x_low", [P, kt, T], F32R))
        block = ctx.enter_context(nc.Block())
        ring = K.ring
        ready, read, squared, summed = K.s("chunk_ready"), K.s("chunk_read"), K.s("squared"), K.s("summed")
        totaled, stat_ready, rooted, scaled = K.s("totaled"), K.s("stat_ready"), K.s("rooted"), K.s("y_scaled")
        whole, split = K.s("x_high"), K.s("x_low")
        slots = DC * halves // per_slot
        rounds, body = slots // 2, 2 * per_slot // halves
        banks = 4
        stat = K.ps[:, 7, :]
        pairs = [] if parts else [(src[:, k, :], x[0][:, k, :], x[1][:, k, :]) for k in range(kt)]

        @block.sync
        def _(sp):
            ring.stream(sp, plan, slots, following)

        @block.tensor
        def _(pe):
            if pairs:
                pe.wait_ge(split.handle, split.at(kt))
            kh = kt // halves
            def chunk(c, bank, k0, start, stop, w, j):
                return product3(nc, bank, lambda a, k: w[a][:, k, j * P:(j + 1) * P],
                                lambda a, k: x[a][:, k0 + k, :], kh, start, stop)

            if halves == 1:
                with pe.Fori(0, rounds) as i:
                    for u in range(2):
                        w = [tiles(t, kt, per_slot * P) for t in ring.use(pe, u, i)]
                        for j in range(per_slot):
                            q = u * per_slot + j
                            pe.wait_ge(read.handle, read.at(q) + body * i)
                            chunk(q, K.ps[:, q, :], 0, True, True, w, j).then_inc(ready.handle, 1)
                        pe.drain().then_inc(ring.used, 1)
            else:
                with pe.Fori(0, rounds // 2) as i:
                    for c in range(2):
                        pe.wait_ge(read.handle, read.at(c) + 2 * i)
                        for u in range(2):
                            n = 2 * c + u
                            pe.wait_ge(ring.split, ring.base + n + 1 + 4 * i)
                            w = [tiles(t[:, (ring.base + u) % 2, :], kh, P) for t in (ring.high, ring.low)]
                            last = chunk(c, K.ps[:, c, :], kh * u, u == 0, u == 1, w, 0)
                            if u:
                                last.then_inc(ready.handle, 1)
                            pe.drain().then_inc(ring.used, 1)
            pe.wait_ge(totaled.handle, totaled.at(DC))
            nc.tensor.matmul(stat, K.ones[:], total[:], start=True, stop=True).then_inc(stat_ready.handle, 1)

        per = 4 if halves == 1 else 2

        def each(engine, turn):
            n, step = DC // per, per * halves // per_slot
            with engine.Fori(0, n - 1) as i:
                turn(i, lambda k: (k, i * (step // 2)))
            turn(n - 1, lambda k: (step * (n - 1) + k, None))

        @block.scalar
        def _(act):
            split_all(nc, K, act, None, pairs, whole, split)
            for _ in range(per - 1):
                act.drain().then_inc(read.handle, 1)

            def take(q, i):
                act.wait_ge(ready.handle, ready.at(q + 1) + per * i)
                bank = K.ps[:, q, :]
                nc.scalar.activation(yT[:, bass.ds(per * i + q, 1), :].rearrange("p a t -> p (a t)"), bank, ACT.Copy)
                act.wait_ge(summed.handle, summed.at(q) + per * i)
                nc.scalar.activation(sq[:, q % 2, :], bank, ACT.Square).then_inc(squared.handle, 1)
                act.drain().then_inc(read.handle, 1)

            def turn(i, slot):
                if halves == 1:
                    for u in range(2):
                        for j in range(2):
                            take(2 * u + j, i)
                        ring.split_high(act, *slot(u + 2))
                else:
                    for c in range(2):
                        ring.split_high(act, *slot(2 * c + 2))
                        take(c, i)
                        ring.split_high(act, *slot(2 * c + 3))

            each(act, turn)
            act.wait_ge(stat_ready.handle, stat_ready.at(1))
            nc.scalar.activation(rstd[:], stat, ACT.Sqrt, bias=K.eps[:], scale=1.0 / D).then_inc(rooted.handle, 1)

        @block.gpsimd
        def _(pool):
            nc.gpsimd.memset(total[:], 0.0)
            pool.drain().then_inc(summed.handle, 1)
            with pool.Fori(0, DC // 2) as i:
                for q in range(2):
                    pool.wait_ge(squared.handle, squared.at(q + 1) + 2 * i)
                    nc.gpsimd.tensor_tensor(total[:], total[:], sq[:, q % 2, :], ALU.add).then_inc(summed.handle, 1)
                    pool.drain().then_inc(totaled.handle, 1)
            for c in range(DC):
                pool.wait_ge(scaled.handle, scaled.at(c + 1))
                nc.gpsimd.tensor_tensor(K.xT[:, c, :], K.xT[:, c, :], yT[:, c, :], ALU.add)
            pool.drain()

        @block.vector
        def _(dve):
            split_all(nc, K, None, dve, pairs, whole, split)

            def turn(i, slot):
                for k in range(per * halves // per_slot):
                    ring.split_low(dve, *slot(k + 2))

            each(dve, turn)
            dve.wait_ge(rooted.handle, rooted.at(1))
            nc.vector.reciprocal(rstd[:], rstd[:])
            dve.drain()
            for c in range(DC):
                nc.vector.scalar_tensor_tensor(out=yT[:, c, :], in0=yT[:, c, :], scalar=gain(c), in1=rstd[:],
                                               op0=ALU.mult, op1=ALU.mult).then_inc(scaled.handle, 1)

        ready.close(DC)
        read.close(DC + per - 1)
        squared.close(DC)
        summed.close(DC + 1)
        totaled.close(DC)
        stat_ready.close(1)
        rooted.close(1)
        scaled.close(DC)
        whole.close(len(pairs))
        split.close(len(pairs))
        ring.close(slots)


def stage_ffn_up(nc, K, high, low, plan, following):
    with ExitStack() as ctx:
        def sb(name, shape):
            return ctx.enter_context(nc.sbuf_tensor(K.name(name), shape, F32))

        taps = sb("taps", [P, 2, 4, 2])
        u_sb = sb("u_sb", [P, 2, 2, T])
        block = ctx.enter_context(nc.Block())
        ring, h = K.ring, K.h
        ready, free, tapped = K.s("chunk_ready"), K.s("banks_read"), K.s("taps_ready")
        biased, conved, gelued, done = K.s("biased"), K.s("conved"), K.s("gelued"), K.s("ffn_done")
        multiplied, whole = K.s("multiplied"), K.s("x_high")

        @block.sync
        def _(sp):
            ring.stream(sp, plan, FC, following)

        @block.tensor
        def _(pe):
            with pe.Fori(0, FC // 2) as i:
                for u in range(2):
                    w = [tiles(x, 2 * DC, P) for x in ring.use(pe, u, i)]
                    pe.wait_ge(free.handle, free.at(u) + 2 * i)
                    for half in range(2):
                        product3(nc, K.ps[:, 2 * u + half, :], lambda a, k: w[a][:, DC * half + k, :],
                                 lambda a, k: h[a][:, k, :], DC).then_inc(ready.handle, 1)
                    pe.drain().then_inc(ring.used, 1)

        @block.gpsimd
        def _(pool):
            conv = K.conv[:].rearrange("p j (h c) -> p j h c", h=2)
            with pool.Fori(0, FC // 2) as i:
                for u in range(2):
                    pool.wait_ge(done.handle, done.at(u) + 2 * i)
                    nc.gpsimd.tensor_copy(taps[:, u, :, :].unsqueeze(3), conv[:, :, :, bass.ds(2 * i + u, 1)])\
                        .then_inc(tapped.handle, 1)

        @block.scalar
        def _(act):
            def chunk(k, it):
                u, n = k % 2, index(k, it)
                act.wait_ge(tapped.handle, tapped.at(1) + n)
                act.wait_ge(done.handle, done.at(0) + n)
                for half in range(2):
                    act.wait_ge(ready.handle, ready.at(half + 1) + 2 * n)
                    nc.scalar.activation(u_sb[:, u, half, :], K.ps[:, 2 * u + half, :], ACT.Identity,
                                         bias=taps[:, u, 3, half:half + 1], scale=taps[:, u, 2, half:half + 1])\
                        .then_inc(biased.handle, 1)
                ring.split_high(act, k + 2, it)
                act.wait_ge(conved.handle, conved.at(1) + n)
                nc.scalar.activation(u_sb[:, u, 0, :], u_sb[:, u, 0, :], ACT.Gelu_apprx_tanh)\
                    .then_inc(gelued.handle, 1)
                act.wait_ge(multiplied.handle, multiplied.at(1) + n)
                nc.scalar.activation(high[:, bass.ds(n, 1), :].rearrange("p a t -> p (a t)"), u_sb[:, u, 0, :],
                                     ACT.Copy).then_inc(whole.handle, 1)

            rounds_of(act, FC // 2, chunk)

        @block.vector
        def _(dve):
            v = nc.vector
            dve.drain().then_inc(free.handle, 1)
            dve.drain().then_inc(done.handle, 1)

            def chunk(k, it):
                u, n = k % 2, index(k, it)
                for half in range(2):
                    dve.wait_ge(biased.handle, biased.at(half + 1) + 2 * n)
                    for back in (1, 2):
                        out = u_sb[:, u, half, back:T]
                        last = v.scalar_tensor_tensor(out=out, in0=K.ps[:, 2 * u + half, 0:T - back],
                                                      scalar=taps[:, u, 2 - back, half:half + 1], in1=out,
                                                      op0=ALU.mult, op1=ALU.add)
                        if back == 1:
                            dve.drain()
                        elif half == 0:
                            last.then_inc(conved.handle, 1)
                        else:
                            last.then_inc(free.handle, 1)
                dve.drain()
                ring.split_low(dve, k + 2, it)
                dve.wait_ge(gelued.handle, gelued.at(1) + n)
                v.tensor_tensor(u_sb[:, u, 0, :], u_sb[:, u, 0, :], u_sb[:, u, 1, :], ALU.mult)\
                    .then_inc(multiplied.handle, 1)
                dve.wait_ge(whole.handle, whole.at(1) + n)
                v.tensor_tensor(low[:, bass.ds(n, 1), :].rearrange("p a t -> p (a t)"), u_sb[:, u, 0, :],
                                high[:, bass.ds(n, 1), :].rearrange("p a t -> p (a t)").bitcast(F32),
                                ALU.subtract).then_inc(done.handle, 1)

            rounds_of(dve, FC // 2, chunk)
            dve.drain()

        ready.close(2 * FC)
        free.close(FC + 1)
        tapped.close(FC)
        biased.close(2 * FC)
        conved.close(FC)
        gelued.close(FC)
        multiplied.close(FC)
        whole.close(FC)
        done.close(FC + 1)
        ring.close(FC)


def stage_bias(nc, K, dr):
    with ExitStack() as ctx:
        def sb(name, shape):
            return ctx.enter_context(nc.sbuf_tensor(name, shape, F32))

        NH = NSA_H + SWA_H
        rel = sb("rel", [34, NH])
        hot = sb("hot", [34, 2, 2 * T])
        vecs = sb("bias_vecs", [NH, 2, 2 * T])
        cmp_t = sb("cmp_t", [CMP, NSA_H, T])
        flip = sb("flip", [P, P])
        s_in, s_rel, s_vec, s_cp = (ctx.enter_context(nc.semaphore(x)) for x in
                                    ("bias_in", "rel_scaled", "bias_by_distance", "bias_copied"))
        s_flip = ctx.enter_context(nc.semaphore("flip_ready"))
        s_out, s_back, s_turn = (ctx.enter_context(nc.semaphore(x)) for x in
                                 ("bias_in_dram", "bias_tiles_loaded", "cmp_bias_turned"))
        block = ctx.enter_context(nc.Block())
        scratch = dr["scratch"]

        @block.sync
        def _(sp):
            sp.dma_start(rel[0:32, :], dr["rel_bias_2"].rearrange("h b -> b h"), allow_slow_non_contiguous=True).then_inc(s_in, 16)
            sp.dma_start(rel[32:34, :], dr["c_mask_rows"]).then_inc(s_in, 16)
            sp.dma_start(hot[:, 0, :], dr["c_hot"]).then_inc(s_in, 16)
            sp.dma_start(hot[:, 1, :], dr["c_back_hot"]).then_inc(s_in, 16)
            sp.dma_start(K.sinks[:, 0, :, :], dr["swa_sinks_2"].partition_broadcast(P)).then_inc(s_in, 16)
            sp.dma_start(K.rope_m[64:128, :], dr["c_rope_m"]).then_inc(s_in, 16)
            sp.wait_ge(s_cp, 4)
            sp.dma_start(scratch.rearrange("a h m -> h a m"), vecs[:]).then_inc(s_out, 16)
            sp.wait_ge(s_out, 16)
            row, back = 2 * T, NH * 2 * T
            sp.dma_start(K.bias_nsa[:], bass.AP(tensor=scratch.tensor, offset=back,
                                                ap=[[1, P], [row, NSA_H], [1, T]])).then_inc(s_back, 16)
            sp.dma_start(K.bias_swa[:], bass.AP(tensor=scratch.tensor, offset=back + NSA_H * row + T - 2 * P,
                                                ap=[[1, P], [row, SWA_H], [1, 2 * P]])).then_inc(s_back, 16)
            sp.dma_start(cmp_t[:], bass.AP(tensor=scratch.tensor, offset=T - 31 - 16 * (CMP - 1),
                                           ap=[[16, CMP], [row, NSA_H], [1, T]])).then_inc(s_back, 16)

        @block.gpsimd
        def _(pool):
            nc.gpsimd.memset(flip[:], 0.0)
            pool.drain()
            nc.gpsimd.affine_select(out=flip[:], in_=flip[:], compare_op=ALU.not_equal, fill=1.0, base=1 - P,
                                    pattern=[[1, P]], channel_multiplier=1).then_inc(s_flip, 1)

        @block.tensor
        def _(pe):
            pe.wait_ge(s_in, 16 * 6)
            pe.wait_ge(s_rel, 1)
            for a in range(4):
                nc.tensor.matmul(K.ps[0:NH, a, :], rel[:], hot[:, a // 2, (a % 2) * T:(a % 2 + 1) * T],
                                 start=True, stop=True).then_inc(s_vec, 1)
            pe.wait_ge(s_back, 48)
            pe.wait_ge(s_flip, 1)
            for h in range(NSA_H):
                nc.tensor.matmul(K.ps[:, h, :], flip[:], K.bias_nsa[:, h, :], start=True, stop=True)\
                    .then_inc(s_turn, 1)
            for b in range(4):
                nc.tensor.matmul(K.ps[:, 4 + b, :], flip[:], K.bias_swa[:, 2 * b:2 * b + 2, :], start=True, stop=True)\
                    .then_inc(s_turn, 1)
            pe.wait_ge(s_cp, 5)
            for h in range(NSA_H):
                for i in range(TT):
                    o = (h * TT + i) * 32
                    last = nc.tensor.matmul(K.ps[:, 0, o:o + CMP], cmp_t[:, h, i * P:(i + 1) * P],
                                            flip[0:CMP, P - CMP:P], start=True, stop=True)
            last.then_inc(s_turn, 1)

        @block.vector
        def _(dve):
            v = nc.vector
            dve.wait_ge(s_in, 16 * 6)
            v.tensor_scalar(rel[0:32, :], rel[0:32, :], 8.0, None, ALU.mult).then_inc(s_rel, 1)
            v.tensor_scalar(K.sinks[:, 1, :, :], K.sinks[:, 0, :, :], 8.0, None, ALU.mult)
            for a in range(4):
                dve.wait_ge(s_vec, a + 1)
                v.tensor_copy(vecs[:, a // 2, (a % 2) * T:(a % 2 + 1) * T], K.ps[0:NH, a, :]).then_inc(s_cp, 1)
            for h in range(NSA_H):
                dve.wait_ge(s_turn, h + 1)
                v.tensor_copy(K.bias_nsa[:, h, :], K.ps[:, h, :]).then_inc(s_cp, 1)
            for b in range(4):
                dve.wait_ge(s_turn, NSA_H + b + 1)
                v.tensor_copy(K.bias_swa[:, 2 * b:2 * b + 2, :].rearrange("p h j -> p (h j)"), K.ps[:, 4 + b, :])
            dve.wait_ge(s_turn, NSA_H + 5)
            v.tensor_copy(K.bias_cmp[:, :, :, 0:CMP],
                          K.ps[:, 0, :].rearrange("p (h i c) -> p h i c", h=NSA_H, c=32)[:, :, :, 0:CMP])
            dve.drain()


LAYER_SLOTS = [[(0, 0, 256)], [(0, 256, 256)], [(0, 512, 128), (128, 1644, 128)], [(0, 652, 256)],
               [(0, 908, 128), (128, 1580, 64), (192, 1036, 32), (224, 1052, 16), (240, 1036, 16)],
               [(0, 640, 12)]] + [[(0, c, 256)] for c in (1068, 1324, 1708, 1964, 2220, 2476)]


def plan_layer(w):
    def plan(raw, c, u):
        parts = LAYER_SLOTS[2 * c + u]
        view = tiles(raw, DC, parts[-1][0] + parts[-1][2])
        return [(view[:, :, o:o + m], w[:, c:c + m].rearrange("(k p) n -> p k n", p=P)) for o, c, m in parts]
    return plan


def stage_layer_project(nc, K, dr, l, L, following):
    with ExitStack() as ctx:
        rot = ctx.enter_context(nc.sbuf_tensor(K.name("rotk"), [P, T], F32))
        kr = ctx.enter_context(nc.sbuf_tensor(K.name("kr"), [P, T], F32))
        block = ctx.enter_context(nc.Block())
        ring, h = K.ring, K.h
        ready, free = K.s("chunk_ready"), [K.s(f"bank_free{b}") for b in range(4)]
        chunks = [(0, 0, P, "q0"), (0, 128, P, "q1"), (1, 0, P, "kv_cmp"), (1, 128, P, "kv_slc"),
                  (2, 0, P, "kv_win"), (2, 128, P, "v_swa"), (3, 0, P, "cq0"), (3, 128, P, "cq1"),
                  (4, 0, P, "ckv"), (4, 128, P, "k_swa_rope"), (5, 0, 12, "gates")]
        chunks += [(6 + j // 2, j % 2 * P, P, f"qs{j}") for j in range(4)]
        chunks += [(8 + j // 2, j % 2 * P, P, f"z{j}") for j in range(8)]
        by_act = ("gates", "z")
        N = len(chunks)

        @block.sync
        def _(sp):
            ring.stream(sp, plan_layer(dr["w_in_2"][l]), len(LAYER_SLOTS), following, loop=False)

        @block.tensor
        def _(pe):
            at = -1
            for c, (s, o, m, what) in enumerate(chunks):
                if s != at:
                    if at >= 0:
                        pe.drain().then_inc(ring.used, 1)
                    at = s
                    w = [tiles(x, DC, LAYER_SLOTS[s][-1][0] + LAYER_SLOTS[s][-1][2]) for x in ring.use(pe, s)]
                if c >= 4:
                    pe.wait_ge(free[c % 4].handle, free[c % 4].at(c // 4))
                bank = K.ps[:, c % 4, :]
                if what == "gates":
                    for t in range(TT):
                        last = product3(nc, bank[:, 12 * t:12 * t + 12], lambda a, k: h[a][:, k, t * P:(t + 1) * P],
                                        lambda a, k: w[a][:, k, o:o + m], DC)
                else:
                    last = product3(nc, bank, lambda a, k: w[a][:, k, o:o + m], lambda a, k: h[a][:, k, :], DC)
                last.then_inc(ready.handle, 1)
            pe.drain().then_inc(ring.used, 1)

        @block.vector
        def _(dve):
            v = nc.vector
            copies = {"q0": L.qn[:, 0, :], "q1": L.qn[:, 1, :], "cq0": L.cq[:, 0, :], "cq1": L.cq[:, 1, :],
                      "ckv": L.cq[:, 2, :]} | {f"qs{j}": L.qs[:, j, :] for j in range(4)}
            for c, (slot, o, _, what) in enumerate(chunks):
                ends = c == N - 1 or chunks[c + 1][0] != slot
                if not what.startswith(by_act):
                    dve.wait_ge(ready.handle, ready.at(c + 1))
                if ends:
                    ring.split_low(dve, slot + 2)
                if what.startswith(by_act):
                    continue
                bank = K.ps[:, c % 4, :]
                if what in copies:
                    last = v.tensor_copy(copies[what], bank)
                elif what == "kv_cmp":
                    for i in range(2):
                        rows = slice(64 * i, 64 * i + 64)
                        for e in range(2):
                            for m0 in range(2):
                                src = bank[rows, :].rearrange("p (c s) -> p s c", s=16)[:, e:16:2, m0:m0 + CMP]
                                pe0 = (2 * l + i) * 32 + 16 * m0 + e
                                pos = K.peT[rows, pe0:pe0 + 15:2].unsqueeze(2).to_broadcast([64, 8, CMP])
                                last = v.tensor_tensor(L.blk[64 * e:64 * e + 64, i, 8 * m0:8 * m0 + 8, 0:CMP], src, pos,
                                                       ALU.add)
                elif what in ("kv_slc", "kv_win"):
                    k, vt = (L.k_slc, L.v_t[:, 0, :]) if what == "kv_slc" else (L.k_win, L.v_t[:, 1, :])
                    v.tensor_copy(k[0:64, :], bank[0:64, :])
                    v.tensor_copy(k[64:128, :], bank[0:64, :])
                    last = v.tensor_copy(vt[64:128, :], bank[64:128, :])
                elif what == "k_swa_rope":
                    v.tensor_copy(L.k_swa[0:64, :], bank[0:64, :])
                    v.tensor_copy(L.k_swa[64:128, :], bank[0:64, :])
                    v.tensor_tensor(rot[64:96, :], bank[96:128, :], K.rope_m[96:128, :], ALU.mult)
                    v.tensor_tensor(kr[64:96, :], bank[64:96, :], K.rope_m[64:96, :], ALU.mult)
                    dve.drain()
                    for h in range(MLA_H):
                        last = v.tensor_tensor(L.kf[64:96, h, :], kr[64:96, :], rot[64:96, :], ALU.add)
                elif what == "v_swa":
                    last = v.tensor_copy(L.v_t[0:64, 0, :], bank[0:64, :])
                last.then_inc(free[c % 4].handle, 1)
            dve.drain()

        @block.scalar
        def _(act):
            for c, (slot, o, _, what) in enumerate(chunks):
                if (c == N - 1 or chunks[c + 1][0] != slot) and not what.startswith(by_act):
                    ring.split_high(act, slot + 2)
                if not what.startswith(by_act):
                    continue
                act.wait_ge(ready.handle, ready.at(c + 1))
                bank = K.ps[:, c % 4, :]
                if what == "gates":
                    last = nc.scalar.activation(L.gates[:], bank[:, 0:12 * TT], ACT.Sigmoid)
                else:
                    last = nc.scalar.activation(L.sz[:, int(what[1:]), :], bank, ACT.Silu)
                last.then_inc(free[c % 4].handle, 1)
                if c == N - 1 or chunks[c + 1][0] != slot:
                    ring.split_high(act, slot + 2)

        ready.close(N)
        for b in range(4):
            free[b].close(len(range(b, N, 4)))
        ring.close(len(LAYER_SLOTS))


def stage_latents(nc, K, dr, l, L):
    with ExitStack() as ctx:
        def sb(name, shape):
            return ctx.enter_context(nc.sbuf_tensor(K.name(name), shape, F32))

        sq, rstd = sb("lsq", [P, 3, T]), sb("lrstd", [P, 2, T])
        hid = sb("hid", [P, 2, 32])
        rot, qr = sb("rotq", [P, T]), sb("qr", [P, T])
        wq, wkv = sb("wq", [P, 2, MLA_H, P]), sb("wkv", [P, MLA_H * P])
        wc1, wc2 = sb("wc1", [P, 2, 16, P]), sb("wc2", [P, 2, HD])
        block = ctx.enter_context(nc.Block())
        in_latent, in_cmp = K.s("latent_weights_in"), K.s("cmp_weights_in")
        ready, free = K.s("chunk_ready"), [K.s(f"bank_free{b}") for b in range(4)]
        squared, rooted, normed, hidden = K.s("squared"), K.s("rooted"), K.s("latents_normed"), K.s("hidden")
        w1, w2 = dr["cmp_w1_2"][l], dr["cmp_w2_2"][l]
        uq, ukv = dr["mla_w_uq_2"][l], dr["mla_w_ukv_2"][l]
        products = ["ss_q", "ss_kv", "v_slc", "v_win", "v_swa"] + [f"uq{h}" for h in range(4)]
        products += [f"uk{h}" for h in range(4)] + ["uv0", "uv1", "hid0", "hid1", "kc", "vc"]
        N = len(products)
        loads = {"latent": 0, "cmp": 0}

        @block.sync
        def _(sp):
            uq4 = uq.rearrange("(k p) (h c) -> p k h c", p=P, h=4)
            for k in range(2):
                for o, c, m in ((0, 0, 96), (96, 80, 16), (112, 64, 16)):
                    sp.dma_start(wq[:, k, :, o:o + m], uq4[:, k, :, c:c + m]).then_inc(in_latent.handle, 16)
                    loads["latent"] += 16
            sp.dma_start(wkv[:], ukv).then_inc(in_latent.handle, 16)
            loads["latent"] += 16
            for i in range(2):
                sp.dma_start(wc1[:, i, :, :], w1[i].rearrange("(m p) n -> p m n", p=P)).then_inc(in_cmp.handle, 16)
            sp.dma_start(wc2[:], w2.rearrange("i p d -> p i d")).then_inc(in_cmp.handle, 16)
            loads["cmp"] += 48

        @block.tensor
        def _(pe):
            t = nc.tensor
            for c, what in enumerate(products):
                if c >= 4:
                    pe.wait_ge(free[c % 4].handle, free[c % 4].at(c // 4))
                bank = K.ps[:, c % 4, :]
                if what == "ss_q":
                    pe.wait_ge(squared.handle, squared.at(2))
                    last = product(nc, bank, lambda k: K.ones[:], lambda k: sq[:, k, :], 2)
                elif what == "ss_kv":
                    pe.wait_ge(squared.handle, squared.at(3))
                    last = product(nc, bank, lambda k: K.ones[:], lambda k: sq[:, 2, :], 1)
                elif what.startswith("hid"):
                    i = int(what[3:])
                    pe.wait_ge(in_cmp.handle, in_cmp.at(loads["cmp"]))
                    last = product(nc, bank[:, 0:CMP], lambda m: wc1[:, i, m, :], lambda m: L.blk[:, i, m, 0:CMP], 16)
                elif what in ("v_slc", "v_win", "v_swa"):
                    i = ("v_slc", "v_win", "v_swa").index(what)
                    rows, half = (slice(64, 128), i) if i < 2 else (slice(0, 64), 0)
                    for b in range(TT):
                        last = t.matmul(bank[:, 64 * b:64 * b + 64], L.v_t[rows, half, b * P:(b + 1) * P],
                                        K.ident[rows, rows], start=True, stop=True)
                elif what == "kc":
                    pe.wait_ge(hidden.handle, hidden.at(2))
                    for half in range(2):
                        last = t.matmul(bank[64 * half:64 * half + 64, 0:CMP], wc2[:, 0, :], hid[:, 0, 0:CMP],
                                        start=True, stop=True)
                elif what == "vc":
                    last = t.matmul(bank[0:CMP, 0:64], hid[:, 1, 0:CMP], wc2[:, 1, :], start=True, stop=True)
                elif what.startswith("uq"):
                    pe.wait_ge(normed.handle, normed.at(2))
                    pe.wait_ge(in_latent.handle, in_latent.at(loads["latent"]))
                    last = product(nc, bank, lambda k: wq[:, k, int(what[2:]), :], lambda k: L.cq[:, k, :], 2)
                elif what.startswith("uk"):
                    h = int(what[2:])
                    pe.wait_ge(normed.handle, normed.at(3))
                    last = product(nc, bank[0:64, :], lambda k: wkv[:, h * P:h * P + 64], lambda k: L.cq[:, 2, :], 1)
                else:
                    values = wkv[:].rearrange("p (h c) -> p h c", h=4)[:, :, 64:128]
                    for b in range(2):
                        tile = 2 * int(what[2:]) + b
                        last = t.matmul(bank[:, 256 * b:256 * b + 256], L.cq[:, 2, tile * P:(tile + 1) * P], values,
                                        start=True, stop=True)
                last.then_inc(ready.handle, 1)

        @block.scalar
        def _(act):
            for i in range(3):
                nc.scalar.activation(sq[:, i, :], L.cq[:, i, :], ACT.Square).then_inc(squared.handle, 1)
            for c, what in enumerate(products):
                bank = K.ps[:, c % 4, :]
                if what.startswith("ss"):
                    act.wait_ge(ready.handle, ready.at(c + 1))
                    nc.scalar.activation(rstd[:, c, :], bank, ACT.Sqrt, bias=K.eps[:], scale=(1.0 / 256, 1.0 / 128)[c])\
                        .then_inc(rooted.handle, 1)
                    act.drain().then_inc(free[c % 4].handle, 1)
                elif what.startswith("hid"):
                    act.wait_ge(ready.handle, ready.at(c + 1))
                    nc.scalar.activation(hid[:, int(what[3:]), 0:CMP], bank[:, 0:CMP], ACT.Silu).then_inc(hidden.handle, 1)
                    act.drain().then_inc(free[c % 4].handle, 1)

        @block.vector
        def _(dve):
            v = nc.vector
            v.tensor_scalar(L.gates[:, 0:12:3], L.gates[:, 0:12:3], K.cols[:, 4:5], None, ALU.mult)
            dve.wait_ge(rooted.handle, rooted.at(2))
            v.reciprocal(rstd[:], rstd[:])
            dve.drain()
            for i in range(3):
                col = 64 + 2 * l + i if i < 2 else 68 + l
                v.scalar_tensor_tensor(out=L.cq[:, i, :], in0=L.cq[:, i, :], scalar=K.vec[:, col:col + 1],
                                       in1=rstd[:, i // 2, :], op0=ALU.mult, op1=ALU.mult).then_inc(normed.handle, 1)
            for c, what in enumerate(products):
                if what.startswith(("ss", "hid")):
                    continue
                dve.wait_ge(ready.handle, ready.at(c + 1))
                bank = K.ps[:, c % 4, :]
                if what in ("v_slc", "v_win", "v_swa"):
                    dst = (L.v_slc, L.v_win, L.v_swa)[c - 2]
                    last = v.tensor_copy(dst[:].rearrange("p b d -> p (b d)"), bank[:, 0:256])
                elif what == "kc":
                    last = v.tensor_copy(L.kc[:, 0:CMP], bank[:, 0:CMP])
                elif what == "vc":
                    last = v.tensor_copy(L.vc[0:CMP, :], bank[0:CMP, 0:64])
                elif what.startswith("uq"):
                    h = int(what[2:])
                    v.tensor_tensor(rot[64:96, :], bank[96:128, :], K.rope_m[96:128, :], ALU.mult)
                    v.tensor_tensor(qr[64:96, :], bank[64:96, :], K.rope_m[64:96, :], ALU.mult)
                    last = v.tensor_copy(L.qf[0:64, h, :], bank[0:64, :])
                elif what.startswith("uk"):
                    last = v.tensor_copy(L.kf[0:64, int(what[2:]), :], bank[0:64, :])
                else:
                    b = 2 * int(what[2:])
                    last = v.tensor_copy(L.v_mla[:, b:b + 2, :].rearrange("p b d -> p (b d)"), bank)
                last.then_inc(free[c % 4].handle, 1)
                if what.startswith("uq"):
                    dve.drain()
                    v.tensor_tensor(L.qf[64:96, h, :], qr[64:96, :], rot[64:96, :], ALU.add)
                    dve.drain()
            dve.drain()

        ready.close(N)
        squared.close(3)
        rooted.close(2)
        normed.close(3)
        hidden.close(2)
        in_latent.close(loads["latent"])
        in_cmp.close(loads["cmp"])
        for b in range(4):
            free[b].close(len(range(b, N, 4)))


def stage_load(nc, K, dst, src):
    with ExitStack() as ctx:
        block = ctx.enter_context(nc.Block())
        loaded = K.s("tensor_loaded")

        @block.sync
        def _(sp):
            sp.dma_start(dst[:], src).then_inc(loaded.handle, 16)
            sp.wait_ge(loaded.handle, loaded.at(16))

        loaded.close(16)


def stage_store(nc, K, out):
    with ExitStack() as ctx:
        o_tok = ctx.enter_context(nc.sbuf_tensor("o_tok", [P, TT, D], F32))
        s_tr, s_cp, s_out = (ctx.enter_context(nc.semaphore(x)) for x in ("out_turned", "out_copied", "out_stored"))
        block = ctx.enter_context(nc.Block())

        @block.tensor
        def _(pe):
            for n in range(2 * TT):
                if n >= 4:
                    pe.wait_ge(s_cp, n - 3)
                for c in range(4):
                    last = nc.tensor.transpose(K.ps[:, n % 4, c * P:(c + 1) * P],
                                               K.xT[:, 4 * (n % 2) + c, (n // 2) * P:(n // 2 + 1) * P], K.ident[:])
                last.then_inc(s_tr, 1)

        @block.vector
        def _(dve):
            for n in range(2 * TT):
                dve.wait_ge(s_tr, n + 1)
                nc.vector.tensor_copy(o_tok[:, n // 2, (n % 2) * T:(n % 2 + 1) * T], K.ps[:, n % 4, :]).then_inc(s_cp, 1)

        @block.sync
        def _(sp):
            for t in range(TT):
                sp.wait_ge(s_cp, 2 * t + 2)
                sp.dma_start(out[0, t * P:(t + 1) * P, :], o_tok[:, t, :]).then_inc(s_out, 16)
            sp.wait_ge(s_out, 16 * TT)



def diff_jobs(K, qk, v_tok, oT):
    for h in range(HEADS):
        for t in range(TT):
            w = P * (t + 1)
            for c in range(2):
                rows = slice(64 * c, 64 * c + 64)
                yield job([(0, qk[rows, h, t * P:(t + 1) * P], qk[rows, HEADS + h, 0:w])], w,
                          K.causal[:, T - w:T], A_DIM ** -0.5,
                          [(b * P, P, v_tok[:, b, h * P:(h + 1) * P]) for b in range(t + 1)],
                          oT[:, h, t * P:(t + 1) * P], first=c == 0, last=c == 1,
                          gate=K.neg_lam[:] if c else None)


def dilated_jobs(mask, qk, v_tok, oT, first_head):
    for h in range(2):
        for r in range(CLASSES):
            own = slice(r * P, (r + 1) * P)
            q = [qk[:, 2 * g + h, own] for g in range(3)]
            k = [qk[:, 6 + 2 * g + h, :] for g in range(3)]
            head = slice(h * P, (h + 1) * P)
            yield job([(0, q[0], k[0]), (T, q[1], k[1][:, own]), (T + P, q[2], k[2][:, own])], T + 2 * P,
                      mask[:, r, :], P ** -0.5,
                      [(b * P, P, v_tok[:, 0, b, head]) for b in range(CLASSES)]
                      + [((3 + g) * P, P, v_tok[:, g, r, head]) for g in (1, 2)],
                      oT[:, first_head + h, r:T:CLASSES])


def plan_a(dr):
    return column_plan(dr["w_in"][0], DC, 256)


def plan_b(dr, half):
    return [column_plan(dr["w_in"][0], DC, 256, 3 * T + first * T + 256 * half, T) for first in (0, 6)]


def plan_gate(dr):
    def plan(raw, c, u):
        view = tiles(raw, 16, P)
        if u == 0:
            parts = [(DC * b, DC, dr["w_in"][0], 8192 - 2 * D + b * D) for b in range(2)]
        else:
            parts = [(0, HEADS, dr["w_a_out"][0], 0), (HEADS, HEADS, dr["w_b_out"][0], 0)]
        return [(view[:, k0:k0 + kt, :], w[:, bass.ds((2 * c + u) * (P // 2) + c0 - u * (P // 2), P)].rearrange("(k p) n -> p k n", p=P))
                for k0, kt, w, c0 in parts]
    return plan


def plan_up(dr):
    def plan(raw, c, u):
        view = tiles(raw, 2 * DC, P)
        return [(view[:, DC * half:DC * (half + 1), :],
                 dr["w_up"][0][:, bass.ds(half * FF + (2 * c + u) * P, P)].rearrange("(k p) n -> p k n", p=P))
                for half in range(2)]
    return plan


def plan_down(dr):
    rows = FF // 2

    def plan(raw, c, u):
        src = dr["w_down"][0][u * rows:(u + 1) * rows, bass.ds(c * P, P)].rearrange("(k p) n -> p k n", p=P)
        return [(tiles(raw, rows // P, P), src)]
    return plan


def layer_jobs(K, L, l):
    for h in range(NSA_H):
        rows = slice(64 * (h % 2), 64 * (h % 2) + 64)
        for t in range(TT):
            w, own = P * (t + 1), slice(t * P, (t + 1) * P)
            q = L.qn[rows, h // 2, own]
            common = dict(out=L.sz[rows, h // 2, own], rows=(rows.start, 64), times=L.sz[rows, h // 2, own])
            gates = [L.gates[:, 12 * t + 3 * h + b:12 * t + 3 * h + b + 1] for b in range(3)]
            yield job([(0, q, L.kc[rows, 0:CMP])], CMP, K.bias_cmp[:, h, t, 0:CMP], HD ** -0.5,
                      [(0, CMP, L.vc[0:CMP, :])], first=True, last=False, gate=gates[0], turned=(CMP, P), **common)
            for b, (k, v) in enumerate([(L.k_slc, L.v_slc), (L.k_win, L.v_win)]):
                yield job([(0, q, k[rows, 0:w])], w, K.bias_nsa[:, h, T - w:T], HD ** -0.5,
                          [(i * P, P, v[:, i, :]) for i in range(t + 1)], first=False, last=b == 1,
                          gate=gates[1 + b], **common)
    for h in range(MLA_H):
        rows = slice(64 * (h % 2), 64 * (h % 2) + 64)
        for t in range(TT):
            w, own = P * (t + 1), slice(t * P, (t + 1) * P)
            yield job([(0, L.qf[0:96, h, own], L.kf[0:96, h, 0:w])], w, K.causal[:, T - w:T], 96 ** -0.5,
                      [(i * P, P, L.v_mla[:, i, 64 * h:64 * h + 64]) for i in range(t + 1)],
                      L.sz[rows, 2 + h // 2, own], rows=(rows.start, 64), times=L.sz[rows, 2 + h // 2, own])
    for h in range(SWA_H):
        rows = slice(64 * (h % 2), 64 * (h % 2) + 64)
        for t in range(TT):
            w = min(2, t + 1) * P
            lo, own = (t + 1) * P - w, slice(t * P, (t + 1) * P)
            yield job([(0, L.qs[rows, h // 2, own], L.k_swa[rows, lo:lo + w])], w, K.bias_swa[:, h, 2 * P - w:2 * P],
                      HD ** -0.5, [(i * P, P, L.v_swa[:, lo // P + i, :]) for i in range(w // P)],
                      L.sz[rows, 4 + h // 2, own], rows=(rows.start, 64), times=L.sz[rows, 4 + h // 2, own],
                      sink=(K.sinks[:, 1, l, h:h + 1], K.sinks[:, 0, l, h:h + 1]))


def build(nc, dr, out, stop=None, probes=None):
    with ExitStack() as ctx:
        K = Kit()

        def sb(name, shape, dt=F32, scope=ctx):
            return scope.enter_context(nc.sbuf_tensor(name, shape, dt))

        names, counted = {}, {}

        def name(n):
            names[n] = names.get(n, 0) + 1
            return f"{n}_{names[n]}"

        def s(n):
            if n not in counted:
                counted[n] = Counted(ctx.enter_context(nc.semaphore(n)))
            return counted[n]

        K.name, K.s = name, s
        K.ps = ctx.enter_context(nc.psum_tensor("ps", [P, 8, T], F32))
        K.ring = Ring(nc, sb("ring_raw", [P, 2, Ring.SIZE]), sb("ring_high", [P, 2, Ring.SIZE], F32R),
                      sb("ring_low", [P, 2, Ring.SIZE], F32R),
                      [ctx.enter_context(nc.semaphore(f"slot{i}_loaded")) for i in range(2)],
                      *[ctx.enter_context(nc.semaphore(x)) for x in ("slots_high", "slots_split", "slots_used")])
        K.xT = sb("xT", [P, DC, T])
        K.ident, K.ones, K.eps = sb("ident", [P, P]), sb("ones", [P, P]), sb("eps", [P, 1])
        K.cols, K.causal = sb("cols", [P, 8]), sb("causal", [P, T])
        K.vec, K.conv, K.peT = sb("vec", [P, NVEC]), sb("conv", [P, 4, 2 * FC]), sb("peT", [P, P])
        K.neg_lam = sb("neg_lam", [P, 1])

        def norm(first, scope):
            K.h = (sb(name("h_high"), [P, DC, T], F32R, scope), sb(name("h_low"), [P, DC, T], F32R, scope))
            stage_norm(nc, K, lambda c: K.vec[:, first + c:first + c + 1], *K.h)

        def probe(what, tensor):
            if probes is not None and what in probes:
                with ExitStack() as e:
                    sm = e.enter_context(nc.semaphore(name("probe")))
                    blk = e.enter_context(nc.Block())

                    @blk.sync
                    def _(sp):
                        sp.dma_start(probes[what], tensor).then_inc(sm, 16)
                        sp.wait_ge(sm, 16)

        def gains(first):
            return lambda c: K.vec[:, first + c:first + c + 1]

        plan_mix = column_plan(dr["w_mix_out"][0], DC, 256)
        with ExitStack() as tables:
            oa, ob = sb("oa", [P, HEADS, T], scope=tables), sb("ob", [P, HEADS, T], scope=tables)
            K.sin_b, K.cos_b = sb("sin_b", [P, T], scope=tables), sb("cos_b", [P, T], scope=tables)
            K.sin_a, K.cos_a = sb("sin_a", [P, T], scope=tables), sb("cos_a", [P, T], scope=tables)
            K.h = None
            stage_setup(nc, K, dr)
            norm(VECS["pre_mix_g"][0], tables)
            with ExitStack() as e:
                qk, v = sb("qk_a", [P, 2 * HEADS, T], scope=e), sb("v_a", [P, TT, T], scope=e)
                stage_project_a(nc, K, dr, qk, v, plan_b(dr, 0)[0])
                stage_attention(nc, K, list(diff_jobs(K, qk, v, oa)), T, 3, 3, 4)
            stage_head_norm(nc, K, oa, K.vec[:, 70:71])
            probe("oa", oa[:])
            for half in range(2):
                following = plan_b(dr, 1)[0] if half == 0 else plan_gate(dr)
                with ExitStack() as e:
                    qk, v = sb(name("qk_b"), [P, 12, T], scope=e), sb(name("v_b"), [P, 3, CLASSES, 256], scope=e)
                    stage_project_b(nc, K, qk, v, *plan_b(dr, half), following)
                    mask = sb(name("mask_b"), [P, CLASSES, 6 * P], scope=e)
                    stage_load(nc, K, mask, dr["c_mask_b"])
                    stage_attention(nc, K, list(dilated_jobs(mask, qk, v, ob, 2 * half)), 6 * P, 2, 1, 4)
            probe("ob", ob[:])
            mixed = sb("mixed", [P, DC, T], scope=tables)
            stage_gate_mix(nc, K, dr, oa, ob, mixed, plan_mix)
            probe("mixed", mixed[:])
            stage_out_project(nc, K, plan_mix, DC, 1, 2, mixed, None, gains(8), plan_up(dr))
            probe("x1", K.xT[:])
        with ExitStack() as e:
            hidden = (sb("ffn_high", [P, FC, T], F32R, e), sb("ffn_low", [P, FC, T], F32R, e))
            with ExitStack() as e2:
                norm(VECS["pre_ffn_g"][0], e2)
                stage_ffn_up(nc, K, *hidden, plan_up(dr), plan_down(dr))
            stage_out_project(nc, K, plan_down(dr), FC, 2, 1, None, hidden, gains(24), plan_layer(dr["w_in_2"][0]))
            probe("x2", K.xT[:])
        K.bias_nsa, K.bias_swa = sb("bias_nsa", [P, NSA_H, T]), sb("bias_swa", [P, SWA_H, 2 * P])
        K.bias_cmp, K.sinks = sb("bias_cmp", [P, NSA_H, TT, 32]), sb("sinks", [P, 2, LAYERS, SWA_H])
        K.rope_m = sb("rope_m", [P, T])
        stage_bias(nc, K, dr)
        for l in range(LAYERS):
            with ExitStack() as e:
                L = Kit()
                L.sz = sb(name("sz"), [P, DC, T], scope=e)
                plan_out = column_plan(dr["w_out_2"][l], DC, 256)
                with ExitStack() as inner:
                    L.qn = sb(name("qn"), [P, 2, T], scope=inner)
                    L.cq = sb(name("cq"), [P, 3, T], scope=inner)
                    L.blk = sb(name("blk"), [P, 2, 16, 32], scope=inner)
                    L.k_slc = sb(name("k_slc"), [P, T], scope=inner)
                    L.k_win = sb(name("k_win"), [P, T], scope=inner)
                    L.k_swa = sb(name("k_swa"), [P, T], scope=inner)
                    L.v_t = sb(name("v_t"), [P, 2, T], scope=inner)
                    L.kf = sb(name("kf"), [P, MLA_H, T], scope=inner)
                    L.qf = sb(name("qf"), [P, MLA_H, T], scope=inner)
                    L.qs = sb(name("qs"), [P, SWA_H // 2, T], scope=inner)
                    L.gates = sb(name("gates"), [P, 12 * TT], scope=inner)
                    L.kc = sb(name("kc"), [P, 32], scope=inner)
                    L.vc = sb(name("vc"), [32, HD], scope=inner)
                    L.v_slc = sb(name("v_slc"), [P, TT, HD], scope=inner)
                    L.v_win = sb(name("v_win"), [P, TT, HD], scope=inner)
                    L.v_swa = sb(name("v_swa"), [P, TT, HD], scope=inner)
                    L.v_mla = sb(name("v_mla"), [P, TT, MLA_H * HD], scope=inner)
                    with ExitStack() as e2:
                        norm(VECS["norm_pre_2"][0] + DC * l, e2)
                        stage_layer_project(nc, K, dr, l, L, plan_out)
                    stage_latents(nc, K, dr, l, L)
                    stage_attention(nc, K, list(layer_jobs(K, L, l)), T, 3, 3, 4)
                following = plan_layer(dr["w_in_2"][l + 1]) if l + 1 < LAYERS else None
                stage_out_project(nc, K, plan_out, DC, 1, 2, L.sz, None, gains(48 + DC * l), following)
                probe(f"y{l}", K.xT[:])
        stage_store(nc, K, out)


def kernel(**inputs):
    import concourse.bacc as bacc
    from concourse.bass_utils import run_bass_kernel_spmd

    nc = bacc.Bacc("TRN2", target_bir_lowering=False, num_devices=1)
    arrays = {k: np.ascontiguousarray(v) for k, v in inputs.items()}
    arrays |= shape_constants()
    dr = {k: nc.dram_tensor(f"{k}_dram", a.shape, mybir.dt.from_np(a.dtype), kind="ExternalInput").ap()
          for k, a in arrays.items()}
    dr["scratch"] = nc.dram_tensor("bias_scratch", (2, NSA_H + SWA_H, 2 * T), F32, kind="Internal").ap()
    out = nc.dram_tensor("out_dram", (1, T, D), F32, kind="ExternalOutput").ap()
    build(nc, dr, out)
    r = run_bass_kernel_spmd(nc, [{f"{k}_dram": a for k, a in arrays.items()}], core_ids=[0])
    return r.results[0]["out_dram"]
```

```python
import math
from contextlib import ExitStack

import numpy as np

import concourse.bass as bass
from concourse import mybir

F32 = mybir.dt.float32
F32R = mybir.dt.float32r
I32 = mybir.dt.int32
ALU = mybir.AluOpType
ACT = mybir.ActivationFunctionType
AX_X = mybir.AxisListType.X

P = 128
T = 512
TT = T // P
D = 1024
DC = D // P
EPS = 1e-6
NEG = -1e30
FF = 2816
FC = FF // P
HEADS = 4
CLASSES = 4
A_DIM = 64
LAM_INIT = 0.8 - 0.6 * math.exp(0.0)
LAYERS = 2
NSA_H, MLA_H, SWA_H = 4, 4, 8
HD = 64
CMP = T // 16 - 1
D_IN2 = 2732
THETA = 10000.0

VECS = {"pre_mix_g": (0, 8), "post_mix_g": (8, 8), "pre_ffn_g": (16, 8), "post_ffn_g": (24, 8),
        "norm_pre_2": (32, 16), "norm_post_2": (48, 16), "mla_q_norm_2": (64, 4), "mla_kv_norm_2": (68, 2),
        "diff_head_g": (70, 1)}
NVEC = 71


def shape_constants():
    f = np.float32
    p = np.arange(P)
    cols = np.zeros((P, 8), f)
    inv64 = f(THETA) ** (-np.arange(0, 64, 2, dtype=f) / f(64))
    inv128 = f(THETA) ** (-np.arange(0, 128, 2, dtype=f) / f(128))
    cols[:, 0] = inv64[p % 32]
    cols[:, 1] = inv128[p % 64]
    cols[:, 2] = np.where(p % 64 < 32, 1.0, -1.0)
    cols[:, 3] = np.where(p < 64, 1.0, -1.0)
    cols[:, 4] = p >= 31
    j = np.arange(T)
    causal = np.where(p[:, None] + (T - P) - j[None] >= 0, 0.0, NEG).astype(f)
    i = np.arange(P)
    mask_b = np.full((P, CLASSES, 6 * P), NEG, f)
    for r in range(CLASSES):
        for b in range(CLASSES):
            dist = CLASSES * (p[:, None] - i[None]) + r - b
            mask_b[:, r, b * P:(b + 1) * P] = np.where((dist >= 0) & (dist <= 128), 0.0, NEG)
        back = p[:, None] - i[None]
        mask_b[:, r, 4 * P:5 * P] = np.where(back >= 0, 0.0, NEG)
        mask_b[:, r, 5 * P:6 * P] = np.where((back >= 0) & (back % 4 == 0), 0.0, NEG)
    dist = np.arange(-T, T)
    d0 = np.maximum(dist, 0)
    large = 16 + (np.log(np.maximum(d0, 1).astype(f) / f(16)) / f(math.log(512 / 16)) * f(16)).astype(np.int32)
    bucket = np.where(d0 < 16, d0, np.minimum(large, 31))
    hot = np.zeros((34, 2 * T), f)
    hot[bucket, np.arange(2 * T)] = 1.0
    hot[32] = np.where(dist < 0, NEG, 0.0)
    hot[33] = np.where(dist >= 128, NEG, 0.0)
    back_hot = np.zeros_like(hot)
    back_hot[:, :2 * T - 1] = hot[:, 1:][:, ::-1]
    mask_rows = np.zeros((2, NSA_H + SWA_H), f)
    mask_rows[0] = 1.0
    mask_rows[1, NSA_H:] = 1.0
    inv32 = f(THETA) ** (-np.arange(16, dtype=f) / f(16))
    ang = np.arange(T, dtype=f)[None] * inv32[:, None]
    cos, sin = np.cos(ang), np.sin(ang)
    rope_m = np.concatenate([cos, cos, -sin, sin]).astype(f)
    return {"c_cols": cols, "c_causal": causal, "c_mask_b": mask_b, "c_hot": hot, "c_back_hot": back_hot,
            "c_mask_rows": mask_rows, "c_rope_m": rope_m}


class Counted:

    def __init__(self, handle):
        self.handle, self.base = handle, 0

    def at(self, n):
        return self.base + n

    def close(self, n):
        self.base += n


class Ring:

    SIZE = 2048

    def __init__(self, nc, raw, high, low, loaded, whole, split):
        self.nc, self.raw, self.high, self.low = nc, raw, high, low
        self.loaded = loaded
        self.whole = whole
        self.split = split
        self.base = 0
        self.total = [0, 0]
        self.seen, self.parts = [], []

    def load(self, sp, plan, k, it=None):
        n = len(self.seen)
        parts = plan(self.raw[:, n % 2, :], k // 2 + (0 if it is None else it), k % 2)
        if n >= 2:
            sp.wait_ge(self.split, n - 1 + (0 if it is None else 2 * it))
        for dst, src in parts:
            sp.dma_start(dst, src).then_inc(self.loaded[n % 2], 16)
        self.note(len(parts))

    def note(self, parts):
        self.total[len(self.seen) % 2] += 16 * parts
        self.seen.append(self.total[len(self.seen) % 2])
        self.parts.append(parts)

    def stream(self, sp, plan, slots, following, loop=True):
        if loop and slots > 2:
            with sp.Fori(0, slots // 2 - 1) as i:
                for u in range(2):
                    self.load(sp, plan, 2 + u, i)
            for _ in range(slots // 2 - 2):
                for _ in range(2):
                    self.note(self.parts[-2])
        elif slots > 2:
            for k in range(2, slots):
                self.load(sp, plan, k)
        if following is not None:
            for k in range(2):
                self.load(sp, following, k)

    def split_high(self, act, k, it=None):
        n = self.base + k
        if n >= len(self.seen):
            return
        s = n % 2
        act.wait_ge(self.loaded[s], self.seen[n] + (0 if it is None else 16 * self.parts[n] * it))
        self.nc.scalar.activation(self.high[:, s, :], self.raw[:, s, :], ACT.Copy).then_inc(self.whole, 1)

    def split_low(self, dve, k, it=None):
        n = self.base + k
        if n >= len(self.seen):
            return
        s = n % 2
        dve.wait_ge(self.whole, n + 1 + (0 if it is None else 2 * it))
        self.nc.vector.tensor_tensor(self.low[:, s, :], self.raw[:, s, :], self.high[:, s, :].bitcast(F32),
                                     ALU.subtract).then_inc(self.split, 1)

    def use(self, pe, k, it=None):
        n = self.base + k
        pe.wait_ge(self.split, n + 1 + (0 if it is None else 2 * it))
        return self.high[:, n % 2, :], self.low[:, n % 2, :]

    def close(self, slots):
        self.base += slots


def rounds_of(engine, rounds, body):
    if rounds > 1:
        with engine.Fori(0, rounds - 1) as i:
            for u in range(2):
                body(u, i)
    for u in range(2):
        body(2 * (rounds - 1) + u, None)


def index(k, it):
    return k if it is None else k + 2 * it


class Kit:
    pass


def tiles(flat, a, b):
    return flat[:, 0:a * b].rearrange("p (a b) -> p a b", b=b)


def column_plan(w, kt, width, first=0, step=None):
    step = step or width

    def plan(raw, c, u):
        src = w[:, bass.ds(first + (2 * c + u) * step, width)].rearrange("(k p) n -> p k n", p=P)
        return [(tiles(raw, kt, width), src)]
    return plan



def reduce_angle(ns, engine, K, col, quarter, ang, turns, part, red):
    TWO_PI = 2 * math.pi
    HI = 6.28125
    MID = float(np.float32(np.round((TWO_PI - HI) * 2 ** 21) / 2 ** 21))
    LO = TWO_PI - HI - MID
    MAGIC = 1.5 * 2 ** 23
    if not quarter:
        ns.tensor_scalar(ang[:], K.pos_f[:], K.cols[:, col:col + 1], None, ALU.mult)
        engine.drain()
    ns.tensor_scalar(turns[:], ang[:], 1 / TWO_PI, 0.25 * quarter, ALU.mult, ALU.add)
    engine.drain()
    ns.tensor_scalar(turns[:], turns[:], MAGIC, None, ALU.add)
    engine.drain()
    ns.tensor_scalar(turns[:], turns[:], MAGIC, None, ALU.subtract)
    engine.drain()
    for n, c in enumerate((HI, MID, LO)):
        src = red if n else ang
        if part is None:
            ns.scalar_tensor_tensor(out=red[:], in0=turns[:], scalar=-c, in1=src[:], op0=ALU.mult, op1=ALU.add)
        else:
            ns.tensor_scalar(part[:], turns[:], -c, None, ALU.mult)
            engine.drain()
            ns.tensor_tensor(red[:], src[:], part[:], ALU.add)
        engine.drain()
    if quarter:
        ns.tensor_scalar(red[:], red[:], math.pi / 2, None, ALU.add)
        engine.drain()
    return ns.tensor_scalar(red[:], red[:], 3.1415925, -3.1415925, ALU.min, ALU.max)


FROM_ONE = ("gated", "bank_free", "chunk_read", "banks_read", "ffn_done", "summed")


def stage_setup(nc, K, dr):
    with ExitStack() as ctx:
        def sb(name, shape, dt=F32):
            return ctx.enter_context(nc.sbuf_tensor(name, shape, dt))

        def sem(name):
            return ctx.enter_context(nc.semaphore(name))

        x_tok = sb("x_tok", [P, TT, D])
        vec_rows = sb("vec_rows", [NVEC, P])
        conv_rows = sb("conv_rows", [2 * FC, 4, P])
        pos_rows = sb("pos_rows", [P, P])
        pos_i = sb("pos_i", [P, T], I32)
        ang = sb("ang", [P, T])
        turns = sb("turns", [P, T])
        red = sb("red", [P, 2, T])
        sq = sb("x_sq", [P, 2, T])
        bias = BiasVectors(nc, K, dr, ctx)
        lam_in = sb("lam_in", [P, 4 * A_DIM])
        lam_prod = sb("lam_prod", [P, 2, A_DIM])
        lam_sum = sb("lam_sum", [P, 2])
        lam_exp = sb("lam_exp", [P, 2])
        s_x, s_in, s_ident, s_tr = sem("x_loaded"), sem("setup_loaded"), sem("ident_ready"), sem("setup_transposed")
        s_sq, s_sum, s_root = sem("x_squared"), sem("x_summed"), sem("x_rooted")
        s_free_v, s_free_a = sem("setup_bank_free_dve"), sem("setup_bank_free_act")
        s_red, s_sin, s_lsum, s_lexp = sem("angle_reduced"), sem("sin_done"), sem("lam_summed"), sem("lam_exped")
        block = ctx.enter_context(nc.Block())
        n_loads = 0

        @block.sync
        def _(sp):
            nonlocal n_loads

            def load(dst, src):
                nonlocal n_loads
                sp.dma_start(dst, src).then_inc(s_in, 16)
                n_loads += 1

            for t in range(TT):
                sp.dma_start(x_tok[:, t, :], dr["x"][0, t * P:(t + 1) * P, :]).then_inc(s_x, 16)
            load(pos_i[:], dr["positions"].partition_broadcast(P)[:, 0, :])
            load(K.cols[:], dr["c_cols"])
            for name, (r0, n) in VECS.items():
                load(vec_rows[r0:r0 + n, :], dr[name].rearrange("l (c p) -> (l c) p", p=P))
            load(conv_rows[:, 0:3, :], dr["conv_w"].rearrange("l j (c p) -> c (l j) p", p=P))
            load(conv_rows[:, 3, :], dr["conv_b"].rearrange("l (c p) -> (l c) p", p=P))
            for half in range(2):
                load(pos_rows[:, half * HD:(half + 1) * HD], dr["cmp_pos_2"].rearrange("l i s d -> (l i s) d"))
            load(lam_in[:], dr["diff_lambda"].rearrange("l a d -> l (a d)").partition_broadcast(P)[:, 0, :])
            load(K.causal[:], dr["c_causal"])
            bias.sync(sp)
            K.ring.stream(sp, None, 0, plan_a(dr), loop=False)
            bias.store(sp)

        @block.gpsimd
        def _(pool):
            nc.gpsimd.memset(K.ident[:], 0.0)
            nc.gpsimd.memset(K.ones[:], 1.0)
            nc.gpsimd.memset(K.eps[:], EPS)
            pool.drain()
            nc.gpsimd.affine_select(out=K.ident[:], in_=K.ident[:], compare_op=ALU.not_equal, fill=1.0, base=0,
                                    pattern=[[-1, P]], channel_multiplier=1).then_inc(s_ident, 1)

        N_TR = DC + 6

        @block.tensor
        def _(pe):
            pe.wait_ge(s_ident, 1)
            pe.wait_ge(s_x, 16 * TT)
            for n in range(N_TR):
                if n == DC:
                    pe.wait_ge(s_in, 16 * n_loads)
                if n >= 8:
                    pe.wait_ge((s_free_v, s_free_a)[n % 2], (n - 8) // 2 + 1)
                bank = K.ps[:, n % 8, :]
                if n < DC:
                    for t in range(TT):
                        last = nc.tensor.transpose(bank[:, t * P:(t + 1) * P], x_tok[:, t, n * P:(n + 1) * P], K.ident[:])
                elif n == DC:
                    last = nc.tensor.transpose(bank[:, 0:NVEC], vec_rows[:], K.ident[0:NVEC, 0:NVEC])
                elif n < DC + 5:
                    last = nc.tensor.transpose(bank[:, 0:2 * FC], conv_rows[:, n - DC - 1, :], K.ident[0:2 * FC, 0:2 * FC])
                else:
                    last = nc.tensor.transpose(bank[:, 0:P], pos_rows[:], K.ident[:])
                last.then_inc(s_tr, 1)
            pe.wait_ge(s_free_v, N_TR // 2)
            pe.wait_ge(s_free_a, N_TR // 2)
            for c in range(DC):
                pe.wait_ge(s_sq, c + 1)
                nc.tensor.matmul(K.ps[:, 7, :], K.ones[:], sq[:, c % 2, :], start=(c == 0), stop=(c == DC - 1))\
                    .then_inc(s_sum, 1)
            bias.pe(pe)

        def copy_of(n):
            bank = K.ps[:, n % 8, :]
            if n < DC:
                return K.xT[:, n, :], bank[:, 0:T]
            if n == DC:
                return K.vec[:], bank[:, 0:NVEC]
            if n < DC + 5:
                return K.conv[:, n - DC - 1, :], bank[:, 0:2 * FC]
            return K.peT[:], bank[:, 0:P]

        @block.vector
        def _(dve):
            v = nc.vector
            dve.wait_ge(s_x, 16 * TT)
            for n in range(0, DC, 2):
                dve.wait_ge(s_tr, n + 1)
                v.tensor_copy(*copy_of(n)).then_inc(s_free_v, 1)
            dve.wait_ge(s_in, 16 * n_loads)
            for n in range(DC, N_TR, 2):
                dve.wait_ge(s_tr, n + 1)
                v.tensor_copy(*copy_of(n)).then_inc(s_free_v, 1)
            bias.dve(dve)
            lam4 = lam_in[:].rearrange("p (a d) -> p a d", d=A_DIM)
            v.tensor_tensor(lam_prod[:], lam4[:, 0:4:2, :], lam4[:, 1:4:2, :], ALU.mult)
            v.tensor_copy(K.pos_f[:], pos_i[:])
            dve.drain()
            v.reduce_sum(lam_sum[:], lam_prod[:], AX_X).then_inc(s_lsum, 1)
            for quarter in range(2):
                reduce_angle(v, dve, K, 0, quarter, ang, turns, None, red[:, quarter, :]).then_inc(s_red, 1)
            dve.wait_ge(s_root, 1)
            v.reciprocal(K.rstd[:], K.rstd[:])
            dve.wait_ge(s_lexp, 1)
            v.tensor_scalar(K.neg_lam[:], lam_exp[:, 1:2], lam_exp[:, 0:1], -LAM_INIT, ALU.subtract, ALU.add)
            v.tensor_scalar(K.vec[:, 70:71], K.vec[:, 70:71], 1.0 - LAM_INIT, None, ALU.mult)
            dve.wait_ge(s_sin, 1)
            v.tensor_scalar(K.sin_a[:], K.sin_a[:], K.cols[:, 2:3], None, ALU.mult)
            for k in range(2):
                K.ring.split_low(dve, k)
            dve.drain()

        @block.scalar
        def _(act):
            for n in range(1, N_TR, 2):
                act.wait_ge(s_tr, n + 1)
                nc.scalar.activation(*copy_of(n), ACT.Copy).then_inc(s_free_a, 1)
            act.drain()
            for c in range(DC):
                if c % 2 == 0:
                    act.wait_ge(s_free_v, c // 2 + 1)
                if c >= 2:
                    act.wait_ge(s_sum, c - 1)
                nc.scalar.activation(sq[:, c % 2, :], K.xT[:, c, :], ACT.Square).then_inc(s_sq, 1)
            act.wait_ge(s_sum, DC)
            nc.scalar.activation(K.rstd[:], K.ps[:, 7, :], ACT.Sqrt, bias=K.eps[:], scale=1.0 / D).then_inc(s_root, 1)
            for k in range(2):
                K.ring.split_high(act, k)
            for quarter, table in enumerate((K.sin_a, K.cos_a)):
                act.wait_ge(s_red, quarter + 1)
                nc.scalar.activation(table[:], red[:, quarter, :], ACT.Sin).then_inc(s_sin, 1)
            bias.act(act)
            act.wait_ge(s_lsum, 1)
            nc.scalar.activation(lam_exp[:], lam_sum[:], ACT.Exp).then_inc(s_lexp, 1)
            for n in FROM_ONE:
                act.drain().then_inc(K.s(n).handle, 1)

        for n in FROM_ONE:
            K.s(n).close(1)


class Norm:

    def __init__(self, nc, K, scope, gain):
        self.nc, self.K, self.gain = nc, K, gain
        self.tmp = scope.enter_context(nc.sbuf_tensor(K.name("h_tmp"), [P, 2, T], F32))
        self.normed, self.whole, self.split = K.s("h_normed"), K.s("h_high"), K.s("h_low")

    def act(self, act):
        for c in range(DC):
            act.wait_ge(self.normed.handle, self.normed.at(c + 1))
            self.nc.scalar.activation(self.K.h[0][:, c, :], self.tmp[:, c % 2, :], ACT.Copy)\
                .then_inc(self.whole.handle, 1)

    def dve(self, dve):
        v, K = self.nc.vector, self.K

        def take_low(c):
            dve.wait_ge(self.whole.handle, self.whole.at(c + 1))
            v.tensor_tensor(K.h[1][:, c, :], self.tmp[:, c % 2, :], K.h[0][:, c, :].bitcast(F32), ALU.subtract)\
                .then_inc(self.split.handle, 1)
            dve.drain()

        for c in range(DC):
            if c >= 2:
                take_low(c - 2)
            v.scalar_tensor_tensor(out=self.tmp[:, c % 2, :], in0=K.xT[:, c, :], scalar=self.gain(c), in1=K.rstd[:],
                                   op0=ALU.mult, op1=ALU.mult).then_inc(self.normed.handle, 1)
        for c in range(DC - 2, DC):
            take_low(c)

    def wait(self, pe):
        return lambda k: pe.wait_ge(self.split.handle, self.split.at(k + 1))

    def close(self):
        for c in (self.normed, self.whole, self.split):
            c.close(DC)


class HeadNorm:

    def __init__(self, nc, K, scope, oT, gain):
        self.nc, self.K, self.oT, self.gain = nc, K, oT, gain
        self.sq = scope.enter_context(nc.sbuf_tensor("head_sq", [P, HEADS, T], F32))
        self.squared, self.summed, self.rooted = (scope.enter_context(nc.semaphore(x)) for x in
                                                  ("head_squared", "head_summed", "head_rooted"))

    def act(self, act):
        for h in range(HEADS):
            self.nc.scalar.activation(self.sq[:, h, :], self.oT[:, h, :], ACT.Square).then_inc(self.squared, 1)
        for h in range(HEADS):
            act.wait_ge(self.summed, h + 1)
            self.nc.scalar.activation(self.sq[:, h, :], self.K.ps[:, 4 + h, :], ACT.Sqrt, bias=self.K.eps[:],
                                      scale=1.0 / P).then_inc(self.rooted, 1)

    def pe(self, pe):
        for h in range(HEADS):
            pe.wait_ge(self.squared, h + 1)
            self.nc.tensor.matmul(self.K.ps[:, 4 + h, :], self.K.ones[:], self.sq[:, h, :], start=True, stop=True)\
                .then_inc(self.summed, 1)

    def dve(self, dve):
        for h in range(HEADS):
            dve.wait_ge(self.rooted, h + 1)
            self.nc.vector.reciprocal(self.sq[:, h, :], self.sq[:, h, :])
            dve.drain()
            self.nc.vector.scalar_tensor_tensor(out=self.oT[:, h, :], in0=self.oT[:, h, :], scalar=self.gain,
                                                in1=self.sq[:, h, :], op0=ALU.mult, op1=ALU.mult)


def product(nc, bank, w, src, kt):
    for k in range(kt):
        last = nc.tensor.matmul(bank, w(k), src(k), start=(k == 0), stop=(k == kt - 1))
    return last


def product3(nc, bank, stationary, moving, kt, start=True, stop=True, wait=None):
    for k in range(kt):
        if wait is not None:
            wait(k)
        for i, (a, b) in enumerate(((0, 0), (0, 1), (1, 0))):
            last = nc.tensor.matmul(bank, stationary(a, k), moving(b, k), start=start and k == 0 and i == 0,
                                    stop=stop and k == kt - 1 and i == 2)
    return last


def product3_pair(nc, banks, stationary, moving, kt, wait=None):
    for k in range(kt):
        if wait is not None:
            wait(k)
        last = []
        for j in range(2):
            for i, (a, b) in enumerate(((0, 0), (0, 1), (1, 0))):
                m = nc.tensor.matmul(banks[j], stationary(j, a, k), moving(b, k), start=k == 0 and i == 0,
                                     stop=k == kt - 1 and i == 2)
            last.append(m)
    return last


def stage_project_a(nc, K, dr, qk, v_tok, gain, mask, following):
    with ExitStack() as ctx:
        rot = ctx.enter_context(nc.sbuf_tensor(K.name("rot"), [P, 2, T], F32))
        work = [ctx.enter_context(nc.sbuf_tensor(K.name("angle"), [P, T], F32)) for _ in range(4)]
        norm = Norm(nc, K, ctx, gain)
        block = ctx.enter_context(nc.Block())
        s_mask, s_red, s_sin = K.s("mask_loaded"), K.s("angle_reduced"), K.s("sin_done")
        ring, h = K.ring, K.h
        ready, free = K.s("chunk_ready"), [K.s(f"bank_free{b}") for b in range(4)]
        QK = 2 * HEADS
        N = QK + 2 * TT

        @block.sync
        def _(sp):
            sp.dma_start(mask[:], dr["c_mask_b"]).then_inc(s_mask.handle, 16)
            ring.stream(sp, plan_a(dr), 6, following)
            sp.wait_ge(s_mask.handle, s_mask.at(16))

        @block.tensor
        def _(pe):
            w = [tiles(x, DC, 256) for x in ring.use(pe, 0)]
            for last in product3_pair(nc, [K.ps[:, j, :] for j in range(2)],
                                      lambda j, a, k: w[a][:, k, j * P:(j + 1) * P],
                                      lambda a, k: h[a][:, k, :], DC, norm.wait(pe)):
                last.then_inc(ready.handle, 1)
            c = 2
            for g in range(1, 6):
                w = [tiles(x, DC, 256) for x in ring.use(pe, g)]
                for j in range(2 if g < 4 else TT):
                    if c >= 4:
                        pe.wait_ge(free[c % 4].handle, free[c % 4].at(c // 4))
                    bank = K.ps[:, c % 4, :]
                    if g < 4:
                        last = product3(nc, bank, lambda a, k: w[a][:, k, j * P:(j + 1) * P],
                                        lambda a, k: h[a][:, k, :], DC)
                    else:
                        last = product3(nc, bank[:, 0:256], lambda a, k: h[a][:, k, j * P:(j + 1) * P],
                                        lambda a, k: w[a][:, k, :], DC)
                    last.then_inc(ready.handle, 1)
                    c += 1

        @block.gpsimd
        def _(pool):
            for quarter in range(2):
                if quarter:
                    pool.wait_ge(s_sin.handle, s_sin.at(1))
                reduce_angle(nc.gpsimd, pool, K, 1, quarter, *work).then_inc(s_red.handle, 1)
            pool.wait_ge(s_sin.handle, s_sin.at(2))
            nc.gpsimd.tensor_scalar(K.sin_b[:], K.sin_b[:], K.cols[:, 3:4], None, ALU.mult)
            pool.drain()

        @block.scalar
        def _(act):
            norm.act(act)
            for g in range(6):
                if g in (4, 5):
                    act.wait_ge(s_red.handle, s_red.at(g - 3))
                    nc.scalar.activation((K.sin_b, K.cos_b)[g - 4][:], work[3][:], ACT.Sin).then_inc(s_sin.handle, 1)
                act.wait_ge(ready.handle, ready.at(2 * g + 2 if g < 4 else 4 * g - 4))
                ring.split_high(act, g + 2)

        @block.vector
        def _(dve):
            v = nc.vector
            norm.dve(dve)
            for c in range(N):
                dve.wait_ge(ready.handle, ready.at(c + 1))
                if c < QK and c % 2 == 1 or c >= QK and c % 4 == 3:
                    ring.split_low(dve, (c // 2 if c < QK else 4 + (c - QK) // 4) + 2)
                bank = K.ps[:, c % 4, :]
                if c >= QK:
                    t, half = (c - QK) % 4, (c - QK) // 4
                    v.tensor_copy(v_tok[:, t, 256 * half:256 * half + 256], bank[:, 0:256])\
                        .then_inc(free[c % 4].handle, 1)
                    continue
                for q in range(4):
                    o = 32 * (q ^ 1)
                    v.tensor_tensor(rot[o:o + 32, c % 2, :], bank[32 * q:32 * q + 32, :],
                                    K.sin_a[32 * q:32 * q + 32, :], ALU.mult)
                v.tensor_tensor(qk[:, c, :], bank, K.cos_a[:], ALU.mult).then_inc(free[c % 4].handle, 1)
                dve.drain()
                v.tensor_tensor(qk[:, c, :], qk[:, c, :], rot[:, c % 2, :], ALU.add)
            dve.drain()

        ready.close(N)
        for b in range(4):
            free[b].close(N // 4)
        ring.close(6)
        norm.close()
        s_mask.close(16)
        s_red.close(2)
        s_sin.close(2)


def stage_project_b(nc, K, qk, v_tok, plan_qk, plan_v, following, heads=None):
    with ExitStack() as ctx:
        rot = ctx.enter_context(nc.sbuf_tensor(K.name("rotb"), [P, 2, T], F32))
        turned = ctx.enter_context(nc.sbuf_tensor(K.name("rope_tmp"), [P, 2, T], F32))
        head_norm = HeadNorm(nc, K, ctx, *heads) if heads else None
        block = ctx.enter_context(nc.Block())
        ring, h = K.ring, K.h
        ready, free = K.s("chunk_ready"), [K.s(f"bank_free{b}") for b in range(4)]

        @block.sync
        def _(sp):
            with sp.Fori(0, 2) as i:
                for u in range(2):
                    ring.load(sp, plan_qk, 2 + u, i)
            for _ in range(2):
                ring.note(1)
            for k in range(3):
                ring.load(sp, plan_v, k)
            if following is not None:
                for k in range(2):
                    ring.load(sp, following, k)

        @block.tensor
        def _(pe):
            if head_norm:
                head_norm.pe(pe)
            with pe.Fori(0, 3) as i:
                for u in range(2):
                    w = [tiles(x, DC, 256) for x in ring.use(pe, u, i)]
                    for j in range(2):
                        b = 2 * u + j
                        pe.wait_ge(free[b].handle, free[b].at(0) + i)
                        product3(nc, K.ps[:, b, :], lambda a, k: w[a][:, k, j * P:(j + 1) * P],
                                 lambda a, k: h[a][:, k, :], DC).then_inc(ready.handle, 1)
            for g in range(3):
                w = [tiles(x, DC, 256) for x in ring.use(pe, 6 + g)]
                for r in range(CLASSES):
                    pe.wait_ge(free[r].handle, free[r].at(3 + g))
                    product3(nc, K.ps[:, r, 0:256], lambda a, k: h[a][:, k, r:T:CLASSES],
                             lambda a, k: w[a][:, k, :], DC).then_inc(ready.handle, 1)

        @block.scalar
        def _(act):
            if head_norm:
                head_norm.act(act)
            with act.Fori(0, 3) as i:
                for u in range(2):
                    act.wait_ge(ready.handle, ready.at(2 * u + 2) + 4 * i)
                    ring.split_high(act, u + 2, i)
            for g in range(3):
                act.wait_ge(ready.handle, ready.at(12 + 4 * g + 4))
                ring.split_high(act, 6 + g + 2)

        @block.vector
        def _(dve):
            v = nc.vector
            if head_norm:
                head_norm.dve(dve)
            with dve.Fori(0, 3) as i:
                for u in range(2):
                    for j in range(2):
                        b = 2 * u + j
                        dve.wait_ge(ready.handle, ready.at(b + 1) + 4 * i)
                        if j == 1:
                            ring.split_low(dve, u + 2, i)
                        bank = K.ps[:, b, :]
                        for q in range(2):
                            o = 64 * (q ^ 1)
                            v.tensor_tensor(rot[o:o + 64, j, :], bank[64 * q:64 * q + 64, :],
                                            K.sin_b[64 * q:64 * q + 64, :], ALU.mult)
                        v.tensor_tensor(turned[:, j, :], bank, K.cos_b[:], ALU.mult).then_inc(free[b].handle, 1)
                        dve.drain()
                        v.tensor_tensor(qk[:, bass.ds(4 * i + b, 1), :].rearrange("p a (r i) -> p (a i) r", r=CLASSES),
                                        turned[:, j, :].rearrange("p (i r) -> p i r", r=CLASSES),
                                        rot[:, j, :].rearrange("p (i r) -> p i r", r=CLASSES), ALU.add)
            for g in range(3):
                for r in range(CLASSES):
                    dve.wait_ge(ready.handle, ready.at(12 + 4 * g + r + 1))
                    if r == CLASSES - 1:
                        ring.split_low(dve, 6 + g + 2)
                    v.tensor_copy(v_tok[:, g, r, :], K.ps[:, r, 0:256]).then_inc(free[r].handle, 1)
            dve.drain()

        ready.close(24)
        for b in range(4):
            free[b].close(6)
        ring.close(9)


def stage_attention(nc, K, jobs, width, n_s, n_t, look):
    with ExitStack() as ctx:
        def sb(name, shape):
            return ctx.enter_context(nc.sbuf_tensor(K.name(name), shape, F32))

        banks = -(-width // T)
        n_p = look + 2
        prob = sb("prob", [P, n_p, width])
        lag = 2
        n_c = lag + 1
        prob_t = sb("prob_t", [P, n_c, width])
        top = sb("top", [P, n_p])
        neg_top = sb("neg_top", [P, n_p])
        den = sb("den", [P, n_p])
        sink_exp = sb("sink_exp", [P, n_p])
        coef = sb("coef", [P, n_p])
        block = ctx.enter_context(nc.Block())
        n = len(jobs)
        by_dve = [j % 4 == 2 for j in range(n)]
        nth = [by_dve[:j + 1].count(by_dve[j]) for j in range(n)]
        flat = K.ps[:].rearrange("p b t -> p (b t)")

        def scores_at(j):
            o = (j % n_s) * banks * T
            return flat[:, o:o + width]

        def probs_t_at(j):
            o = (n_s + j % n_t) * banks * T
            return flat[:, o:o + width]

        o_bank = (n_s + n_t) * banks
        group, g = [], 0
        for job in jobs:
            group.append(g)
            g += job["last"]
        n_out = g

        def out_at(j):
            p0, m = jobs[j]["rows"]
            return K.ps[p0:p0 + m, o_bank + group[j] % 2, 0:P]

        scored, masked, topped = K.s("scored"), K.s("masked"), K.s("topped")
        exped, weighed, scaled = K.s("exped"), K.s("weighed"), [K.s("scaled_pool"), K.s("scaled_dve")]
        turned, copied, mixed, stored = K.s("turned"), K.s("copied"), K.s("mixed"), K.s("stored")

        @block.tensor
        def _(pe):
            def scores(j):
                if j >= n_s:
                    pe.wait_ge(masked.handle, masked.at(j - n_s + 1))
                for c0, q, k in jobs[j]["scores"]:
                    last = nc.tensor.matmul(scores_at(j)[:, c0:c0 + k.shape[-1]], q, k, start=True, stop=True)
                last.then_inc(scored.handle, 1)

            def turn(j):
                pe.wait_ge(scaled[by_dve[j]].handle, scaled[by_dve[j]].at(nth[j]))
                if j >= n_t:
                    pe.wait_ge(copied.handle, copied.at(j - n_t + 1))
                for c0, m, _ in jobs[j]["values"]:
                    src = prob[:, j % n_p, c0:c0 + m]
                    if m == P:
                        last = nc.tensor.transpose(probs_t_at(j)[:, c0:c0 + P], src, K.ident[:])
                    else:
                        last = nc.tensor.matmul(probs_t_at(j)[0:m, c0:c0 + P], src, K.ident[:], start=True, stop=True)
                last.then_inc(turned.handle, 1)

            def mix(j):
                pe.wait_ge(copied.handle, copied.at(j + 1))
                if jobs[j]["first"] and group[j] >= 2:
                    pe.wait_ge(stored.handle, stored.at(group[j] - 1))
                values = jobs[j]["values"]
                for i, (c0, m, v) in enumerate(values):
                    last = nc.tensor.matmul(out_at(j), v, prob_t[0:m, j % n_c, c0:c0 + P],
                                            start=jobs[j]["first"] and i == 0,
                                            stop=jobs[j]["last"] and i == len(values) - 1)
                last.then_inc(mixed.handle, 1)

            for s in range(n + look + lag):
                if s < n:
                    scores(s)
                if 0 <= s - look < n:
                    turn(s - look)
                if 0 <= s - look - lag < n:
                    mix(s - look - lag)

        @block.vector
        def _(dve):
            v = nc.vector

            def mask_and_top(j):
                job = jobs[j]
                b, w = j % n_p, job["width"]
                dve.wait_ge(scored.handle, scored.at(j + 1))
                if j >= n_p:
                    dve.wait_ge(turned.handle, turned.at(j - n_p + 1))
                v.tensor_tensor_reduce(out=prob[:, b, 0:w], in0=scores_at(j)[:, 0:w], in1=job["bias"], scale=1.0,
                                       scalar=-3e38, op0=ALU.add, op1=ALU.max, accum_out=top[:, b:b + 1])\
                    .then_inc(masked.handle, 1)
                dve.drain()
                if job["sink"] is None:
                    v.tensor_scalar(neg_top[:, b:b + 1], top[:, b:b + 1], -job["scale"], None, ALU.mult)\
                        .then_inc(topped.handle, 1)
                else:
                    v.tensor_scalar(neg_top[:, b:b + 1], top[:, b:b + 1], job["sink"][0], -job["scale"],
                                    ALU.max, ALU.mult).then_inc(topped.handle, 1)

            def weigh(j):
                job = jobs[j]
                b = j % n_p
                dve.wait_ge(exped.handle, exped.at(j + 1))
                d = den[:, b:b + 1]
                if job["sink"] is not None:
                    v.tensor_tensor(d, d, sink_exp[:, b:b + 1], ALU.add)
                    dve.drain()
                out = coef[:, b:b + 1]
                if job["gate"] is None:
                    last = v.reciprocal(out, d)
                else:
                    v.reciprocal(d, d)
                    dve.drain()
                    last = v.tensor_tensor(out, d, job["gate"], ALU.mult)
                if by_dve[j]:
                    dve.drain()
                    p = prob[:, b, 0:job["width"]]
                    v.tensor_scalar(p, p, out, None, ALU.mult).then_inc(scaled[1].handle, 1)
                else:
                    last.then_inc(weighed.handle, 1)

            def store(j):
                job = jobs[j]
                if not job["last"]:
                    return
                dve.wait_ge(mixed.handle, mixed.at(j + 1))
                if job["times"] is None:
                    v.tensor_copy(job["out"], out_at(j)).then_inc(stored.handle, 1)
                else:
                    v.tensor_tensor(job["out"], out_at(j), job["times"], ALU.mult).then_inc(stored.handle, 1)

            for s in range(n + look + lag + 1):
                if 0 <= s - look - lag - 1 < n:
                    store(s - look - lag - 1)
                if s < n:
                    mask_and_top(s)
                if 0 <= s - 1 < n:
                    weigh(s - 1)
            dve.drain()

        @block.scalar
        def _(act):
            a = nc.scalar

            def exp(j):
                job = jobs[j]
                b, w = j % n_p, job["width"]
                act.wait_ge(topped.handle, topped.at(j + 1))
                if job["sink"] is not None:
                    a.activation(sink_exp[:, b:b + 1], job["sink"][1], ACT.Exp, bias=neg_top[:, b:b + 1])
                a.activation(prob[:, b, 0:w], prob[:, b, 0:w], ACT.Exp, bias=neg_top[:, b:b + 1], scale=job["scale"],
                             accum_out=den[:, b:b + 1]).then_inc(exped.handle, 1)

            def copy(j):
                act.wait_ge(turned.handle, turned.at(j + 1))
                if j >= n_c:
                    act.wait_ge(mixed.handle, mixed.at(j - n_c + 1))
                rows, end = jobs[j]["turned"]
                a.activation(prob_t[0:rows, j % n_c, 0:end], probs_t_at(j)[0:rows, 0:end], ACT.Copy)\
                    .then_inc(copied.handle, 1)

            for s in range(n + look):
                if 0 <= s - look < n:
                    copy(s - look)
                if s < n:
                    exp(s)

        @block.gpsimd
        def _(pool):
            for j in range(n):
                if by_dve[j]:
                    continue
                b, w = j % n_p, jobs[j]["width"]
                pool.wait_ge(weighed.handle, weighed.at(nth[j]))
                nc.gpsimd.tensor_scalar(prob[:, b, 0:w], prob[:, b, 0:w], coef[:, b:b + 1], None, ALU.mult)\
                    .then_inc(scaled[0].handle, 1)

        for c in (scored, masked, topped, exped, turned, copied, mixed):
            c.close(n)
        weighed.close(by_dve.count(False))
        for i in range(2):
            scaled[i].close(by_dve.count(bool(i)))
        stored.close(n_out)


def job(scores, width, bias, scale, values, out, rows=(0, P), first=True, last=True, gate=None, sink=None,
        times=None, turned=None):
    return dict(scores=scores, width=width, bias=bias, scale=scale, values=values, out=out, rows=rows, first=first,
                last=last, gate=gate, sink=sink, times=times, turned=turned or (P, width))


def split_all(nc, K, act, dve, pairs, whole, split):
    for n, (src, high, low) in enumerate(pairs):
        if act is not None:
            nc.scalar.activation(high, src, ACT.Copy).then_inc(whole.handle, 1)
        else:
            dve.wait_ge(whole.handle, whole.at(n + 1))
            nc.vector.tensor_tensor(low, src, high.bitcast(F32), ALU.subtract).then_inc(split.handle, 1)


def stage_gate_mix(nc, K, dr, oa, ob, high, low, following):
    with ExitStack() as ctx:
        def sb(name, shape, dt=F32):
            return ctx.enter_context(nc.sbuf_tensor(K.name(name), shape, dt))

        sig, mixed = sb("sig", [P, 2, 2, T]), sb("mixed", [P, T])
        o_high, o_low = sb("o_high", [P, 2, HEADS, T], F32R), sb("o_low", [P, 2, HEADS, T], F32R)
        block = ctx.enter_context(nc.Block())
        ring, h = K.ring, K.h
        KA = HEADS
        ready, gated, free = K.s("chunk_ready"), K.s("gated"), K.s("bank_free")
        summed, whole, split = K.s("summed"), K.s("x_high"), K.s("x_low")
        pairs = [(src[:, c, :], o_high[:, i, c, :], o_low[:, i, c, :]) for i, src in enumerate((oa, ob))
                 for c in range(HEADS)]

        @block.sync
        def _(sp):
            with sp.Fori(0, DC - 1) as i:
                for u in range(2):
                    ring.load(sp, plan_gate(dr), 2 + u, i)
            for _ in range(2 * (DC - 2)):
                ring.note(2)
            for k in range(2):
                ring.load(sp, following, k)

        @block.tensor
        def _(pe):
            def chunk(i):
                gates = [tiles(x, 2 * DC, P) for x in ring.use(pe, 0, i)]
                pe.wait_ge(gated.handle, gated.at(0) + 2 * i)
                for b in range(2):
                    product3(nc, K.ps[:, b, :], lambda a, k: gates[a][:, DC * b + k, :],
                             lambda a, k: h[a][:, k, :], DC).then_inc(ready.handle, 1)
                outs = [tiles(x, 2 * KA, P) for x in ring.use(pe, 1, i)]
                pe.wait_ge(free.handle, free.at(0) + i)
                pe.wait_ge(split.handle, split.at(2 * HEADS))
                for b in range(2):
                    product3(nc, K.ps[:, 2 + b, :], lambda a, k: outs[a][:, KA * b + k, :],
                             lambda a, k: (o_high, o_low)[a][:, b, k, :], KA).then_inc(ready.handle, 1)

            with pe.Fori(0, DC) as i:
                chunk(i)

        def rounds(engine, body):
            with engine.Fori(0, DC - 1) as i:
                body(i, lambda k: (k, i))
            body(DC - 1, lambda k: (2 * (DC - 1) + k, None))

        @block.scalar
        def _(act):
            split_all(nc, K, act, None, pairs, whole, split)

            def chunk(i, slot):
                for b in range(2):
                    act.wait_ge(ready.handle, ready.at(b + 1) + 4 * i)
                    nc.scalar.activation(sig[:, 0, b, :], K.ps[:, b, :], ACT.Sigmoid).then_inc(gated.handle, 1)
                ring.split_high(act, *slot(2))
                act.wait_ge(ready.handle, ready.at(4) + 4 * i)
                ring.split_high(act, *slot(3))
                act.wait_ge(summed.handle, summed.at(1) + i)
                nc.scalar.activation(high[:, bass.ds(i, 1), :].rearrange("p a t -> p (a t)"), mixed[:], ACT.Copy)\
                    .then_inc(whole.handle, 1)

            rounds(act, chunk)

        @block.vector
        def _(dve):
            v = nc.vector
            split_all(nc, K, None, dve, pairs, whole, split)

            def chunk(i, slot):
                dve.wait_ge(gated.handle, gated.at(2) + 2 * i)
                ring.split_low(dve, *slot(2))
                for b in range(2):
                    dve.wait_ge(ready.handle, ready.at(3 + b) + 4 * i)
                    last = v.tensor_tensor(sig[:, 1, b, :], sig[:, 0, b, :], K.ps[:, 2 + b, :], ALU.mult)
                last.then_inc(free.handle, 1)
                dve.drain()
                v.tensor_tensor(mixed[:], sig[:, 1, 0, :], sig[:, 1, 1, :], ALU.add).then_inc(summed.handle, 1)
                ring.split_low(dve, *slot(3))
                dve.wait_ge(whole.handle, whole.at(2 * HEADS + 1) + i)
                at = (slice(None), bass.ds(i, 1), slice(None))
                v.tensor_tensor(low[at].rearrange("p a t -> p (a t)"), mixed[:],
                                high[at].bitcast(F32).rearrange("p a t -> p (a t)"), ALU.subtract)

            rounds(dve, chunk)
            dve.drain()

        ready.close(4 * DC)
        gated.close(2 * DC)
        free.close(DC)
        summed.close(DC)
        whole.close(2 * HEADS + DC)
        split.close(2 * HEADS)
        ring.close(2 * DC)


def token_sums(nc, sums, sources, ones, start=True, stop=True):
    for t in range(TT):
        for n, src in enumerate(sources):
            last = nc.tensor.matmul(sums[t], src[:, t * P:(t + 1) * P], ones[:, 0:1], start=start and n == 0,
                                    stop=stop and n == len(sources) - 1)
    return last


class Factor:

    def __init__(self, nc, K, scope):
        self.nc, self.K = nc, K
        self.value = scope.enter_context(nc.sbuf_tensor(K.name("factor"), [P, TT, 1], F32))
        self.diag = scope.enter_context(nc.sbuf_tensor(K.name("diag"), [P, TT, P], F32))
        self.bank = K.ps[:, 7, :]
        self.rooted, self.ready, self.done = K.s("rooted"), K.s("diagonals_ready"), K.s("factor_spread")

    def root(self, act, n):
        self.nc.scalar.activation(self.value[:], self.K.ps[:, 0:TT, 0:1], ACT.Sqrt, bias=self.K.eps[:], scale=1.0 / n)\
            .then_inc(self.rooted.handle, 1)

    def invert(self, dve, n):
        v = self.nc.vector
        dve.wait_ge(self.rooted.handle, self.rooted.at(n + 1))
        v.reciprocal(self.value[:], self.value[:])
        dve.drain()
        for t in range(TT):
            v.tensor_scalar(self.diag[:, t, :], self.K.ident[:], self.value[:, t, :], None, ALU.mult)\
                .then_inc(self.ready.handle, 1)

    def spread(self, pe, n):
        for t in range(TT):
            pe.wait_ge(self.ready.handle, self.ready.at(TT * n + t + 1))
            last = self.nc.tensor.matmul(self.bank[:, t * P:(t + 1) * P], self.K.ones[:], self.diag[:, t, :],
                                         start=True, stop=True)
        last.then_inc(self.done.handle, 1)

    def wait(self, engine, n):
        engine.wait_ge(self.done.handle, self.done.at(n + 1))

    def close(self, n):
        self.rooted.close(n)
        self.ready.close(TT * n)
        self.done.close(n)


def stage_out_project(nc, K, plan, kt, halves, per_slot, src, parts, gain, following, out=None):
    with ExitStack() as ctx:
        def sb(name, shape, dt=F32):
            return ctx.enter_context(nc.sbuf_tensor(K.name(name), shape, dt))

        yT = sb("yT", [P, DC, T])
        sq, total = sb("sq", [P, 2, T]), sb("total", [P, T])
        if not following:
            o_tok = sb("o_tok", [P, TT, D])
            turned, copied, stored = (ctx.enter_context(nc.semaphore(n)) for n in ("out_turned", "out_copied", "out_stored"))
        x = parts or (sb("x_high", [P, kt, T], F32R), sb("x_low", [P, kt, T], F32R))
        block = ctx.enter_context(nc.Block())
        ring = K.ring
        ready, read, squared, summed = K.s("chunk_ready"), K.s("chunk_read"), K.s("squared"), K.s("summed")
        totaled, stat_ready, scaled, root_next = K.s("totaled"), K.s("stat_ready"), K.s("y_scaled"), K.s("root_next")
        whole, split, half_ready = K.s("x_high"), K.s("x_low"), K.s("half_ready")
        added = K.s("added_dve"), K.s("added_pool")
        slots = DC * halves // per_slot
        rounds, body = slots // 2, 2 * per_slot // halves
        sums = [K.ps[:, t, 0:1] for t in range(TT)]
        factor = Factor(nc, K, ctx)
        pairs = [] if parts else [(src[:, k, :], x[0][:, k, :], x[1][:, k, :]) for k in range(kt)]

        @block.sync
        def _(sp):
            ring.stream(sp, plan, slots, following)
            if not following:
                rows = out[0].rearrange("(t p) d -> p t d", p=P)
                for half in range(2):
                    cols = slice(half * T, (half + 1) * T)
                    sp.wait_ge(copied, 4 * half + 4)
                    sp.dma_start(rows[:, :, cols], o_tok[:, :, cols]).then_inc(stored, 16)
                sp.wait_ge(stored, 32)

        @block.tensor
        def _(pe):
            kh = kt // halves
            split_k = (lambda k: pe.wait_ge(split.handle, split.at(k + 1))) if pairs else None
            if halves == 1:
                with pe.Fori(0, rounds) as i:
                    for u in range(2):
                        w = [tiles(t, kt, per_slot * P) for t in ring.use(pe, u, i)]
                        for j in range(2):
                            pe.wait_ge(read.handle, read.at(2 * u + j) + body * i)
                        for last in product3_pair(nc, [K.ps[:, 2 * u + j, :] for j in range(2)],
                                                  lambda j, a, k: w[a][:, k, j * P:(j + 1) * P],
                                                  lambda a, k: x[a][:, k, :], kt, None if u else split_k):
                            last.then_inc(ready.handle, 1)
            else:
                with pe.Fori(0, rounds // 2) as i:
                    for c in range(2):
                        pe.wait_ge(read.handle, read.at(c) + 2 * i)
                        for u in range(2):
                            n = 2 * c + u
                            pe.wait_ge(ring.split, ring.base + n + 1 + 4 * i)
                            w = [tiles(t[:, (ring.base + u) % 2, :], kh, P) for t in (ring.high, ring.low)]
                            product3(nc, K.ps[:, c, :], lambda a, k: w[a][:, k, :], lambda a, k: x[a][:, kh * u + k, :],
                                     kh, u == 0, u == 1).then_inc((half_ready, ready)[u].handle, 1)
            pe.wait_ge(totaled.handle, totaled.at(DC - 1))
            pe.wait_ge(squared.handle, squared.at(DC))
            token_sums(nc, sums, [total[:], sq[:, (DC - 1) % 2, :]], K.ones).then_inc(stat_ready.handle, 1)
            factor.spread(pe, 0)
            if following:
                for c in range(DC):
                    pe.wait_ge(squared.handle, squared.at(DC + c + 1))
                    nc.tensor.matmul(K.ps[:, 6, :], K.ones[:], sq[:, c % 2, :], start=(c == 0), stop=(c == DC - 1))\
                        .then_inc(stat_ready.handle, 1)
            else:
                for c in range(DC):
                    pe.wait_ge(added[c % 2].handle, added[c % 2].at(c // 2 + 1))
                    if c >= 4:
                        pe.wait_ge(copied, c - 3)
                    for t in range(TT):
                        last = nc.tensor.transpose(K.ps[:, c % 4, t * P:(t + 1) * P], K.xT[:, c, t * P:(t + 1) * P],
                                                   K.ident[:])
                    last.then_inc(turned, 1)

        per = 4 if halves == 1 else 2

        def each(engine, turn):
            n, step = DC // per, per * halves // per_slot
            with engine.Fori(0, n - 1) as i:
                turn(i, lambda k: (k, i * (step // 2)))
            turn(n - 1, lambda k: (step * (n - 1) + k, None))

        @block.scalar
        def _(act):
            split_all(nc, K, act, None, pairs, whole, split)
            for _ in range(per - 1):
                act.drain().then_inc(read.handle, 1)

            def take(q, i):
                act.wait_ge(ready.handle, ready.at(q + 1) + per * i)
                bank = K.ps[:, q, :]
                nc.scalar.activation(yT[:, bass.ds(per * i + q, 1), :].rearrange("p a t -> p (a t)"), bank, ACT.Copy)
                act.wait_ge(summed.handle, summed.at(q) + per * i)
                nc.scalar.activation(sq[:, q % 2, :], bank, ACT.Square).then_inc(squared.handle, 1)
                act.drain().then_inc(read.handle, 1)

            def turn(i, slot):
                if halves == 1:
                    for u in range(2):
                        for j in range(2):
                            take(2 * u + j, i)
                        ring.split_high(act, *slot(u + 2))
                else:
                    for c in range(2):
                        act.wait_ge(half_ready.handle, half_ready.at(c + 1) + 2 * i)
                        ring.split_high(act, *slot(2 * c + 2))
                        take(c, i)
                        ring.split_high(act, *slot(2 * c + 3))

            each(act, turn)
            act.wait_ge(stat_ready.handle, stat_ready.at(1))
            factor.root(act, D)
            if following:
                for c in range(DC):
                    act.wait_ge(added[c % 2].handle, added[c % 2].at(c // 2 + 1))
                    if c >= 2:
                        act.wait_ge(stat_ready.handle, stat_ready.at(c))
                    nc.scalar.activation(sq[:, c % 2, :], K.xT[:, c, :], ACT.Square).then_inc(squared.handle, 1)
                act.wait_ge(stat_ready.handle, stat_ready.at(1 + DC))
                nc.scalar.activation(K.rstd[:], K.ps[:, 6, :], ACT.Sqrt, bias=K.eps[:], scale=1.0 / D)\
                    .then_inc(root_next.handle, 1)
            else:
                for c in range(DC):
                    act.wait_ge(turned, c + 1)
                    nc.scalar.activation(o_tok[:, :, c * P:(c + 1) * P], K.ps[:, c % 4, :].rearrange("p (t q) -> p t q", q=P),
                                         ACT.Copy).then_inc(copied, 1)

        @block.gpsimd
        def _(pool):
            nc.gpsimd.memset(total[:], 0.0)
            pool.drain().then_inc(summed.handle, 1)

            def add(q, i):
                pool.wait_ge(squared.handle, squared.at(q + 1) + 2 * i)
                nc.gpsimd.tensor_tensor(total[:], total[:], sq[:, q, :], ALU.add).then_inc(summed.handle, 1)
                pool.drain().then_inc(totaled.handle, 1)

            with pool.Fori(0, DC // 2 - 1) as i:
                for q in range(2):
                    add(q, i)
            add(0, DC // 2 - 1)
            for c in range(1, DC, 2):
                pool.wait_ge(scaled.handle, scaled.at(c))
                nc.gpsimd.tensor_tensor(K.xT[:, c, :], K.xT[:, c, :], yT[:, c, :], ALU.add).then_inc(added[1].handle, 1)
            pool.drain()

        @block.vector
        def _(dve):
            split_all(nc, K, None, dve, pairs, whole, split)

            def turn(i, slot):
                for k in range(per * halves // per_slot):
                    ring.split_low(dve, *slot(k + 2))

            each(dve, turn)
            factor.invert(dve, 0)
            factor.wait(dve, 0)
            for c in range(0, DC, 2):
                for b in (c + 1, c):
                    nc.vector.scalar_tensor_tensor(out=yT[:, b, :], in0=yT[:, b, :], scalar=gain(b), in1=factor.bank,
                                                   op0=ALU.mult, op1=ALU.mult).then_inc(scaled.handle, 1)
                dve.drain()
                nc.vector.tensor_tensor(K.xT[:, c, :], K.xT[:, c, :], yT[:, c, :], ALU.add).then_inc(added[0].handle, 1)
            if following:
                dve.wait_ge(root_next.handle, root_next.at(1))
                nc.vector.reciprocal(K.rstd[:], K.rstd[:])
            dve.drain()

        ready.close(DC)
        read.close(DC + per - 1)
        again = 1 if following else 0
        squared.close(DC * (1 + again))
        summed.close(DC)
        totaled.close(DC - 1)
        stat_ready.close(1 + DC * again)
        factor.close(1)
        root_next.close(again)
        scaled.close(DC)
        half_ready.close(DC if halves == 2 else 0)
        for a in added:
            a.close(DC // 2)
        whole.close(len(pairs))
        split.close(len(pairs))
        ring.close(slots)


def stage_ffn_up(nc, K, high, low, gain, plan, following):
    with ExitStack() as ctx:
        def sb(name, shape):
            return ctx.enter_context(nc.sbuf_tensor(K.name(name), shape, F32))

        taps = sb("taps", [P, 2, 4, 2])
        u_sb = sb("u_sb", [P, 2, 2, T])
        norm = Norm(nc, K, ctx, gain)
        block = ctx.enter_context(nc.Block())
        ring, h = K.ring, K.h
        ready, free, tapped = K.s("chunk_ready"), K.s("banks_read"), K.s("taps_ready")
        biased, conved, gelued, done = K.s("biased"), K.s("conved"), K.s("gelued"), K.s("ffn_done")
        multiplied, whole = K.s("multiplied"), K.s("x_high")

        @block.sync
        def _(sp):
            ring.stream(sp, plan, FC, following)

        @block.tensor
        def _(pe):
            with pe.Fori(0, FC // 2) as i:
                for u in range(2):
                    w = [tiles(x, 2 * DC, P) for x in ring.use(pe, u, i)]
                    pe.wait_ge(free.handle, free.at(u) + 2 * i)
                    for last in product3_pair(nc, [K.ps[:, 2 * u + half, :] for half in range(2)],
                                              lambda half, a, k: w[a][:, DC * half + k, :],
                                              lambda a, k: h[a][:, k, :], DC, None if u else norm.wait(pe)):
                        last.then_inc(ready.handle, 1)

        @block.gpsimd
        def _(pool):
            conv = K.conv[:].rearrange("p j (h c) -> p j h c", h=2)
            with pool.Fori(0, FC // 2) as i:
                for u in range(2):
                    pool.wait_ge(done.handle, done.at(u) + 2 * i)
                    nc.gpsimd.tensor_copy(taps[:, u, :, :].unsqueeze(3), conv[:, :, :, bass.ds(2 * i + u, 1)])\
                        .then_inc(tapped.handle, 1)

        @block.scalar
        def _(act):
            def chunk(k, it):
                u, n = k % 2, index(k, it)
                act.wait_ge(tapped.handle, tapped.at(1) + n)
                act.wait_ge(done.handle, done.at(0) + n)
                for half in range(2):
                    act.wait_ge(ready.handle, ready.at(half + 1) + 2 * n)
                    nc.scalar.activation(u_sb[:, u, half, :], K.ps[:, 2 * u + half, :], ACT.Identity,
                                         bias=taps[:, u, 3, half:half + 1], scale=taps[:, u, 2, half:half + 1])\
                        .then_inc(biased.handle, 1)
                ring.split_high(act, k + 2, it)
                act.wait_ge(conved.handle, conved.at(1) + n)
                nc.scalar.activation(u_sb[:, u, 0, :], u_sb[:, u, 0, :], ACT.Gelu_apprx_tanh)\
                    .then_inc(gelued.handle, 1)
                act.wait_ge(multiplied.handle, multiplied.at(1) + n)
                nc.scalar.activation(high[:, bass.ds(n, 1), :].rearrange("p a t -> p (a t)"), u_sb[:, u, 0, :],
                                     ACT.Copy).then_inc(whole.handle, 1)

            norm.act(act)
            rounds_of(act, FC // 2, chunk)

        @block.vector
        def _(dve):
            v = nc.vector
            dve.drain().then_inc(free.handle, 1)
            dve.drain().then_inc(done.handle, 1)

            def chunk(k, it):
                u, n = k % 2, index(k, it)
                for half in range(2):
                    dve.wait_ge(biased.handle, biased.at(half + 1) + 2 * n)
                    for back in (1, 2):
                        out = u_sb[:, u, half, back:T]
                        last = v.scalar_tensor_tensor(out=out, in0=K.ps[:, 2 * u + half, 0:T - back],
                                                      scalar=taps[:, u, 2 - back, half:half + 1], in1=out,
                                                      op0=ALU.mult, op1=ALU.add)
                        if back == 1:
                            dve.drain()
                        elif half == 0:
                            last.then_inc(conved.handle, 1)
                        else:
                            last.then_inc(free.handle, 1)
                dve.drain()
                ring.split_low(dve, k + 2, it)
                dve.wait_ge(gelued.handle, gelued.at(1) + n)
                v.tensor_tensor(u_sb[:, u, 0, :], u_sb[:, u, 0, :], u_sb[:, u, 1, :], ALU.mult)\
                    .then_inc(multiplied.handle, 1)
                dve.wait_ge(whole.handle, whole.at(1) + n)
                v.tensor_tensor(low[:, bass.ds(n, 1), :].rearrange("p a t -> p (a t)"), u_sb[:, u, 0, :],
                                high[:, bass.ds(n, 1), :].rearrange("p a t -> p (a t)").bitcast(F32),
                                ALU.subtract).then_inc(done.handle, 1)

            norm.dve(dve)
            rounds_of(dve, FC // 2, chunk)
            dve.drain()

        ready.close(2 * FC)
        free.close(FC + 1)
        tapped.close(FC)
        biased.close(2 * FC)
        conved.close(FC)
        gelued.close(FC)
        multiplied.close(FC)
        whole.close(FC)
        done.close(FC + 1)
        norm.close()
        ring.close(FC)


class BiasVectors:

    def __init__(self, nc, K, dr, scope):
        def sb(name, shape):
            return scope.enter_context(nc.sbuf_tensor(name, shape, F32))

        self.nc, self.K, self.dr = nc, K, dr
        self.rel, self.hot = sb("rel", [34, NSA_H + SWA_H]), sb("hot", [34, 2, 2 * T])
        self.vecs = sb("bias_vecs", [NSA_H + SWA_H, 2, 2 * T])
        self.loaded, self.scaled, self.ready, self.copied, self.stored = (
            scope.enter_context(nc.semaphore(x)) for x in
            ("bias_in", "rel_scaled", "bias_by_distance", "bias_copied", "bias_in_dram"))

    def sync(self, sp):
        rel, dr = self.rel, self.dr
        sp.dma_start(rel[0:32, :], dr["rel_bias_2"].rearrange("h b -> b h"), allow_slow_non_contiguous=True)\
            .then_inc(self.loaded, 16)
        sp.dma_start(rel[32:34, :], dr["c_mask_rows"]).then_inc(self.loaded, 16)
        sp.dma_start(self.hot[:, 0, :], dr["c_hot"]).then_inc(self.loaded, 16)
        sp.dma_start(self.hot[:, 1, :], dr["c_back_hot"]).then_inc(self.loaded, 16)

    def store(self, sp):
        sp.wait_ge(self.copied, 4)
        sp.dma_start(self.dr["scratch"].rearrange("a h m -> h a m"), self.vecs[:]).then_inc(self.stored, 16)
        sp.wait_ge(self.stored, 16)

    def pe(self, pe):
        pe.wait_ge(self.scaled, 1)
        for a in range(4):
            self.nc.tensor.matmul(self.K.ps[0:NSA_H + SWA_H, a, :], self.rel[:],
                                  self.hot[:, a // 2, (a % 2) * T:(a % 2 + 1) * T], start=True, stop=True)\
                .then_inc(self.ready, 1)

    def dve(self, dve):
        dve.wait_ge(self.loaded, 16 * 4)
        self.nc.vector.tensor_scalar(self.rel[0:32, :], self.rel[0:32, :], 8.0, None, ALU.mult).then_inc(self.scaled, 1)

    def act(self, act):
        for a in range(4):
            act.wait_ge(self.ready, a + 1)
            self.nc.scalar.activation(self.vecs[:, a // 2, (a % 2) * T:(a % 2 + 1) * T],
                                      self.K.ps[0:NSA_H + SWA_H, a, :], ACT.Copy).then_inc(self.copied, 1)


class BiasTiles:

    def __init__(self, nc, K, dr, scope, room):
        self.nc, self.K, self.dr, self.cmp_t = nc, K, dr, room
        self.flip = scope.enter_context(nc.sbuf_tensor("flip", [P, P], F32))
        self.loaded, self.flipper, self.turned, self.copied = (
            scope.enter_context(nc.semaphore(x)) for x in
            ("bias_tiles_loaded", "flip_ready", "bias_turned", "bias_tiles_copied"))

    def sync(self, sp):
        K, dr, row = self.K, self.dr, 2 * T
        scratch, back = dr["scratch"], (NSA_H + SWA_H) * 2 * T
        sp.dma_start(K.bias_nsa[:], bass.AP(tensor=scratch.tensor, offset=back,
                                            ap=[[1, P], [row, NSA_H], [1, T]])).then_inc(self.loaded, 16)
        sp.dma_start(K.bias_swa[:], bass.AP(tensor=scratch.tensor, offset=back + NSA_H * row + T - 2 * P,
                                            ap=[[1, P], [row, SWA_H], [1, 2 * P]])).then_inc(self.loaded, 16)
        sp.dma_start(self.cmp_t, bass.AP(tensor=scratch.tensor, offset=T - 31 - 16 * (CMP - 1),
                                            ap=[[16, CMP], [row, NSA_H], [1, T]])).then_inc(self.loaded, 16)
        sp.dma_start(K.sinks[:, 0, :, :], dr["swa_sinks_2"].partition_broadcast(P)).then_inc(self.loaded, 16)
        sp.dma_start(K.rope_m[64:128, :], dr["c_rope_m"]).then_inc(self.loaded, 16)

    def pool(self, pool):
        flip = self.flip
        self.nc.gpsimd.memset(flip[:], 0.0)
        pool.drain()
        self.nc.gpsimd.affine_select(out=flip[:], in_=flip[:], compare_op=ALU.not_equal, fill=1.0, base=1 - P,
                                     pattern=[[1, P]], channel_multiplier=1).then_inc(self.flipper, 1)

    def pe(self, pe):
        nc, K, flip = self.nc, self.K, self.flip
        pe.wait_ge(self.loaded, 16 * 5)
        pe.wait_ge(self.flipper, 1)
        for n in range(8):
            if n >= 4:
                pe.wait_ge(self.copied, n - 3)
            src = K.bias_nsa[:, n, :] if n < 4 else K.bias_swa[:, 2 * n - 8:2 * n - 6, :]
            nc.tensor.matmul(K.ps[:, 4 + n % 4, :], flip[:], src, start=True, stop=True).then_inc(self.turned, 1)
        pe.wait_ge(self.copied, 5)
        for h in range(NSA_H):
            for i in range(TT):
                o = (h * TT + i) * 32
                last = nc.tensor.matmul(K.ps[:, 4, o:o + CMP], self.cmp_t[:, h, i * P:(i + 1) * P],
                                        flip[0:CMP, P - CMP:P], start=True, stop=True)
        last.then_inc(self.turned, 1)

    def dve(self, dve):
        v, K = self.nc.vector, self.K
        for n in range(8):
            dve.wait_ge(self.turned, n + 1)
            dst = K.bias_nsa[:, n, :] if n < 4 else K.bias_swa[:, 2 * n - 8:2 * n - 6, :].rearrange("p h j -> p (h j)")
            v.tensor_copy(dst, K.ps[:, 4 + n % 4, :]).then_inc(self.copied, 1)
        v.tensor_scalar(K.sinks[:, 1, :, :], K.sinks[:, 0, :, :], 8.0, None, ALU.mult)
        dve.wait_ge(self.turned, 9)
        v.tensor_copy(K.bias_cmp[:, :, :, 0:CMP],
                      K.ps[:, 4, :].rearrange("p (h i c) -> p h i c", h=NSA_H, c=32)[:, :, :, 0:CMP])


LAYER_SLOTS = [[(0, 0, 256)], [(0, 256, 256)], [(0, 512, 128), (128, 1644, 128)], [(0, 652, 256)],
               [(0, 908, 128), (128, 1580, 64), (192, 1036, 32), (224, 1052, 16), (240, 1036, 16)],
               [(0, 640, 128)]] + [[(0, c, 256)] for c in (1068, 1324, 1708, 1964, 2220, 2476)]


def plan_layer(w):
    def plan(raw, c, u):
        parts = LAYER_SLOTS[2 * c + u]
        view = tiles(raw, DC, parts[-1][0] + parts[-1][2])
        return [(view[:, :, o:o + m], w[:, c:c + m].rearrange("(k p) n -> p k n", p=P)) for o, c, m in parts]
    return plan


def stage_layer_project(nc, K, dr, l, L, gain, following):
    with ExitStack() as ctx:
        rot = ctx.enter_context(nc.sbuf_tensor(K.name("rotk"), [P, T], F32))
        kr = ctx.enter_context(nc.sbuf_tensor(K.name("kr"), [P, T], F32))
        norm = Norm(nc, K, ctx, gain)
        bias = BiasTiles(nc, K, dr, ctx, L.qf[0:CMP, :, :]) if l == 0 else None
        block = ctx.enter_context(nc.Block())
        ring, h = K.ring, K.h
        ready, free = K.s("chunk_ready"), [K.s(f"bank_free{b}") for b in range(4)]
        chunks = [(0, 0, P, "q0"), (0, 128, P, "q1"), (1, 0, P, "kv_cmp"), (1, 128, P, "kv_slc"),
                  (2, 0, P, "kv_win"), (2, 128, P, "v_swa"), (3, 0, P, "cq0"), (3, 128, P, "cq1"),
                  (4, 0, P, "ckv"), (4, 128, P, "k_swa_rope"), (5, 0, P, "gates")]
        chunks += [(6 + j // 2, j % 2 * P, P, f"qs{j}") for j in range(4)]
        chunks += [(8 + j // 2, j % 2 * P, P, f"z{j}") for j in range(8)]
        by_act = ("gates", "z")
        N = len(chunks)

        @block.sync
        def _(sp):
            if bias:
                bias.sync(sp)
            ring.stream(sp, plan_layer(dr["w_in_2"][l]), len(LAYER_SLOTS), following, loop=False)

        @block.tensor
        def _(pe):
            at = -1
            for c, (s, o, m, what) in enumerate(chunks):
                if s != at:
                    at = s
                    w = [tiles(x, DC, LAYER_SLOTS[s][-1][0] + LAYER_SLOTS[s][-1][2]) for x in ring.use(pe, s)]
                if c == 0:
                    for last in product3_pair(nc, [K.ps[:, j, :] for j in range(2)],
                                              lambda j, a, k: w[a][:, k, j * P:(j + 1) * P],
                                              lambda a, k: h[a][:, k, :], DC, norm.wait(pe)):
                        last.then_inc(ready.handle, 1)
                if c < 2:
                    continue
                if c >= 4:
                    pe.wait_ge(free[c % 4].handle, free[c % 4].at(c // 4))
                product3(nc, K.ps[:, c % 4, :], lambda a, k: w[a][:, k, o:o + m], lambda a, k: h[a][:, k, :], DC)\
                    .then_inc(ready.handle, 1)
            if bias:
                bias.pe(pe)

        @block.vector
        def _(dve):
            v = nc.vector
            norm.dve(dve)
            copies = {"q0": L.qn[:, 0, :], "q1": L.qn[:, 1, :], "cq0": L.cq[:, 0, :], "cq1": L.cq[:, 1, :],
                      "ckv": L.cq[:, 2, :]} | {f"qs{j}": L.qs[:, j, :] for j in range(4)}
            for c, (slot, o, _, what) in enumerate(chunks):
                ends = c == N - 1 or chunks[c + 1][0] != slot
                if not what.startswith(by_act):
                    dve.wait_ge(ready.handle, ready.at(c + 1))
                if ends:
                    ring.split_low(dve, slot + 2)
                if what.startswith(by_act):
                    continue
                bank = K.ps[:, c % 4, :]
                if what in copies:
                    last = v.tensor_copy(copies[what], bank)
                elif what == "kv_cmp":
                    for i in range(2):
                        rows = slice(64 * i, 64 * i + 64)
                        for e in range(2):
                            for m0 in range(2):
                                src = bank[rows, :].rearrange("p (c s) -> p s c", s=16)[:, e:16:2, m0:m0 + CMP]
                                pe0 = (2 * l + i) * 32 + 16 * m0 + e
                                pos = K.peT[rows, pe0:pe0 + 15:2].unsqueeze(2).to_broadcast([64, 8, CMP])
                                last = v.tensor_tensor(L.blk[64 * e:64 * e + 64, i, 8 * m0:8 * m0 + 8, 0:CMP], src, pos,
                                                       ALU.add)
                elif what in ("kv_slc", "kv_win"):
                    k, vt = (L.k_slc, L.v_t[:, 0, :]) if what == "kv_slc" else (L.k_win, L.v_t[:, 1, :])
                    v.tensor_copy(k[0:64, :], bank[0:64, :])
                    v.tensor_copy(k[64:128, :], bank[0:64, :])
                    last = v.tensor_copy(vt[64:128, :], bank[64:128, :])
                elif what == "k_swa_rope":
                    if bias:
                        dve.wait_ge(bias.loaded, 16 * 5)
                    v.tensor_copy(L.k_swa[0:64, :], bank[0:64, :])
                    v.tensor_copy(L.k_swa[64:128, :], bank[0:64, :])
                    v.tensor_tensor(rot[64:96, :], bank[96:128, :], K.rope_m[96:128, :], ALU.mult)
                    v.tensor_tensor(kr[64:96, :], bank[64:96, :], K.rope_m[64:96, :], ALU.mult)
                    dve.drain()
                    for h in range(MLA_H):
                        for half in (slice(64, 96), slice(96, 128)):
                            last = v.tensor_tensor(L.kf[half, h, :], kr[64:96, :], rot[64:96, :], ALU.add)
                elif what == "v_swa":
                    last = v.tensor_copy(L.v_t[0:64, 0, :], bank[0:64, :])
                last.then_inc(free[c % 4].handle, 1)
            if bias:
                bias.dve(dve)
            dve.drain()

        @block.gpsimd
        def _(pool):
            if bias:
                bias.pool(pool)

        @block.scalar
        def _(act):
            norm.act(act)
            for c, (slot, o, _, what) in enumerate(chunks):
                if (c == N - 1 or chunks[c + 1][0] != slot) and not what.startswith(by_act):
                    act.wait_ge(ready.handle, ready.at(c + 1))
                    ring.split_high(act, slot + 2)
                if not what.startswith(by_act):
                    continue
                act.wait_ge(ready.handle, ready.at(c + 1))
                bank = K.ps[:, c % 4, :]
                if what == "gates":
                    last = nc.scalar.activation(L.gates_t[:], bank[0:12, :], ACT.Sigmoid)
                else:
                    last = nc.scalar.activation(L.sz[:, int(what[1:]), :], bank, ACT.Silu)
                last.then_inc(free[c % 4].handle, 1)
                if c == N - 1 or chunks[c + 1][0] != slot:
                    ring.split_high(act, slot + 2)

        ready.close(N)
        for b in range(4):
            free[b].close(len(range(b, N, 4)))
        ring.close(len(LAYER_SLOTS))
        norm.close()


def stage_latents(nc, K, dr, l, L):
    with ExitStack() as ctx:
        def sb(name, shape):
            return ctx.enter_context(nc.sbuf_tensor(K.name(name), shape, F32))

        sq, rstd = sb("lsq", [P, 3, T]), sb("lrstd", [P, 2, T])
        hid = sb("hid", [P, 2, 32])
        wq, wkv = sb("wq", [P, 2, MLA_H, P]), sb("wkv", [P, MLA_H * P])
        wc1, wc2 = sb("wc1", [P, 2, 16, P]), sb("wc2", [P, 2, HD])
        BANKS = 8
        block = ctx.enter_context(nc.Block())
        in_latent, in_cmp = K.s("latent_weights_in"), K.s("cmp_weights_in")
        ready, free = K.s("chunk_ready"), [K.s(f"bank_free{b}") for b in range(BANKS)]
        squared, rooted, normed, hidden = K.s("squared"), K.s("rooted"), K.s("latents_normed"), K.s("hidden")
        w1, w2 = dr["cmp_w1_2"][l], dr["cmp_w2_2"][l]
        uq, ukv = dr["mla_w_uq_2"][l], dr["mla_w_ukv_2"][l]
        products = ["v_slc", "v_win", "v_swa", "gates", "ss_q", "ss_kv", "hid0", "hid1"]
        products += [f"uq{h}" for h in range(4)] + [f"uk{h}" for h in range(4)] + ["uv0", "uv1", "kc", "vc"]
        by_dve = ("v_", "gates", "uq")
        N = len(products)
        loads = {"latent": 0, "cmp": 0}

        @block.sync
        def _(sp):
            for i in range(2):
                sp.dma_start(wc1[:, i, :, :], w1[i].rearrange("(m p) n -> p m n", p=P)).then_inc(in_cmp.handle, 16)
            sp.dma_start(wc2[:], w2.rearrange("i p d -> p i d")).then_inc(in_cmp.handle, 16)
            loads["cmp"] += 48
            uq4 = uq.rearrange("(k p) (h c) -> p k h c", p=P, h=4)
            for k in range(2):
                for o, c, m in ((0, 0, 96), (96, 80, 16), (112, 64, 16)):
                    sp.dma_start(wq[:, k, :, o:o + m], uq4[:, k, :, c:c + m]).then_inc(in_latent.handle, 16)
                    loads["latent"] += 16
            sp.dma_start(wkv[:], ukv).then_inc(in_latent.handle, 16)
            loads["latent"] += 16

        @block.tensor
        def _(pe):
            t = nc.tensor
            for c, what in enumerate(products):
                if c >= BANKS:
                    pe.wait_ge(free[c % BANKS].handle, free[c % BANKS].at(c // BANKS))
                bank = K.ps[:, c % BANKS, :]
                if what == "ss_q":
                    pe.wait_ge(squared.handle, squared.at(2))
                    last = product(nc, bank, lambda k: K.ones[:], lambda k: sq[:, k, :], 2)
                elif what == "ss_kv":
                    pe.wait_ge(squared.handle, squared.at(3))
                    last = product(nc, bank, lambda k: K.ones[:], lambda k: sq[:, 2, :], 1)
                elif what.startswith("hid"):
                    i = int(what[3:])
                    pe.wait_ge(in_cmp.handle, in_cmp.at(loads["cmp"]))
                    last = product(nc, bank[:, 0:CMP], lambda m: wc1[:, i, m, :], lambda m: L.blk[:, i, m, 0:CMP], 16)
                elif what in ("v_slc", "v_win", "v_swa"):
                    i = ("v_slc", "v_win", "v_swa").index(what)
                    rows, half = (slice(64, 128), i) if i < 2 else (slice(0, 64), 0)
                    for b in range(TT):
                        last = t.matmul(bank[:, 64 * b:64 * b + 64], L.v_t[rows, half, b * P:(b + 1) * P],
                                        K.ident[rows, rows], start=True, stop=True)
                elif what == "gates":
                    for b in range(TT):
                        last = t.matmul(bank[:, 12 * b:12 * b + 12], L.gates_t[:, b * P:(b + 1) * P],
                                        K.ident[0:12, 0:12], start=True, stop=True)
                elif what == "kc":
                    pe.wait_ge(hidden.handle, hidden.at(2))
                    for half in range(2):
                        last = t.matmul(bank[64 * half:64 * half + 64, 0:CMP], wc2[:, 0, :], hid[:, 0, 0:CMP],
                                        start=True, stop=True)
                elif what == "vc":
                    last = t.matmul(bank[0:CMP, 0:64], hid[:, 1, 0:CMP], wc2[:, 1, :], start=True, stop=True)
                elif what.startswith("uq"):
                    pe.wait_ge(normed.handle, normed.at(2))
                    pe.wait_ge(in_latent.handle, in_latent.at(loads["latent"]))
                    last = product(nc, bank, lambda k: wq[:, k, int(what[2:]), :], lambda k: L.cq[:, k, :], 2)
                elif what.startswith("uk"):
                    h = int(what[2:])
                    pe.wait_ge(normed.handle, normed.at(3))
                    last = product(nc, bank[0:64, :], lambda k: wkv[:, h * P:h * P + 64], lambda k: L.cq[:, 2, :], 1)
                else:
                    values = wkv[:].rearrange("p (h c) -> p h c", h=4)[:, :, 64:128]
                    for b in range(2):
                        tile = 2 * int(what[2:]) + b
                        last = t.matmul(bank[:, 256 * b:256 * b + 256], L.cq[:, 2, tile * P:(tile + 1) * P], values,
                                        start=True, stop=True)
                last.then_inc(ready.handle, 1)

        @block.scalar
        def _(act):
            for i in range(3):
                nc.scalar.activation(sq[:, i, :], L.cq[:, i, :], ACT.Square).then_inc(squared.handle, 1)
            for c, what in enumerate(products):
                if what.startswith(by_dve):
                    continue
                bank = K.ps[:, c % BANKS, :]
                act.wait_ge(ready.handle, ready.at(c + 1))
                if what.startswith("ss"):
                    i = ("ss_q", "ss_kv").index(what)
                    nc.scalar.activation(rstd[:, i, :], bank, ACT.Sqrt, bias=K.eps[:], scale=(1.0 / 256, 1.0 / 128)[i])\
                        .then_inc(rooted.handle, 1)
                    act.drain().then_inc(free[c % BANKS].handle, 1)
                    continue
                if what.startswith("hid"):
                    nc.scalar.activation(hid[:, int(what[3:]), 0:CMP], bank[:, 0:CMP], ACT.Silu).then_inc(hidden.handle, 1)
                    act.drain().then_inc(free[c % BANKS].handle, 1)
                    continue
                if what == "kc":
                    dst, src = L.kc[:, 0:CMP], bank[:, 0:CMP]
                elif what == "vc":
                    dst, src = L.vc[0:CMP, :], bank[0:CMP, 0:64]
                elif what.startswith("uk"):
                    dst, src = L.kf[0:64, int(what[2:]), :], bank[0:64, :]
                else:
                    b = 2 * int(what[2:])
                    dst, src = L.v_mla[:, b:b + 2, :].rearrange("p b d -> p (b d)"), bank
                nc.scalar.activation(dst, src, ACT.Copy).then_inc(free[c % BANKS].handle, 1)

        @block.vector
        def _(dve):
            v = nc.vector
            for c, what in enumerate(products):
                if what == "ss_q":
                    for n in range(2):
                        dve.wait_ge(rooted.handle, rooted.at(n + 1))
                        v.reciprocal(rstd[:, n, :], rstd[:, n, :])
                        dve.drain()
                        for i in ((0, 1), (2,))[n]:
                            col = 64 + 2 * l + i if i < 2 else 68 + l
                            v.scalar_tensor_tensor(out=L.cq[:, i, :], in0=L.cq[:, i, :], scalar=K.vec[:, col:col + 1],
                                                   in1=rstd[:, n, :], op0=ALU.mult, op1=ALU.mult)\
                                .then_inc(normed.handle, 1)
                if not what.startswith(by_dve):
                    continue
                dve.wait_ge(ready.handle, ready.at(c + 1))
                bank = K.ps[:, c % BANKS, :]
                if what in ("v_slc", "v_win", "v_swa"):
                    dst = (L.v_slc, L.v_win, L.v_swa)[c]
                    last = v.tensor_copy(dst[:].rearrange("p b d -> p (b d)"), bank[:, 0:256])
                elif what == "gates":
                    last = v.tensor_copy(L.gates[:], bank[:, 0:12 * TT])
                else:
                    h = int(what[2:])
                    v.tensor_tensor(L.qf[64:128, h, :], bank[64:128, :], K.rope_m[64:128, :], ALU.mult)
                    last = v.tensor_copy(L.qf[0:64, h, :], bank[0:64, :])
                last.then_inc(free[c % BANKS].handle, 1)
                if what == "gates":
                    dve.drain()
                    v.tensor_scalar(L.gates[:, 0:12:3], L.gates[:, 0:12:3], K.cols[:, 4:5], None, ALU.mult)
            dve.drain()

        ready.close(N)
        squared.close(3)
        rooted.close(2)
        normed.close(3)
        hidden.close(2)
        in_latent.close(loads["latent"])
        in_cmp.close(loads["cmp"])
        for b in range(BANKS):
            free[b].close(len(range(b, N, BANKS)))



def diff_jobs(K, qk, v_tok, oT):
    for h in range(HEADS):
        for t in range(TT):
            w = P * (t + 1)
            for c in range(2):
                rows = slice(64 * c, 64 * c + 64)
                yield job([(0, qk[rows, h, t * P:(t + 1) * P], qk[rows, HEADS + h, 0:w])], w,
                          K.causal[:, T - w:T], A_DIM ** -0.5,
                          [(b * P, P, v_tok[:, b, h * P:(h + 1) * P]) for b in range(t + 1)],
                          oT[:, h, t * P:(t + 1) * P], first=c == 0, last=c == 1,
                          gate=K.neg_lam[:] if c else None)


def dilated_jobs(mask, qk, v_tok, oT, first_head):
    for h in range(2):
        for r in range(CLASSES):
            own = slice(r * P, (r + 1) * P)
            q = [qk[:, 2 * g + h, own] for g in range(3)]
            k = [qk[:, 6 + 2 * g + h, :] for g in range(3)]
            head = slice(h * P, (h + 1) * P)
            yield job([(0, q[0], k[0]), (T, q[1], k[1][:, own]), (T + P, q[2], k[2][:, own])], T + 2 * P,
                      mask[:, r, :], P ** -0.5,
                      [(b * P, P, v_tok[:, 0, b, head]) for b in range(CLASSES)]
                      + [((3 + g) * P, P, v_tok[:, g, r, head]) for g in (1, 2)],
                      oT[:, first_head + h, r:T:CLASSES])


def plan_a(dr):
    return column_plan(dr["w_in"][0], DC, 256)


def plan_b(dr, half):
    return [column_plan(dr["w_in"][0], DC, 256, 3 * T + first * T + 256 * half, T) for first in (0, 6)]


def plan_gate(dr):
    def plan(raw, c, u):
        view = tiles(raw, 16, P)
        if u == 0:
            parts = [(DC * b, DC, dr["w_in"][0], 8192 - 2 * D + b * D) for b in range(2)]
        else:
            parts = [(0, HEADS, dr["w_a_out"][0], 0), (HEADS, HEADS, dr["w_b_out"][0], 0)]
        return [(view[:, k0:k0 + kt, :], w[:, bass.ds((2 * c + u) * (P // 2) + c0 - u * (P // 2), P)].rearrange("(k p) n -> p k n", p=P))
                for k0, kt, w, c0 in parts]
    return plan


def plan_up(dr):
    def plan(raw, c, u):
        view = tiles(raw, 2 * DC, P)
        return [(view[:, DC * half:DC * (half + 1), :],
                 dr["w_up"][0][:, bass.ds(half * FF + (2 * c + u) * P, P)].rearrange("(k p) n -> p k n", p=P))
                for half in range(2)]
    return plan


def plan_down(dr):
    rows = FF // 2

    def plan(raw, c, u):
        src = dr["w_down"][0][u * rows:(u + 1) * rows, bass.ds(c * P, P)].rearrange("(k p) n -> p k n", p=P)
        return [(tiles(raw, rows // P, P), src)]
    return plan


def layer_jobs(K, L, l):
    for h in range(NSA_H):
        rows = slice(64 * (h % 2), 64 * (h % 2) + 64)
        for t in range(TT):
            w, own = P * (t + 1), slice(t * P, (t + 1) * P)
            q = L.qn[rows, h // 2, own]
            common = dict(out=L.sz[rows, h // 2, own], rows=(rows.start, 64), times=L.sz[rows, h // 2, own])
            gates = [L.gates[:, 12 * t + 3 * h + b:12 * t + 3 * h + b + 1] for b in range(3)]
            yield job([(0, q, L.kc[rows, 0:CMP])], CMP, K.bias_cmp[:, h, t, 0:CMP], HD ** -0.5,
                      [(0, CMP, L.vc[0:CMP, :])], first=True, last=False, gate=gates[0], turned=(CMP, P), **common)
            for b, (k, v) in enumerate([(L.k_slc, L.v_slc), (L.k_win, L.v_win)]):
                yield job([(0, q, k[rows, 0:w])], w, K.bias_nsa[:, h, T - w:T], HD ** -0.5,
                          [(i * P, P, v[:, i, :]) for i in range(t + 1)], first=False, last=b == 1,
                          gate=gates[1 + b], **common)
    for h in range(MLA_H):
        rows = slice(64 * (h % 2), 64 * (h % 2) + 64)
        for t in range(TT):
            w, own = P * (t + 1), slice(t * P, (t + 1) * P)
            yield job([(0, L.qf[:, h, own], L.kf[:, h, 0:w])], w, K.causal[:, T - w:T], 96 ** -0.5,
                      [(i * P, P, L.v_mla[:, i, 64 * h:64 * h + 64]) for i in range(t + 1)],
                      L.sz[rows, 2 + h // 2, own], rows=(rows.start, 64), times=L.sz[rows, 2 + h // 2, own])
    for h in range(SWA_H):
        rows = slice(64 * (h % 2), 64 * (h % 2) + 64)
        for t in range(TT):
            w = min(2, t + 1) * P
            lo, own = (t + 1) * P - w, slice(t * P, (t + 1) * P)
            yield job([(0, L.qs[rows, h // 2, own], L.k_swa[rows, lo:lo + w])], w, K.bias_swa[:, h, 2 * P - w:2 * P],
                      HD ** -0.5, [(i * P, P, L.v_swa[:, lo // P + i, :]) for i in range(w // P)],
                      L.sz[rows, 4 + h // 2, own], rows=(rows.start, 64), times=L.sz[rows, 4 + h // 2, own],
                      sink=(K.sinks[:, 1, l, h:h + 1], K.sinks[:, 0, l, h:h + 1]))


def build(nc, dr, out, stop=None, probes=None):
    with ExitStack() as ctx:
        K = Kit()

        def sb(name, shape, dt=F32, scope=ctx):
            return scope.enter_context(nc.sbuf_tensor(name, shape, dt))

        names, counted = {}, {}

        def name(n):
            names[n] = names.get(n, 0) + 1
            return f"{n}_{names[n]}"

        def s(n):
            if n not in counted:
                counted[n] = Counted(ctx.enter_context(nc.semaphore(n)))
            return counted[n]

        K.name, K.s = name, s
        K.ps = ctx.enter_context(nc.psum_tensor("ps", [P, 8, T], F32))
        K.ring = Ring(nc, sb("ring_raw", [P, 2, Ring.SIZE]), sb("ring_high", [P, 2, Ring.SIZE], F32R),
                      sb("ring_low", [P, 2, Ring.SIZE], F32R),
                      [ctx.enter_context(nc.semaphore(f"slot{i}_loaded")) for i in range(2)],
                      *[ctx.enter_context(nc.semaphore(x)) for x in ("slots_high", "slots_split")])
        K.xT = sb("xT", [P, DC, T])
        K.ident, K.ones, K.eps = sb("ident", [P, P]), sb("ones", [P, P]), sb("eps", [P, 1])
        K.cols, K.causal = sb("cols", [P, 8]), sb("causal", [P, T])
        K.vec, K.conv, K.peT = sb("vec", [P, NVEC]), sb("conv", [P, 4, 2 * FC]), sb("peT", [P, P])
        K.neg_lam, K.rstd = sb("neg_lam", [P, 1]), sb("rstd", [P, T])

        def h_tiles(scope):
            K.h = (sb(name("h_high"), [P, DC, T], F32R, scope), sb(name("h_low"), [P, DC, T], F32R, scope))

        def probe(what, tensor):
            if probes is not None and what in probes:
                with ExitStack() as e:
                    sm = e.enter_context(nc.semaphore(name("probe")))
                    blk = e.enter_context(nc.Block())

                    @blk.sync
                    def _(sp):
                        sp.dma_start(probes[what], tensor).then_inc(sm, 16)
                        sp.wait_ge(sm, 16)

        def gains(first):
            return lambda c: K.vec[:, first + c:first + c + 1]

        plan_mix = column_plan(dr["w_mix_out"][0], DC, 256)
        with ExitStack() as mix:
            oa, ob = sb("oa", [P, HEADS, T], scope=mix), sb("ob", [P, HEADS, T], scope=mix)
            h_tiles(mix)
            with ExitStack() as tables:
                K.sin_b, K.cos_b = sb("sin_b", [P, T], scope=tables), sb("cos_b", [P, T], scope=tables)
                K.sin_a, K.cos_a = sb("sin_a", [P, T], scope=tables), sb("cos_a", [P, T], scope=tables)
                K.pos_f = sb("pos_f", [P, T], scope=tables)
                mask = sb("mask_b", [P, CLASSES, 6 * P], scope=tables)
                stage_setup(nc, K, dr)
                with ExitStack() as e:
                    qk, v = sb("qk_a", [P, 2 * HEADS, T], scope=e), sb("v_a", [P, TT, T], scope=e)
                    stage_project_a(nc, K, dr, qk, v, gains(VECS["pre_mix_g"][0]), mask, plan_b(dr, 0)[0])
                    stage_attention(nc, K, list(diff_jobs(K, qk, v, oa)), T, 3, 3, 5)
                for half in range(2):
                    following = plan_b(dr, 1)[0] if half == 0 else plan_gate(dr)
                    with ExitStack() as e:
                        qk, v = sb(name("qk_b"), [P, 12, T], scope=e), sb(name("v_b"), [P, 3, CLASSES, 256], scope=e)
                        stage_project_b(nc, K, qk, v, *plan_b(dr, half), following,
                                        heads=None if half else (oa, K.vec[:, 70:71]))
                        stage_attention(nc, K, list(dilated_jobs(mask, qk, v, ob, 2 * half)), 6 * P, 2, 1, 5)
            probe("ob", ob[:])
            mixed = (sb("mixed_high", [P, DC, T], F32R, mix), sb("mixed_low", [P, DC, T], F32R, mix))
            stage_gate_mix(nc, K, dr, oa, ob, *mixed, plan_mix)
            stage_out_project(nc, K, plan_mix, DC, 1, 2, None, mixed, gains(8), plan_up(dr))
            probe("x1", K.xT[:])
        with ExitStack() as e:
            hidden = (sb("ffn_high", [P, FC, T], F32R, e), sb("ffn_low", [P, FC, T], F32R, e))
            with ExitStack() as e2:
                h_tiles(e2)
                stage_ffn_up(nc, K, *hidden, gains(VECS["pre_ffn_g"][0]), plan_up(dr), plan_down(dr))
            stage_out_project(nc, K, plan_down(dr), FC, 2, 1, None, hidden, gains(24), plan_layer(dr["w_in_2"][0]))
            probe("x2", K.xT[:])
        K.bias_nsa, K.bias_swa = sb("bias_nsa", [P, NSA_H, T]), sb("bias_swa", [P, SWA_H, 2 * P])
        K.bias_cmp, K.sinks = sb("bias_cmp", [P, NSA_H, TT, 32]), sb("sinks", [P, 2, LAYERS, SWA_H])
        K.rope_m = sb("rope_m", [P, T])
        for l in range(LAYERS):
            with ExitStack() as e:
                L = Kit()
                L.sz = sb(name("sz"), [P, DC, T], scope=e)
                plan_out = column_plan(dr["w_out_2"][l], DC, 256)
                with ExitStack() as inner:
                    L.qn = sb(name("qn"), [P, 2, T], scope=inner)
                    L.cq = sb(name("cq"), [P, 3, T], scope=inner)
                    L.blk = sb(name("blk"), [P, 2, 16, 32], scope=inner)
                    L.k_slc = sb(name("k_slc"), [P, T], scope=inner)
                    L.k_win = sb(name("k_win"), [P, T], scope=inner)
                    L.k_swa = sb(name("k_swa"), [P, T], scope=inner)
                    L.v_t = sb(name("v_t"), [P, 2, T], scope=inner)
                    L.kf = sb(name("kf"), [P, MLA_H, T], scope=inner)
                    L.qf = sb(name("qf"), [P, MLA_H, T], scope=inner)
                    L.qs = sb(name("qs"), [P, SWA_H // 2, T], scope=inner)
                    L.gates_t = sb(name("gates_t"), [12, T], scope=inner)
                    L.gates = sb(name("gates"), [P, 12 * TT], scope=inner)
                    L.kc = sb(name("kc"), [P, 32], scope=inner)
                    L.vc = sb(name("vc"), [32, HD], scope=inner)
                    L.v_slc = sb(name("v_slc"), [P, TT, HD], scope=inner)
                    L.v_win = sb(name("v_win"), [P, TT, HD], scope=inner)
                    L.v_swa = sb(name("v_swa"), [P, TT, HD], scope=inner)
                    L.v_mla = sb(name("v_mla"), [P, TT, MLA_H * HD], scope=inner)
                    with ExitStack() as e2:
                        h_tiles(e2)
                        stage_layer_project(nc, K, dr, l, L, gains(VECS["norm_pre_2"][0] + DC * l), plan_out)
                    stage_latents(nc, K, dr, l, L)
                    stage_attention(nc, K, list(layer_jobs(K, L, l)), T, 3, 3, 5)
                following = plan_layer(dr["w_in_2"][l + 1]) if l + 1 < LAYERS else None
                stage_out_project(nc, K, plan_out, DC, 1, 2, L.sz, None, gains(48 + DC * l), following, out)
                probe(f"y{l}", K.xT[:])


def kernel(**inputs):
    import concourse.bacc as bacc
    from concourse.bass_utils import run_bass_kernel_spmd

    nc = bacc.Bacc("TRN2", target_bir_lowering=False, num_devices=1)
    arrays = {k: np.ascontiguousarray(v) for k, v in inputs.items()}
    arrays |= shape_constants()
    dr = {k: nc.dram_tensor(f"{k}_dram", a.shape, mybir.dt.from_np(a.dtype), kind="ExternalInput").ap()
          for k, a in arrays.items()}
    dr["scratch"] = nc.dram_tensor("bias_scratch", (2, NSA_H + SWA_H, 2 * T), F32, kind="Internal").ap()
    out = nc.dram_tensor("out_dram", (1, T, D), F32, kind="ExternalOutput").ap()
    build(nc, dr, out)
    r = run_bass_kernel_spmd(nc, [{f"{k}_dram": a for k, a in arrays.items()}], core_ids=[0])
    return r.results[0]["out_dram"]
```
